# Optimizing a Trainium2 kernel written in Bass

```python
import math
import jax
import jax.numpy as jnp
from jax import lax
import numpy as np

D_MODEL = 1024
BATCH = 1
SEQ = 256
DEPTH = 2

SB_HEADS = 8
SB_HEAD_DIM = 64
SB_BLOCK = 128
SB_WIDTH = SB_HEADS * SB_HEAD_DIM
DN_HEADS = 4
DN_HEAD_DIM = 128
DN_WIDTH = DN_HEADS * DN_HEAD_DIM
DN_CONV = 4
DN_CHUNK = 64
IN_SPLITS = [SB_WIDTH, SB_WIDTH, SB_WIDTH, 3 * DN_WIDTH, DN_HEADS, DN_HEADS, DN_WIDTH]
IN_DIM_EVEN = sum(IN_SPLITS)
MIX_WIDTH_EVEN = SB_WIDTH + DN_WIDTH
S5_GROUP = 16
S5_GROUPS = D_MODEL // S5_GROUP
S5_STATE = 64
S5_CHUNK = 128
S5_MIN_NEG = -1e-4
MOE_GROUPS = 4
MOE_PER_GROUP = 8
N_EXPERTS = MOE_GROUPS * MOE_PER_GROUP
EXPERT_FF = 256
MOE_TOPK = 2
N_EVEN = (DEPTH + 1) // 2
N_ODD = DEPTH // 2
RMS_EPS = 1e-6
L2_EPS = 1e-6

kernel_name = 'hybrid_stickbreak_deltanet_s5_hmoe'

def rmsnorm(x, g):
    xf = x.astype(jnp.float32)
    y = xf * lax.rsqrt(jnp.mean(xf * xf, axis=-1, keepdims=True) + RMS_EPS)
    return (y * g.astype(jnp.float32)).astype(x.dtype)

def l2norm(x):
    return x * lax.rsqrt(jnp.sum(x * x, axis=-1, keepdims=True) + L2_EPS)

def stick_breaking_attention(q, k, v):
    b, l, h, d = q.shape
    nb = l // SB_BLOCK
    qf = q.astype(jnp.float32) * (1.0 / math.sqrt(d))
    kf = k.astype(jnp.float32)
    vf = v.astype(jnp.float32)
    q_blocks = qf.reshape(b, nb, SB_BLOCK, h, d).transpose(1, 0, 3, 2, 4)
    key_pos = jnp.arange(l)

    def block(args):
        qb, i = args
        z = jnp.einsum('bhqd,bshd->bhqs', qb, kf)
        q_pos = i * SB_BLOCK + jnp.arange(SB_BLOCK)
        causal = key_pos[None, :] < q_pos[:, None]
        log_1m = jnp.where(causal, jax.nn.log_sigmoid(-z), 0.0)
        after = lax.cumsum(log_1m, axis=3, reverse=True) - log_1m
        log_w = jnp.where(causal, jax.nn.log_sigmoid(z) + after, -jnp.inf)
        return jnp.einsum('bhqs,bshd->bqhd', jnp.exp(log_w), vf)

    out = lax.map(block, (q_blocks, jnp.arange(nb)))
    return out.transpose(1, 0, 2, 3, 4).reshape(b, l, h * d)

def causal_depthwise_conv(x, w):
    kk, c = w.shape
    return lax.conv_general_dilated(
        x, w.reshape(kk, 1, c).astype(x.dtype), window_strides=(1,),
        padding=[(kk - 1, 0)], dimension_numbers=('NWC', 'WIO', 'NWC'),
        feature_group_count=c)

def gated_delta_rule(q, k, v, beta, g):
    b, h, l, dk = q.shape
    dv = v.shape[-1]
    c = DN_CHUNK
    n = l // c
    rs = lambda t: t.reshape((b, h, n, c) + t.shape[3:])
    q, k, v, beta, g = rs(q), rs(k), rs(v), rs(beta), rs(g)
    decay = jnp.cumsum(g, axis=-1)
    idx = jnp.arange(c)
    incl = idx[:, None] >= idx[None, :]
    strict = idx[:, None] > idx[None, :]
    dmask = jnp.exp(jnp.where(incl, decay[..., :, None] - decay[..., None, :], -jnp.inf))
    k_beta = k * beta[..., None]
    m = jnp.where(strict, jnp.einsum('bhnid,bhnjd->bhnij', k_beta, k) * dmask, 0.0)
    rhs = jnp.concatenate([k_beta * jnp.exp(decay)[..., None], v * beta[..., None]], axis=-1)
    sol = lax.linalg.triangular_solve(m + jnp.eye(c, dtype=m.dtype), rhs,
                                      left_side=True, lower=True)
    w, u = sol[..., :dk], sol[..., dk:]
    attn = jnp.einsum('bhnid,bhnjd->bhnij', q, k) * dmask
    q_dec = q * jnp.exp(decay)[..., None]
    k_tail = k * jnp.exp(decay[..., -1:] - decay)[..., None]
    chunk_dec = jnp.exp(decay[..., -1])

    def step(state, xs):
        w_n, u_n, attn_n, qd_n, kt_n, cd_n = xs
        v_new = u_n - jnp.einsum('bhcd,bhde->bhce', w_n, state)
        o = (jnp.einsum('bhcd,bhde->bhce', qd_n, state)
             + jnp.einsum('bhij,bhje->bhie', attn_n, v_new))
        state = state * cd_n[..., None, None] + jnp.einsum('bhcd,bhce->bhde', kt_n, v_new)
        return state, o

    xs = tuple(jnp.moveaxis(t, 2, 0) for t in (w, u, attn, q_dec, k_tail, chunk_dec))
    s0 = jnp.zeros((b, h, dk, dv), jnp.float32)
    _, o = lax.scan(step, s0, xs)
    return jnp.moveaxis(o, 0, 2).reshape(b, h, l, dv)

def gated_deltanet(qkv, beta_logit, a_logit, gate, conv_w, a_log, dt_bias, out_norm):
    b, l, _ = qkv.shape
    qkv = jax.nn.silu(causal_depthwise_conv(qkv, conv_w)).astype(jnp.float32)
    q, k, v = jnp.split(qkv, 3, axis=-1)
    heads = lambda t: t.reshape(b, l, DN_HEADS, DN_HEAD_DIM).transpose(0, 2, 1, 3)
    q = l2norm(heads(q)) * (DN_HEAD_DIM ** -0.5)
    k = l2norm(heads(k))
    v = heads(v)
    beta = jax.nn.sigmoid(beta_logit.astype(jnp.float32)).transpose(0, 2, 1)
    g = (-jnp.exp(a_log.astype(jnp.float32))
         * jax.nn.softplus(a_logit.astype(jnp.float32) + dt_bias.astype(jnp.float32)))
    g = g.transpose(0, 2, 1)
    o = gated_delta_rule(q, k, v, beta, g).transpose(0, 2, 1, 3)
    z = gate.astype(jnp.float32).reshape(b, l, DN_HEADS, DN_HEAD_DIM)
    o = rmsnorm(o, out_norm) * jax.nn.silu(z)
    return o.reshape(b, l, DN_WIDTH)

def even_mixer(h, w_in, conv_w, a_log, dt_bias, out_norm, w_out):
    b, l, _ = h.shape
    proj = h @ w_in
    cuts = np.cumsum(IN_SPLITS)[:-1].tolist()
    sb_q, sb_k, sb_v, dn_qkv, dn_beta, dn_a, dn_gate = jnp.split(proj, cuts, axis=-1)
    heads = lambda t: t.reshape(b, l, SB_HEADS, SB_HEAD_DIM)
    y_sb = stick_breaking_attention(heads(sb_q), heads(sb_k), heads(sb_v))
    y_dn = gated_deltanet(dn_qkv, dn_beta, dn_a, dn_gate, conv_w, a_log, dt_bias, out_norm)
    y = jnp.concatenate([y_sb, y_dn], axis=-1).astype(h.dtype)
    return y @ w_out

def _ssm_combine(e1, e2):
    a1r, a1i, b1r, b1i = e1
    a2r, a2i, b2r, b2i = e2
    return (a2r * a1r - a2i * a1i, a2r * a1i + a2i * a1r,
            a2r * b1r - a2i * b1i + b2r, a2r * b1i + a2i * b1r + b2i)

def s5_mixer(h, lam_re, lam_im, log_step, b_re, b_im, c_re, c_im, d_skip, w_glu, b_glu):
    bsz, l, _ = h.shape
    f32 = jnp.float32
    u = h.astype(f32).reshape(bsz, l, S5_GROUPS, S5_GROUP)
    lre = jnp.minimum(lam_re.astype(f32), S5_MIN_NEG)
    lim = lam_im.astype(f32)
    dt = jnp.exp(log_step.astype(f32))[:, None]
    mag = jnp.exp(lre * dt)
    ab_re, ab_im = mag * jnp.cos(lim * dt), mag * jnp.sin(lim * dt)
    den = lre * lre + lim * lim
    nr, ni = ab_re - 1.0, ab_im
    coef_re = (nr * lre + ni * lim) / den
    coef_im = (ni * lre - nr * lim) / den
    br, bi = b_re.astype(f32), b_im.astype(f32)
    bb_re = coef_re[..., None] * br - coef_im[..., None] * bi
    bb_im = coef_re[..., None] * bi + coef_im[..., None] * br
    cr, ci = c_re.astype(f32), c_im.astype(f32)
    a_shape = (bsz, S5_CHUNK, S5_GROUPS, S5_STATE)
    a_re_b = jnp.broadcast_to(ab_re, a_shape)
    a_im_b = jnp.broadcast_to(ab_im, a_shape)
    n = l // S5_CHUNK
    u_chunks = jnp.moveaxis(u.reshape(bsz, n, S5_CHUNK, S5_GROUPS, S5_GROUP), 1, 0)

    def chunk(carry, u_c):
        hr0, hi0 = carry
        bu_re = jnp.einsum('blgc,gpc->blgp', u_c, bb_re)
        bu_im = jnp.einsum('blgc,gpc->blgp', u_c, bb_im)
        pr, pi, lr, li = lax.associative_scan(_ssm_combine, (a_re_b, a_im_b, bu_re, bu_im), axis=1)
        hr = lr + pr * hr0[:, None] - pi * hi0[:, None]
        hi = li + pr * hi0[:, None] + pi * hr0[:, None]
        y = jnp.einsum('blgp,gcp->blgc', hr, cr) - jnp.einsum('blgp,gcp->blgc', hi, ci)
        return (hr[:, -1], hi[:, -1]), y

    h0 = jnp.zeros((bsz, S5_GROUPS, S5_STATE), f32)
    _, y = lax.scan(chunk, (h0, h0), u_chunks)
    u_flat = u.reshape(bsz, l, D_MODEL)
    y = jnp.moveaxis(y, 0, 1).reshape(bsz, l, D_MODEL) + d_skip.astype(f32) * u_flat
    y = jax.nn.gelu(y)
    zv, zg = jnp.split(y @ w_glu.astype(f32) + b_glu.astype(f32), 2, axis=-1)
    return (zv * jax.nn.sigmoid(zg)).astype(h.dtype)

def hier_moe(h, w_rg, w_re, w_e_in, w_e_out):
    b, l, d = h.shape
    f32 = jnp.float32
    xt = h.reshape(b * l, d)
    grp_logits = (xt @ w_rg).astype(f32)
    grp_prob = jax.nn.softmax(grp_logits, axis=-1)
    grp = jnp.argmax(grp_logits, axis=-1)
    grp_onehot = jax.nn.one_hot(grp, MOE_GROUPS, dtype=f32)
    grp_w = jnp.sum(grp_prob * grp_onehot, axis=-1)
    exp_logits = (xt @ w_re).astype(f32).reshape(-1, MOE_GROUPS, MOE_PER_GROUP)
    in_grp = jnp.take_along_axis(exp_logits, grp[:, None, None], axis=1)[:, 0]
    top_v, top_i = lax.top_k(in_grp, MOE_TOPK)
    top_w = jax.nn.softmax(top_v, axis=-1)
    within = jnp.einsum('tk,tke->te', top_w, jax.nn.one_hot(top_i, MOE_PER_GROUP, dtype=f32))
    gate = (grp_w[:, None, None] * grp_onehot[:, :, None] * within[:, None, :]).reshape(-1, N_EXPERTS)
    y = jnp.zeros((b * l, d), f32)
    for e in range(N_EXPERTS):
        a, v = jnp.split(xt @ w_e_in[e], 2, axis=-1)
        y = y + gate[:, e:e + 1] * ((jax.nn.silu(a) * v) @ w_e_out[e]).astype(f32)
    return y.reshape(b, l, d).astype(h.dtype)

def setup_inputs(seed: int = 0) -> dict:
    key = jax.random.key(seed)
    ks = jax.random.split(key, 32)
    nrm = lambda k, s, sc: jax.random.normal(k, s, jnp.float32) * sc
    gain = lambda k, s: 1.0 + 0.02 * jax.random.normal(k, s, jnp.float32)
    x = jax.random.normal(ks[0], (BATCH, SEQ, D_MODEL), jnp.float32)
    mix_norm_even = gain(ks[1], (N_EVEN, D_MODEL))
    w_in_even = nrm(ks[2], (N_EVEN, D_MODEL, IN_DIM_EVEN), D_MODEL ** -0.5)
    dn_conv_w = nrm(ks[3], (N_EVEN, DN_CONV, 3 * DN_WIDTH), DN_CONV ** -0.5)
    dn_a_log = jnp.log(jax.random.uniform(ks[4], (N_EVEN, DN_HEADS), jnp.float32, 1.0, 16.0))
    dt = jnp.exp(jax.random.uniform(ks[5], (N_EVEN, DN_HEADS), jnp.float32,
                                    math.log(1e-3), math.log(1e-1)))
    dn_dt_bias = dt + jnp.log(-jnp.expm1(-dt))
    dn_out_norm = gain(ks[6], (N_EVEN, DN_HEAD_DIM))
    w_out_even = nrm(ks[7], (N_EVEN, MIX_WIDTH_EVEN, D_MODEL), MIX_WIDTH_EVEN ** -0.5)
    mix_norm_odd = gain(ks[8], (N_ODD, D_MODEL))
    s5_lambda_re = -0.5 + 0.01 * jax.random.normal(ks[9], (N_ODD, S5_GROUPS, S5_STATE), jnp.float32)
    s5_lambda_im = (math.pi * jnp.arange(S5_STATE, dtype=jnp.float32)
                    + 0.01 * jax.random.normal(ks[10], (N_ODD, S5_GROUPS, S5_STATE), jnp.float32))
    s5_log_step = jax.random.uniform(ks[11], (N_ODD, S5_GROUPS), jnp.float32,
                                     math.log(1e-3), math.log(1e-1))
    s5_b_re = nrm(ks[12], (N_ODD, S5_GROUPS, S5_STATE, S5_GROUP), (2 * S5_GROUP) ** -0.5)
    s5_b_im = nrm(ks[13], (N_ODD, S5_GROUPS, S5_STATE, S5_GROUP), (2 * S5_GROUP) ** -0.5)
    s5_c_re = nrm(ks[14], (N_ODD, S5_GROUPS, S5_GROUP, S5_STATE), (2 * S5_STATE) ** -0.5)
    s5_c_im = nrm(ks[15], (N_ODD, S5_GROUPS, S5_GROUP, S5_STATE), (2 * S5_STATE) ** -0.5)
    s5_d = nrm(ks[16], (N_ODD, D_MODEL), 1.0)
    w_glu = nrm(ks[17], (N_ODD, D_MODEL, 2 * D_MODEL), D_MODEL ** -0.5)
    b_glu = nrm(ks[18], (N_ODD, 2 * D_MODEL), 0.01)
    ffn_norm = gain(ks[19], (DEPTH, D_MODEL))
    w_router_group = nrm(ks[20], (DEPTH, D_MODEL, MOE_GROUPS), D_MODEL ** -0.5)
    w_router_expert = nrm(ks[21], (DEPTH, D_MODEL, N_EXPERTS), D_MODEL ** -0.5)
    w_expert_in = nrm(ks[22], (DEPTH, N_EXPERTS, D_MODEL, 2 * EXPERT_FF), D_MODEL ** -0.5)
    w_expert_out = nrm(ks[23], (DEPTH, N_EXPERTS, EXPERT_FF, D_MODEL), EXPERT_FF ** -0.5)
    final_norm = gain(ks[24], (D_MODEL,))
    return {'x': x, 'mix_norm_even': mix_norm_even, 'w_in_even': w_in_even,
            'dn_conv_w': dn_conv_w, 'dn_a_log': dn_a_log, 'dn_dt_bias': dn_dt_bias,
            'dn_out_norm': dn_out_norm, 'w_out_even': w_out_even,
            'mix_norm_odd': mix_norm_odd, 's5_lambda_re': s5_lambda_re,
            's5_lambda_im': s5_lambda_im, 's5_log_step': s5_log_step,
            's5_b_re': s5_b_re, 's5_b_im': s5_b_im, 's5_c_re': s5_c_re, 's5_c_im': s5_c_im,
            's5_d': s5_d, 'w_glu': w_glu, 'b_glu': b_glu, 'ffn_norm': ffn_norm,
            'w_router_group': w_router_group, 'w_router_expert': w_router_expert,
            'w_expert_in': w_expert_in, 'w_expert_out': w_expert_out, 'final_norm': final_norm}

def reference(x, mix_norm_even, w_in_even, dn_conv_w, dn_a_log, dn_dt_bias, dn_out_norm,
              w_out_even, mix_norm_odd, s5_lambda_re, s5_lambda_im, s5_log_step,
              s5_b_re, s5_b_im, s5_c_re, s5_c_im, s5_d, w_glu, b_glu, ffn_norm,
              w_router_group, w_router_expert, w_expert_in, w_expert_out, final_norm):
    h = x
    for layer in range(DEPTH):
        j = layer // 2
        if layer % 2 == 0:
            h = h + even_mixer(rmsnorm(h, mix_norm_even[j]), w_in_even[j], dn_conv_w[j],
                               dn_a_log[j], dn_dt_bias[j], dn_out_norm[j], w_out_even[j])
        else:
            h = h + s5_mixer(rmsnorm(h, mix_norm_odd[j]), s5_lambda_re[j], s5_lambda_im[j],
                             s5_log_step[j], s5_b_re[j], s5_b_im[j], s5_c_re[j], s5_c_im[j],
                             s5_d[j], w_glu[j], b_glu[j])
        h = h + hier_moe(rmsnorm(h, ffn_norm[layer]), w_router_group[layer],
                         w_router_expert[layer], w_expert_in[layer], w_expert_out[layer])
    return rmsnorm(h, final_norm)


_drawn_inputs = setup_inputs


def setup_inputs(seed=0):
    import zlib

    import numpy as np

    out = dict(_drawn_inputs(seed))
    spreads = {}
    factors = {'s5_lambda_re': 200.0,
     'b_glu': 11.051,
     'final_norm': 23.231,
     'mix_norm_odd': 3.039,
     's5_lambda_im': 34.6,
     's5_log_step': 32.792,
     's5_b_re': 50.25,
     's5_b_im': 54.856,
     's5_c_re': 35.944,
     's5_c_im': 43.296}
    for name, (base, spread) in spreads.items():
        noise = np.random.default_rng([zlib.crc32(name.encode()), seed]).standard_normal(out[name].shape)
        drawn = base * np.exp(spread * noise) if base else spread * noise
        out[name] = jnp.asarray(drawn.astype(out[name].dtype))
    for name, factor in factors.items():
        out[name] = (out[name] * factor).astype(out[name].dtype)
    return out
```

```python
from contextlib import ExitStack

import concourse.bass as bass
from concourse import mybir

P = 128
T = 256
NT = T // P
D = 1024
KD = D // P
SBH, SBD = 8, 64
DNH, DND = 4, 128
TAPS = 4
CH = 64
NU = DNH * NT
NEXP, NGRP, PERG = 32, 4, 8
FF = 256
CAP = 64
PASSES = T // CAP
SLOTS = 2 * T
NS5 = 32
S5C = 128
NW, NV = 4, 4
EPS = 1e-6
BIG = 1e30

F32 = mybir.dt.float32
I32 = mybir.dt.int32
U32 = mybir.dt.uint32
ALU = mybir.AluOpType
ACT = mybir.ActivationFunctionType
AX = mybir.AxisListType

PROJ_BLOCKS = ["dn_q", "dn_k", "dn_v", "gate", "sb_q", "sb_k", "sb_v"]
PROJ_COL = {"sb_q": 0, "sb_k": 512, "sb_v": 1024, "dn_q": 1536, "dn_k": 2048, "dn_v": 2560, "gate": 3080}
W_OUT0 = len(PROJ_BLOCKS)
W_EXP = [W_OUT0 + 2, W_OUT0 + 2 + NEXP + 4]
W_GLU = W_OUT0 + 2 + NEXP

N_PAR = 16

TWO_PI = (6.28125, 0.0019350051879882812, 3.0199159795074593e-07)
ROUND = 1.5 * 2.0 ** 23
PI = 3.141592502593994
EXP_LN = "natural_log_exp_and_others"


class Chain:

    def __init__(self, eng, sem):
        self.eng, self.sem, self.n = eng, sem, 0

    def mark(self, ins):
        ins.then_inc(self.sem, 1)
        self.n += 1

    def wait(self):
        self.eng.wait_ge(self.sem, self.n)

    def link(self, ins):
        self.mark(ins)
        self.wait()


def bc(ap, shape):
    return ap.unsqueeze(len(ap.shape)).to_broadcast(shape)


def trunk(nc, x, mix_norm_even, w_in_even, dn_conv_w, dn_a_log, dn_dt_bias, dn_out_norm, w_out_even,
          mix_norm_odd, s5_lambda_re, s5_lambda_im, s5_log_step, s5_b_re, s5_b_im, s5_c_re, s5_c_im,
          s5_d, w_glu, b_glu, ffn_norm, w_router_group, w_router_expert, w_expert_in, w_expert_out,
          final_norm, out):
    ctx = ExitStack()
    with ctx:
        def sb(name, shape, dt=F32, stack=ctx):
            return stack.enter_context(nc.sbuf_tensor(name, shape, dt))

        def sem(name):
            return ctx.enter_context(nc.semaphore(name))

        bank = [ctx.enter_context(nc.psum_tensor(f"bank{i}", [P, 512], F32)) for i in range(8)]

        def halves(b0, n=P):
            return [bank[b0 + u // 4][:, (u % 4) * P:(u % 4) * P + n] for u in range(NU)]

        ring_w = sb("ring_w", [P, NW, KD, 512])
        ring_v = sb("ring_v", [P, NV, 2, D])
        res = sb("res", [P, NT, D])
        xn = sb("xn", [P, NT, D])
        xT = sb("xT", [P, KD, T])
        gains = sb("gains", [P, 4, KD])
        ssq = sb("ssq", [P, 5, NT])
        msq = sb("msq", [P, 5, NT])
        rstd = sb("rstd", [P, 5, NT])
        neghalf = sb("neghalf", [P, NU])
        one_col = sb("one_col", [P, 1])
        ident = sb("ident", [P, P])
        ones = sb("ones", [P, P])
        before = sb("before", [P, P])

        wr = sb("wr", [P, 2, KD, NGRP + NEXP])
        iota_e = sb("iota_e", [P, NEXP])

        s5t = sb("s5t", [P, 7, NS5])
        cmask = sb("cmask", [P, 2])
        s5d = sb("s5d", [P, KD])

        mixer = ExitStack()
        neg_upto = sb("neg_upto", [P, P], stack=mixer)
        neg_ones = sb("neg_ones", [P, P], stack=mixer)
        causal3 = sb("causal3", [P, 3, P], stack=mixer)
        negcausal3 = sb("negcausal3", [P, 3, P], stack=mixer)
        chunk_incl = sb("chunk_incl", [P, P], stack=mixer)
        negchunk = sb("negchunk", [P, P], stack=mixer)
        chunk_ones = sb("chunk_ones", [P, P], stack=mixer)
        level = sb("level", [P, 6, P], stack=mixer)
        wba = sb("wba", [P, KD, 8], stack=mixer)
        convw_rows = sb("convw_rows", [TAPS * 12, P], stack=mixer)
        convw = sb("convw", [P, TAPS * 12], stack=mixer)
        dn_par = sb("dn_par", [P, 2, DNH], stack=mixer)
        neg_a = sb("neg_a", [P, DNH], stack=mixer)
        out_gain = sb("out_gain", [P, 1], stack=mixer)
        eps_col = sb("eps_col", [P, 1], stack=mixer)
        raw = sb("raw", [P, 12, TAPS - 1 + T], stack=mixer)
        qkvT = sb("qkvT", [P, 12, T], stack=mixer)
        gate = sb("gate", [P, NT, 512], stack=mixer)
        sbqT = sb("sbqT", [P, 4, T], stack=mixer)
        sbkT = sb("sbkT", [P, 4, T], stack=mixer)
        sbv = sb("sbv", [P, NT, 512], stack=mixer)
        yT = sb("yT", [P, KD, T], stack=mixer)
        ba = sb("ba", [P, NT, 8], stack=mixer)
        sml = sb("sml", [P, 16, NU], stack=mixer)
        state = sb("state", [P, DNH, DND], stack=mixer)
        sb_e = sb("sb_e", [P, 2, 3 * P], stack=mixer)
        sb_sp = sb("sb_sp", [P, 2, 3 * P], stack=mixer)
        sb_w = sb("sb_w", [P, 2, 3 * P], stack=mixer)
        mixer.close()

        def mat(ap):
            return ap.rearrange("p (u q) -> p u q", q=P)

        dmT, expd, btl, X, XT, P1, kbe, ktail = [mat(ring_v[:, m // 2, m % 2, :]) for m in range(8)]
        raw_flat = raw[:, :, :].rearrange("p c t -> p (c t)")
        vbeta, wT, uu = [mat(raw_flat[:, m * D:(m + 1) * D]) for m in range(3)]
        mT, attnT = [mat(xn[:, m, :]) for m in range(2)]
        qT = mat(qkvT[:, 0:4, :].rearrange("p c t -> p (c t)"))
        kT = mat(qkvT[:, 4:8, :].rearrange("p c t -> p (c t)"))
        vT = mat(qkvT[:, 8:12, :].rearrange("p c t -> p (c t)"))
        sq_q, sq_k, kbT, rs = btl, X, P1, XT
        vnew, oo, yg = X, P1, btl
        BETA, G, SP_, E1, T1, DCOL, DTOT, KF, TF, SSO, RSO = range(11)

        s5w = yT[0:NS5, :, :].rearrange("p k t -> p (k t)").rearrange("p (n s) -> p n s", s=P)
        LRE, LIM, THE, TK, TR, TH, MAG, COS, SIN, DEN, NRE, CRE, CIM, TMP, VEC = range(15)
        s5dt = yT[0:NS5, 7, 250:252]

        rot = sb("rot", [P, 2, NS5, S5C])
        rot_f = sb("rot_f", [P, 2, NS5, 8])
        rot_c = sb("rot_c", [P, 2, NS5, 16])
        turn128 = sb("turn128", [P, 2, NS5])

        moe = ExitStack()
        iota_slot = sb("iota_slot", [P, SLOTS], stack=moe)
        s5tmp = sb("s5tmp", [P, 4, NS5, 8], stack=moe)
        xs = sb("xs", [P, KD, SLOTS + CAP], stack=moe)
        perm = sb("perm", [P, NT, SLOTS], stack=moe)
        xe = sb("xe", [P, 2, KD, CAP], stack=moe)
        act_a = sb("act_a", [P, 2, P], stack=moe)
        act_g = sb("act_g", [P, 2, P], stack=moe)
        act_gT = sb("act_gT", [P, 2, 2 * CAP], stack=moe)
        yrow = sb("yrow", [P, 2, 512], stack=moe)
        gpad = sb("gpad", [P, NT, 8], stack=moe)
        elog = sb("elog", [P, NT, NEXP], stack=moe)
        top8 = sb("top8", [P, NT, 2, 8], stack=moe)
        idx8 = sb("idx8", [P, NT, 2, 8], U32, stack=moe)
        idxf = sb("idxf", [P, NT, 2, 8], stack=moe)
        goh = sb("goh", [P, NT, NGRP], stack=moe)
        prod = sb("prod", [P, NT, NEXP], stack=moe)
        ingrp = sb("ingrp", [P, NT, 8], stack=moe)
        rv = sb("rv", [P, 12, NT, 2], stack=moe)
        gexp = sb("gexp", [P, NT, NGRP], stack=moe)
        onehot = sb("onehot", [P, NT, 2, NEXP], stack=moe)
        sel = sb("sel", [P, NT, NEXP], stack=moe)
        pos = sb("pos", [P, NT, NEXP], stack=moe)
        cnt = sb("cnt", [P, NEXP], stack=moe)
        base = sb("base", [P, NEXP], stack=moe)
        cum = sb("cum", [P, NEXP], stack=moe)
        slot_all = sb("slot_all", [P, NT, NEXP], stack=moe)
        prod2 = sb("prod2", [P, NT, 2, NEXP], stack=moe)
        base_i = sb("base_i", [1, PASSES, NEXP + 2], I32, stack=moe)
        most = sb("most", [P, 1], stack=moe)
        most_i = sb("most_i", [1, 1], I32, stack=moe)
        yidx = sb("yidx", [P, NT, 2], I32, stack=moe)
        moe.close()
        rtmp = s5tmp[:, 0:2, :, :].rearrange("p m (r n) f -> p m r n f", r=2)
        ygath = xs[:, :, :].rearrange("p k c -> p (k c)")[:, 0:4 * D].rearrange("p (t r d) -> p t r d", t=NT, r=2)

        s5 = ExitStack()
        bT = sb("bT", [P, 2, KD, P], stack=s5)
        cT = sb("cT", [P, 2, KD, P], stack=s5)
        wide = sb("wide", [P, 2, KD, P], stack=s5)
        m_in = sb("m_in", [P, 2, 2, 2 * T], stack=s5)
        m_out = sb("m_out", [P, 2, 2, 2 * T], stack=s5)
        s5.close()
        def in_ring(slot, half=None):
            ap = ring_v[:, slot, :, :] if half is None else ring_v[:, slot, half, :]
            return ap
        cT2 = in_ring(0).rearrange("p m (k q) -> p m k q", k=KD)
        cTn, cTn2 = [in_ring(1, h).rearrange("p (k q) -> p k q", k=KD) for h in range(2)]
        bT2 = in_ring(2).rearrange("p m (k q) -> p m k q", k=KD)
        wide2 = in_ring(3).rearrange("p m (k q) -> p m k q", k=KD)
        c_tmp_g = [in_ring(1, 1).rearrange("p (j c) -> p j c", c=32), in_ring(0, 1).rearrange("p (j c) -> p j c", c=32)]
        flat = lambda ap: ap.rearrange("p a k q -> p (a k q)")
        wide_f = flat(wide[:, :, :, :])
        gin = wide_f[:, 0:1024].rearrange("p (b m t) -> p b m t", b=2, m=2)
        gst = wide_f[:, 1024:2048].rearrange("p (b m t) -> p b m t", b=2, m=2)
        c_tmp_v = [flat(bT)[:, m * 1024:(m + 1) * 1024].rearrange("p (j c) -> p j c", c=32) for m in range(2)]
        m_out_f, m_in_f = [m[:, :, :, :].rearrange("p a b c -> p (a b c)") for m in (m_out, m_in)]
        b_prod = m_out_f.rearrange("p (n j c) -> p n j c", n=4, c=16)
        wide_c = m_in_f.rearrange("p (m k h q) -> p m k h q", m=2, k=KD, h=2)
        s5b = ring_v[:, 2, 1, :].rearrange("p (m j c) -> p m j c", m=2, c=16)
        s5c = ring_v[:, 2, 0, :].rearrange("p (m k q) -> p m k q", m=2, k=KD)
        gain_fin = rot[:, 0, 0:KD, :].rearrange("p j q -> p (j q)")
        yg5 = xn[:, :, :].rearrange("p t (k q) -> p (t k) q", q=T)
        bias_glu = ring_v[:, 3, :, :].rearrange("p k n -> p (k n)")


        expert_rows = [nc.dram_tensor(f"expert_rows{l}", [NEXP * T, D], F32, kind="Internal").ap() for l in range(2)]

        x_in, gain_in, par_in = sem("x_in"), sem("gain_in"), sem("par_in")
        w_in = [sem(f"w_in{i}") for i in range(NW)]
        v_in = [sem(f"v_in{i}") for i in range(NV)]
        consts = sem("consts")
        pool_ch, dve_ch, act_ch = sem("pool_chain"), sem("dve_chain"), sem("act_chain")
        ssq_ok, msq_ok, rstd_ok, xn_ok = sem("ssq_ok"), sem("msq_ok"), sem("rstd_ok"), sem("xn_ok")
        xT_ps, xT_act, xT_dve = sem("xT_ps"), sem("xT_act"), sem("xT_dve")
        res_ok = sem("res_ok")
        cw_ps, cw_ok = sem("cw_ps"), sem("cw_ok")
        proj_ps, proj_got = sem("proj_ps"), sem("proj_got")
        conv_ok, silu_ok, sq_ok = sem("conv_ok"), sem("silu_ok"), sem("sq_ok")
        ba_ps, ba_got = sem("ba_ps"), sem("ba_got")
        be_ok, ab_ok, sp_ok, g_ok = sem("be_ok"), sem("ab_ok"), sem("sp_ok"), sem("g_ok")
        rows_ps, dcol_ok, expd_ok, diff_ok, dm_ok = [sem(n) for n in ("rows_ps", "dcol_ok", "expd_ok", "diff_ok", "dm_ok")]
        ssum_ps, rs_ok, qn_ok, kn_ok, fac_ok, fac_exp = [sem(n) for n in ("ssum_ps", "rs_ok", "qn_ok", "kn_ok", "fac_ok", "fac_exp")]
        vt_ps, kt_ps, vt_ok, kt_ok = [sem(n) for n in ("vt_ps", "kt_ps", "vt_ok", "kt_ok")]
        kb_ok, gram_ps, gram_ok, bt_ok = [sem(n) for n in ("kb_ok", "gram_ps", "gram_ok", "bt_ok")]
        p1_ps, p1_ok, delta_ps, deltaT_ps, x_ok, xt_ok = [sem(n) for n in ("p1_ps", "p1_ok", "delta_ps", "deltaT_ps", "x_ok", "xt_ok")]
        wu_ps, wT_ok, u_ok = [sem(n) for n in ("wu_ps", "wT_ok", "u_ok")]
        vs_ps, vn_ok, o_ps, st_ps, st_ok, o_ok = [sem(n) for n in ("vs_ps", "vn_ok", "o_ps", "st_ps", "st_ok", "o_ok")]
        so_ok, ro_ok, yg_ok, yd_ps, yd_ok = [sem(n) for n in ("so_ok", "ro_ok", "yg_ok", "yd_ps", "yd_ok")]
        z_ps, e_ok, sp3_ok, spm_ok, rc_ps, lw_ok, w_ok, ys_ps, ys_ok = [
            sem(n) for n in ("z_ps", "e_ok", "sp3_ok", "spm_ok", "rc_ps", "lw_ok", "w_ok", "ys_ps", "ys_ok")]
        mix_ps = sem("mix_ps")
        osq_ok = sem("osq_ok")
        log_ps, glog_ok, gexp_ok, dv_ok, wexp_ok = [sem(n) for n in ("log_ps", "glog_ok", "gexp_ok", "dv_ok", "wexp_ok")]
        sel_ok, pos_ps, routed, perm_ok = [sem(n) for n in ("sel_ok", "pos_ps", "routed", "perm_ok")]
        xs_ps, xs_act, xs_dve = [sem(n) for n in ("xs_ps", "xs_act", "xs_dve")]
        xe_ok, h_ps, ha_ok, hg_ok, t_ps, gt_ok, y_ps, ya_ok = [
            sem(n) for n in ("xe_ok", "h_ps", "ha_ok", "hg_ok", "t_ps", "gt_ok", "y_ps", "ya_ok")]
        more_in, more_out, more_step = [[sem(f"more_{n}{l}") for l in range(2)] for n in ("in", "out", "step")]
        STEPS = 8
        XE, HID, SILU, GATED, TURNED, GT, PROD, ROW = range(1, STEPS + 1)
        s5_dt, s5_arg, s5_trig, s5_par, s5_tps, s5t_ok = [sem(n) for n in ("s5_dt", "s5_arg", "s5_trig", "s5_par", "s5_tps", "s5t_ok")]
        c2_re, b2_ok = sem("c2_re"), sem("b2_ok")
        c_in, c_used = sem("c_in"), sem("c_used")
        coarse_ok, rot_m, rot_ok, raw_in, bias_in = [sem(n) for n in ("coarse_ok", "rot_m", "rot_ok", "raw_in", "bias_in")]
        wz_ok, wb_ok, wc_ok, bt_ps, ct_ps, bT_ok, cT_ok = [sem(n) for n in ("wz_ok", "wb_ok", "wc_ok", "bt_ps", "ct_ps", "bT_ok", "cT_ok")]
        bu_ps, mc_ok, ms_ok, gin_ok, c2_ok, gst_ok, oc_ok, os_ok, yd5_ok, gelu_ok = [sem(n) for n in (
            "bu_ps", "mc_ok", "ms_ok", "gin_ok", "c2_ok", "gst_ok", "oc_ok", "os_ok", "yd5_ok", "gelu_ok")]
        glu_ps, gz_ok, gs_ok, fin_ok, out_done, fg_in = [sem(n) for n in ("glu_ps", "gz_ok", "gs_ok", "fin_ok", "out_done", "fg_in")]
        y_out = [sem(f"y_out{i}") for i in range(2)]
        y_in = [sem(f"y_in{i}") for i in range(4)]

        plan = [("beta", 0), ("rows", 0), ("l2", 0), ("turn", 0), ("gram", 0)]
        chain = [("level", n) for n in range(6)] + [("wu", 0)] + [("chunk", n) for n in range(4)] + [("dn_out", 0)]
        for s, item in enumerate(chain):
            plan.append(item)
            if 0 <= s - 2 < SBH:
                plan.append(("mixv", s - 2))
            if 0 <= s - 1 < SBH:
                plan.append(("suffix", s - 1))
            if item[0] == "level" and item[1]:
                plan.append(("delta", item[1]))
            if s < SBH:
                plan.append(("score", s))
        z3 = [bank[4], bank[5]]

        block = ctx.enter_context(nc.Block())

        def stored(eng, l, i, par4, lap, par):
            uses = NEXP // 2 * l + [-1, 0, 0, 1][par4]
            if isinstance(lap, int):
                if 2 * lap + uses > 0:
                    eng.wait_ge(y_out[par], 32 * (2 * lap + uses))
            elif l or uses > -1 or par4 == 0:
                eng.wait_ge(y_out[par], lap * 64 + 32 * uses)

        def pipeline(eng, step):
            step(0, 0, 0, True, False)
            with eng.Fori(0, NEXP // 4 - 1) as turn:
                for j in range(1, 5):
                    step(turn * 4 + j, j % 4, turn + j // 4, False, False)
            for i in range(NEXP - 3, NEXP + 1):
                step(i, i % 4, i // 4, False, i == NEXP)

        @block.sync
        def _(sp):
            for t in range(NT):
                sp.dma_start(res[:, t, :], x[0, t * P:(t + 1) * P, :]).then_inc(x_in, 16)

            sp.dma_start(gains[:, 0, :], mix_norm_even[0].rearrange("(p k) -> p k", k=KD)).then_inc(gain_in, 16)

            def load_w(i, src):
                sp.dma_start(ring_w[:, i % NW, :, :], src).then_inc(w_in[i % NW], 16)

            def load_parameters():
                small_loads = [
                    (gains[:, 1, :], ffn_norm[0].rearrange("(p k) -> p k", k=KD)),
                    (gains[:, 3, :], ffn_norm[1].rearrange("(p k) -> p k", k=KD)),
                    (convw_rows[:, :], dn_conv_w[0].rearrange("j (c p) -> (j c) p", p=P)),
                    (wba[:, :, :], w_in_even[0].rearrange("(p k) n -> p k n", k=KD)[:, :, 3072:3080]),
                    (dn_par[:, 0, :], dn_a_log.partition_broadcast(P)[:, 0, :]),
                    (dn_par[:, 1, :], dn_dt_bias.partition_broadcast(P)[:, 0, :]),
                    (out_gain[:, :], dn_out_norm[0].rearrange("(p o) -> p o", o=1)),
                    (s5w[0:KD, VEC, :], mix_norm_odd[0].rearrange("(k p) -> k p", p=P)),
                    (s5w[KD:2 * KD, VEC, :], s5_d[0].rearrange("(k p) -> k p", p=P)),
                    (s5w[:, LRE, :], s5_lambda_re[0].rearrange("(j h) q -> j (h q)", h=2)),
                    (s5w[:, LIM, :], s5_lambda_im[0].rearrange("(j h) q -> j (h q)", h=2)),
                    (s5dt, s5_log_step[0].rearrange("(j h) -> j h", h=2)),
                ] + [(wr[:, l, :, 0:NGRP], w_router_group[l].rearrange("(p k) n -> p k n", k=KD)) for l in range(2)] + [
                    (wr[:, l, :, NGRP:], w_router_expert[l].rearrange("(p k) n -> p k n", k=KD)) for l in range(2)]
                for dst, src in small_loads:
                    sp.dma_start(dst, src).then_inc(par_in, 16)
                assert len(small_loads) == N_PAR

            win = w_in_even[0].rearrange("(p k) n -> p k n", k=KD)
            for i, name in enumerate(PROJ_BLOCKS):
                if i == 2:
                    load_parameters()
                if i >= NW:
                    sp.wait_ge(proj_ps, 2 * (i - NW + 1))
                load_w(i, win[:, :, PROJ_COL[name]:PROJ_COL[name] + 512])
            wo = w_out_even[0].rearrange("(k p) n -> p k n", p=P)
            for h in range(2):
                i = W_OUT0 + h
                sp.wait_ge(proj_ps, 2 * (i - NW + 1))
                load_w(i, wo[:, :, h * 512:(h + 1) * 512])

            def load_expert_w(l, e, slot):
                sp.dma_start(ring_w[:, slot, :, :], w_expert_in[l][e].rearrange("(p k) n -> p k n", k=KD)).then_inc(w_in[slot], 16)

            def load_expert_v(l, e, slot):
                sp.dma_start(ring_v[:, slot, :, :], w_expert_out[l][e].rearrange("(k p) n -> p k n", k=2)).then_inc(v_in[slot], 16)

            def experts(l):
                w0 = W_EXP[l]
                for e in range(NV):
                    if l == 1:
                        sp.wait_ge(glu_ps, 2 * (e + 1))
                    elif e < 2:
                        sp.wait_ge(proj_ps, 2 * (w0 + e - NW + 1))
                    else:
                        sp.wait_ge(mix_ps, 2 * (e - 1))
                    load_expert_w(l, e, (w0 + e) % NW)
                    if l == 0:
                        sp.wait_ge(yd_ps, 1)
                    else:
                        sp.wait_ge(c_used, NS5)
                        if e == NV - 1:
                            sp.wait_ge(res_ok, 3)
                    load_expert_v(l, e, e)
                with sp.Fori(0, NEXP // NV - 1) as turn:
                    for j in range(NV):
                        sp.wait_ge(h_ps, turn * NV + (NEXP * l + j + 1))
                        load_expert_w(l, turn * NV + (NV + j), (w0 + j) % NW)
                        sp.wait_ge(y_ps, turn * NV + (NEXP * l + j + 1))
                        load_expert_v(l, turn * NV + (NV + j), j)
                sp.wait_ge(routed, l + 1)
                with sp.If(sp.value_load(most_i[0:1, 0:1], min_val=0, max_val=SLOTS) > CAP):
                    sp.wait_ge(h_ps, NEXP * (l + 1))
                    sp.wait_ge(y_ps, NEXP * (l + 1))
                    for r in range(PASSES - 1):
                        with sp.Fori(0, NEXP) as e:
                            n = e + r * NEXP
                            sp.wait_ge(more_step[l], n * STEPS)
                            sp.dma_start(ring_w[:, 0, :, :], w_expert_in[l][e].rearrange("(p k) n -> p k n", k=KD)).then_inc(more_in[l], 16)
                            sp.dma_start(ring_v[:, 0, :, :], w_expert_out[l][e].rearrange("(k p) n -> p k n", k=2)).then_inc(more_in[l], 16)
                    sp.wait_ge(more_step[l], (PASSES - 1) * NEXP * STEPS)

            experts(0)
            for i in range(4):
                sp.wait_ge(y_in[i], 16)
            sp.wait_ge(y_ps, NEXP)
            for m, src in enumerate((s5_c_re, s5_c_im)):
                sp.dma_start(s5c[:, m, :, :], src[0].rearrange("(k g) c q -> (g c) k q", k=KD)).then_inc(c_in, 16)
            for m, src in enumerate((s5_b_re, s5_b_im)):
                sp.dma_start(s5b[:, m, :, :], src[0].rearrange("(j h) q c -> (h q) j c", h=2)).then_inc(raw_in, 16)
            sp.wait_ge(bt_ps, 4)
            sp.dma_start(bias_glu, b_glu.partition_broadcast(P)[:, 0, :]).then_inc(bias_in, 16)
            wg = w_glu[0].rearrange("(k p) n -> p k n", p=P)
            for b in range(4):
                h, kind = b // 2, b % 2
                load_w(W_GLU + b, wg[:, :, kind * D + h * 512:kind * D + (h + 1) * 512])
            experts(1)
            sp.dma_start(gain_fin, final_norm.partition_broadcast(P)).then_inc(fg_in, 16)
            for t in range(NT):
                sp.wait_ge(fin_ok, t + 1)
                sp.dma_start(out[0, t * P:(t + 1) * P, :], xn[:, t, :]).then_inc(out_done, 16)
            sp.wait_ge(out_done, 16 * NT)

        @block.gpsimd
        def _(pool):
            c = Chain(pool, pool_ch)
            g = nc.gpsimd

            def norm(n):
                pool.wait_ge(msq_ok, n + 1)
                g.tensor_tensor(rstd[:, n, :], msq[:, n, :], neghalf[:, 0:NT], ALU.pow).then_inc(rstd_ok, 1)

            c.mark(g.memset(neghalf[:, :], -0.5))
            c.link(g.memset(ones[:, :], 1.0))
            g.affine_select(out=ident[:, :], in_=ones[:, :], pattern=[[-1, P]], compare_op=ALU.is_equal, fill=0.0,
                            base=0, channel_multiplier=1).then_inc(consts, 1)
            norm(0)
            c.mark(g.memset(neg_ones[:, :], -1.0))
            c.mark(g.memset(level[:, :, :], 0.0))
            c.mark(g.memset(one_col[:, :], 1.0))
            c.mark(g.memset(eps_col[:, :], EPS))
            c.link(g.memset(causal3[:, 1, :], 1.0))

            def where(dst, src, pattern, base, cm, op=ALU.is_ge, fill=0.0):
                return g.affine_select(out=dst, in_=src, pattern=pattern, compare_op=op, fill=fill,
                                       base=base, channel_multiplier=cm)

            c.mark(where(before[:, :], ones[:, :], [[1, P]], 0, -1, ALU.is_gt))
            c.mark(where(causal3[:, 0, :], ones[:, :], [[1, P]], 0, -1, ALU.is_gt))
            c.mark(where(causal3[:, 2, :], ones[:, :], [[1, P]], 0, -1, ALU.is_gt))
            c.mark(where(neg_upto[:, :], neg_ones[:, :], [[-1, P]], 0, 1))
            two = lambda ap: ap.rearrange("p (c i) -> p c i", i=CH)
            c.link(where(two(chunk_ones[:, :]), two(ones[:, :]), [[-CH, 2], [0, CH]], 0, 1))
            c.link(where(two(chunk_ones[:, :]), two(chunk_ones[:, :]), [[CH, 2], [0, CH]], CH - 1, -1))
            c.link(where(chunk_incl[:, :], chunk_ones[:, :], [[1, P]], 0, -1))
            c.mark(g.tensor_scalar(negchunk[:, :], chunk_incl[:, :], 1.0, BIG, ALU.subtract, ALU.mult))
            c.mark(g.tensor_scalar(negcausal3[:, :, :], causal3[:, :, :], 1.0, BIG, ALU.subtract, ALU.mult))
            for l in range(6):
                s = 2 ** l
                half = level[:, l, :].rearrange("p (c h i) -> p c h i", h=2, i=s)[:, :, 1, :]
                c.link(g.memset(half, 1.0))
                c.link(where(half, half, [[-2 * s, P // (2 * s)], [0, s]], 0, 1))
                c.link(where(half, half, [[2 * s, P // (2 * s)], [0, s]], s - 1, -1))
            c.wait()
            g.memset(raw[:, :, 0:TAPS - 1], 0.0).then_inc(consts, 1)
            g.memset(state[:, :, :], 0.0).then_inc(consts, 1)
            g.iota(iota_e[:, :], [[1, NEXP]], base=0, channel_multiplier=0, allow_small_or_imprecise_dtypes=True).then_inc(consts, 1)

            for c_ in range(2):
                pool.wait_ge(silu_ok, c_ + 1)
                v = (qT, kT)[c_]
                g.tensor_tensor((sq_q, sq_k)[c_], v, v, ALU.mult).then_inc(sq_ok, 1)
            for kind, n in plan:
                for m in [0, 1] if (kind, n) == ("level", 0) else [n + 1] if kind == "level" and n < 5 else []:
                    pool.wait_ge(gram_ok, 2)
                    if m:
                        pool.wait_ge(p1_ps, m)
                    if m == 1:
                        pool.wait_ge(xt_ok, 1)
                    g.tensor_tensor(btl, mT, level[:, m:m + 1, :].to_broadcast((P, NU, P)), ALU.mult).then_inc(bt_ok, 1)
                if kind == "score":
                    pool.wait_ge(sp3_ok, n + 1)
                    g.tensor_tensor(sb_sp[:, n % 2, :], sb_sp[:, n % 2, :], causal3[:, :, :].rearrange("p a b -> p (a b)"),
                                    ALU.mult).then_inc(spm_ok, 1)
                if kind == "dn_out":
                    pool.wait_ge(so_ok, 1)
                    g.tensor_tensor(sml[:, RSO, :], sml[:, SSO, :], neghalf[:, :], ALU.pow).then_inc(ro_ok, 1)

            def experts(l):
                with pool.Fori(0, NEXP // 2) as turn:
                    for j in range(2):
                        pool.wait_ge(ya_ok, turn * 2 + (NEXP * l + j + 1))
                        rows = expert_rows[l].rearrange("(n c) (h d) -> n h c d", c=CAP, h=2)[turn * 2 + j]
                        for h in range(2):
                            g.dma_start(rows[h], yrow[h * CAP:(h + 1) * CAP, j, :]).then_inc(y_out[j], 16)
                for j in range(2):
                    pool.wait_ge(y_out[j], 16 * NEXP * (l + 1))
                pool.wait_ge(xe_ok, (NEXP + 2) * (l + 1))

                def gather(rows):
                    for t in range(NT):
                        for r in range(2):
                            g.indirect_dma_start(ygath[:, t, r, :], None, rows,
                                                 bass.IndirectOffsetOnAxis(ap=yidx[:, t, r:r + 1], axis=0)).then_inc(y_in[2 * t + r], 16)

                pool.wait_ge(routed, l + 1)
                with pool.If(pool.value_load(most_i[0:1, 0:1], min_val=0, max_val=SLOTS) > CAP):
                    for r in range(PASSES - 1):
                        with pool.Fori(0, NEXP) as e:
                            pool.wait_ge(more_step[l], e * STEPS + (r * NEXP * STEPS + ROW))
                            rows = expert_rows[l].rearrange("(n c) (h d) -> n h c d", c=CAP, h=2)[e + (r + 1) * NEXP]
                            for h in range(2):
                                g.dma_start(rows[h], yrow[h * CAP:(h + 1) * CAP, 0, :]).then_inc(more_out[l], 16)
                    pool.wait_ge(more_out[l], 32 * (PASSES - 1) * NEXP)
                    gather(expert_rows[l])
                with pool.Else():
                    gather(expert_rows[l][0:NEXP * CAP, :])

            def slot_numbers(l):
                pool.wait_ge(res_ok, 1 + 2 * l)
                g.iota(iota_slot[:, :], [[1, SLOTS]], base=0, channel_multiplier=0, allow_small_or_imprecise_dtypes=True).then_inc(consts, 1)

            def coarse_turns():
                def cmul(dst, x_, y_, n):
                    xr, xi = x_[0], x_[1]
                    yr, yi = [z if n == 1 else z.to_broadcast((P, NS5, n)) for z in y_]
                    t = [s5tmp[:, q, :, 0:n] for q in range(4)]
                    for q, (a_, b_) in enumerate(((xr, yr), (xi, yi), (xr, yi), (xi, yr))):
                        c.mark(g.tensor_tensor(t[q], a_, b_, ALU.mult))
                    c.wait()
                    c.mark(g.tensor_tensor(dst[0], t[0], t[1], ALU.subtract))
                    c.link(g.tensor_tensor(dst[1], t[2], t[3], ALU.add))

                def at(tab, lo, hi=None):
                    return [tab[:, m, :, lo:(hi or lo + 1)] for m in range(2)]

                pool.wait_ge(s5t_ok, 1)
                for tab in (rot_f, rot_c):
                    c.mark(g.memset(tab[:, 0, :, 0:1], 1.0))
                    c.mark(g.memset(tab[:, 1, :, 0:1], 0.0))
                c.mark(g.tensor_copy(rot_f[:, 0, :, 1], s5t[:, 1, :]))
                c.link(g.tensor_copy(rot_f[:, 1, :, 1], s5t[:, 2, :]))
                cmul(at(rot_f, 2), at(rot_f, 1), at(rot_f, 1), 1)
                cmul(at(rot_f, 3), at(rot_f, 2), at(rot_f, 1), 1)
                cmul(at(rot_f, 4), at(rot_f, 2), at(rot_f, 2), 1)
                cmul(at(rot_f, 5, 8), at(rot_f, 1, 4), at(rot_f, 4), 3)
                cmul(at(rot_c, 1), at(rot_f, 4), at(rot_f, 4), 1)
                cmul(at(rot_c, 2), at(rot_c, 1), at(rot_c, 1), 1)
                cmul(at(rot_c, 3), at(rot_c, 2), at(rot_c, 1), 1)
                cmul(at(rot_c, 4), at(rot_c, 2), at(rot_c, 2), 1)
                cmul(at(rot_c, 5, 8), at(rot_c, 1, 4), at(rot_c, 4), 3)
                cmul(at(rot_c, 8), at(rot_c, 4), at(rot_c, 4), 1)
                cmul(at(rot_c, 9, 16), at(rot_c, 1, 8), at(rot_c, 8), 7)
                cmul([turn128[:, m, :].unsqueeze(2) for m in range(2)], at(rot_c, 8), at(rot_c, 8), 1)
                f, late = [s5t[:, 3 + m, :].unsqueeze(2) for m in range(2)], [s5t[:, 5 + m, :].unsqueeze(2) for m in range(2)]
                t = [s5tmp[:, q, :, 0:1] for q in range(4)]
                for q, (a_, b_) in enumerate(((0, 0), (1, 1), (1, 0), (0, 1))):
                    c.mark(g.tensor_tensor(t[q], f[a_], turn128[:, b_, :].unsqueeze(2), ALU.mult))
                c.wait()
                c.mark(g.tensor_tensor(late[0], t[0], t[1], ALU.add))
                c.link(g.tensor_tensor(late[1], t[2], t[3], ALU.subtract))
                g.memset(s5tmp[:, 0, 0, 0:1], 0.0).then_inc(coarse_ok, 1)

            def zeros(w):
                g.memset(w[:, :, :, :], 0.0).then_inc(wz_ok, 1)

            def late_output_weights():
                t128 = [bc(turn128[:, m, :], (P, NS5, 32)) for m in range(2)]
                flat_c = lambda ap: ap.rearrange("p k (j c) -> p (k j) c", c=32)
                pool.wait_ge(cT_ok, 6)
                c.mark(g.tensor_tensor(c_tmp_g[0], flat_c(cT[:, 1, :, :]), t128[0], ALU.mult))
                c.link(g.tensor_tensor(c_tmp_g[1], flat_c(cT[:, 0, :, :]), t128[1], ALU.mult))
                g.tensor_tensor(flat_c(cT2[:, 1, :, :]), c_tmp_g[0], c_tmp_g[1], ALU.subtract).then_inc(c2_ok, 1)
                pool.wait_ge(c2_ok, 1)

            def s5_layer():
                late_output_weights()

                def turn_back(j, b):
                    pool.wait_ge(mc_ok, j + 1)
                    pool.wait_ge(ms_ok, j + 1)
                    g.tensor_tensor(gin[:, b, 0, :], m_in[:, b, 0, 0:T], m_in[:, b, 1, T:], ALU.add).then_inc(gin_ok, 1)
                    g.tensor_tensor(gin[:, b, 1, :], m_in[:, b, 0, T:], m_in[:, b, 1, 0:T], ALU.subtract).then_inc(gin_ok, 1)

                def by_sine(j, b):
                    pool.wait_ge(gst_ok, j * 2 + 2)
                    g.tensor_tensor(m_out[:, b, 1, :].rearrange("p (a t) -> p a t", t=S5C), gst[:, b, :, :].rearrange("p m (a t) -> p (m a) t", t=S5C),
                                    rot[:, 1, bass.ds(j, 1), :].to_broadcast((P, 4, S5C)), ALU.mult).then_inc(os_ok, 1)

                turn_back(0, 0)
                turn_back(1, 1)
                with pool.Fori(0, NS5 // 2 - 1) as turn:
                    for b in range(2):
                        by_sine(turn * 2 + b, b)
                        turn_back(turn * 2 + (b + 2), b)
                for b in range(2):
                    by_sine(NS5 - 2 + b, b)

            norm(1)
            slot_numbers(0)
            coarse_turns()
            experts(0)
            pool.wait_ge(res_ok, 2)
            zeros(wide)
            norm(2)
            zeros(wide2)
            s5_layer()
            norm(3)
            slot_numbers(1)
            experts(1)
            norm(4)

        @block.scalar
        def _(act):
            c = Chain(act, act_ch)
            a = nc.scalar

            def norm_a(n):
                if n == 0:
                    act.wait_ge(x_in, 16 * NT)
                else:
                    act.wait_ge(res_ok, n)
                for t in range(NT):
                    a.activation(xn[:, t, :], res[:, t, :], ACT.Square, accum_out=ssq[:, n, t:t + 1]).then_inc(ssq_ok, 1)

            def norm_b(n):
                for b in range(2):
                    act.wait_ge(xT_ps, 4 * n + b + 1)
                    for k in (2 * b, 2 * b + 1):
                        a.activation(xT[:, k, :], bank[b][:, (k % 2) * T:(k % 2) * T + T], ACT.Copy,
                                     scale=gains[:, n, k:k + 1]).then_inc(xT_act, 1)

            norm_a(0)
            act.wait_ge(gain_in, 16)
            norm_b(0)
            act.wait_ge(par_in, 16 * N_PAR)
            a.activation(s5dt, s5dt, ACT.Exp).then_inc(s5_dt, 1)
            act.preload_act_table_set("silu_and_others")
            act.wait_ge(consts, 3)
            for i, name in enumerate(PROJ_BLOCKS):
                for h in range(2):
                    act.wait_ge(proj_ps, 2 * i + h + 1)
                    src = bank[4 + 2 * (i % 2) + h]
                    two = src[:, :].rearrange("p (c t) -> p c t", t=T)
                    if name in ("dn_q", "dn_k", "dn_v"):
                        ins = a.activation(raw[:, 4 * i + 2 * h:4 * i + 2 * h + 2, TAPS - 1:], two, ACT.Copy)
                    elif name == "gate":
                        ins = a.activation(gate[:, h, :], src[:, :], ACT.Silu)
                    elif name == "sb_q":
                        ins = a.activation(sbqT[:, 2 * h:2 * h + 2, :], two, ACT.Copy, scale=SBD ** -0.5)
                    elif name == "sb_k":
                        ins = a.activation(sbkT[:, 2 * h:2 * h + 2, :], two, ACT.Copy)
                    else:
                        ins = a.activation(sbv[:, h, :], src[:, :], ACT.Copy)
                    ins.then_inc(proj_got, 1)
                if 1 <= i <= 3:
                    act.wait_ge(conv_ok, i)
                    a.activation(qkvT[:, 4 * i - 4:4 * i, :], qkvT[:, 4 * i - 4:4 * i, :], ACT.Silu).then_inc(silu_ok, 1)
            act.wait_ge(s5_arg, 1)
            a.activation(s5w[:, SIN, :], s5w[:, TR, :], ACT.Sin).then_inc(s5_trig, 1)
            a.activation(s5w[:, TH, :], s5w[:, TR, :], ACT.Sin, scale=0.5).then_inc(s5_trig, 1)
            act.preload_act_table_set(EXP_LN)
            a.activation(s5w[:, MAG, :], s5w[:, MAG, :], ACT.Exp).then_inc(s5_trig, 1)
            for kind, n in plan:
                if kind == "beta":
                    act.wait_ge(ba_ps, 1)
                    a.activation(ba[:, :, :], bank[0][:, 0:16].rearrange("p (t n) -> p t n", t=NT), ACT.Copy).then_inc(ba_got, 1)
                    act.wait_ge(ba_got, 1)
                    c.link(a.activation(sml[:, E1, :].rearrange("p (h t) -> p t h", t=NT), ba[:, :, 0:4], ACT.Exp, scale=-1.0))
                    a.activation(neg_a[:, :], dn_par[:, 0, :], ACT.Exp).then_inc(be_ok, 1)
                    act.wait_ge(ab_ok, 1)
                    c.link(a.activation(sml[:, T1, :], sml[:, SP_, :], ACT.Abs))
                    c.link(a.activation(sml[:, T1, :], sml[:, T1, :], ACT.Exp, scale=-1.0))
                    a.activation(sml[:, T1, :], sml[:, T1, :], ACT.Ln, bias=one_col[:, :]).then_inc(sp_ok, 1)
                if kind == "rows":
                    act.wait_ge(rows_ps, 1)
                    for h in range(2):
                        a.activation(expd[:, 4 * h:4 * h + 4, :].rearrange("p u q -> p (u q)"), bank[h][:, :], ACT.Exp).then_inc(expd_ok, 1)
                    act.wait_ge(diff_ok, 1)
                    a.activation(dmT, dmT, ACT.Exp).then_inc(dm_ok, 1)
                    act.wait_ge(fac_ok, 1)
                    a.activation(sml[:, KF:KF + 2, :], sml[:, KF:KF + 2, :], ACT.Exp).then_inc(fac_exp, 1)
                if kind == "l2":
                    for m in range(2):
                        act.wait_ge(ssum_ps, m + 1)
                        if m:
                            act.wait_ge(qn_ok, 1)
                        for h in range(2):
                            c.mark(a.activation(rs[:, 4 * h:4 * h + 4, :].rearrange("p u q -> p (u q)"),
                                                bank[(6, 4)[m] + h][:, :], ACT.Ln, bias=eps_col[:, :]))
                        c.wait()
                        a.activation(rs, rs, ACT.Exp, scale=-0.5).then_inc(rs_ok, 1)
                if kind == "level":
                    act.wait_ge(p1_ps, n + 1)
                    if n:
                        for h in range(2):
                            a.activation(P1[:, 4 * h:4 * h + 4, :].rearrange("p u q -> p (u q)"), bank[h][:, :], ACT.Copy).then_inc(p1_ok, 1)
                if kind == "wu":
                    act.wait_ge(wu_ps, 1)
                    for h in range(2):
                        a.activation(wT[:, 4 * h:4 * h + 4, :].rearrange("p u q -> p (u q)"), bank[h][:, :], ACT.Copy).then_inc(wT_ok, 1)
                if kind == "chunk":
                    lo = CH * (n % 2)
                    act.wait_ge(o_ps, n + 1)
                    a.activation(oo[lo:lo + CH, 4 * (n // 2):4 * (n // 2) + 4, :].rearrange("p u q -> p (u q)"),
                                 bank[1][lo:lo + CH, :], ACT.Copy).then_inc(o_ok, 1)
                if kind == "dn_out":
                    act.wait_ge(o_ok, 4)
                    for u in range(NU):
                        a.activation(yg[:, u, :], oo[:, u, :], ACT.Square, accum_out=sml[:, E1, u:u + 1]).then_inc(osq_ok, 1)
                    act.wait_ge(yd_ps, 1)
                    for h in range(2):
                        a.activation(yT[:, 4 + 2 * h:6 + 2 * h, :], bank[h][:, :].rearrange("p (c t) -> p c t", t=T), ACT.Copy,
                                     scale=out_gain[:, :]).then_inc(yd_ok, 1)
                if kind == "score":
                    act.wait_ge(z_ps, n + 1)
                    if n >= 2:
                        act.wait_ge(sp3_ok, n - 1)
                    c.link(a.activation(sb_e[:, n % 2, :], z3[n % 2][:, 0:3 * P], ACT.Abs))
                    c.link(a.activation(sb_e[:, n % 2, :], sb_e[:, n % 2, :], ACT.Exp, scale=-1.0))
                    a.activation(sb_e[:, n % 2, :], sb_e[:, n % 2, :], ACT.Ln, bias=one_col[:, :]).then_inc(e_ok, 1)
                if kind == "suffix":
                    act.wait_ge(lw_ok, n + 1)
                    a.activation(sb_w[:, n % 2, :], sb_w[:, n % 2, :], ACT.Exp).then_inc(w_ok, 1)
                if kind == "mixv" and n % 2:
                    act.wait_ge(ys_ps, n + 1)
                    a.activation(yT[:, n // 2, :], bank[7][:, 0:T], ACT.Copy).then_inc(ys_ok, 1)

            def experts(l):
                n0 = NEXP * l
                act.wait_ge(glog_ok, l + 1)
                for t in range(NT):
                    a.activation(gexp[:, t, :], gpad[:, t, 0:NGRP], ACT.Exp, bias=rv[:, 0, t, 0:1],
                                 accum_out=rv[:, 1, t, 0:1]).then_inc(gexp_ok, 1)
                act.wait_ge(dv_ok, l + 1)
                a.activation(rv[:, 3, :, 0], rv[:, 2, :, 0], ACT.Exp).then_inc(wexp_ok, 1)
                act.preload_act_table_set("silu_and_others")
                for k in range(0, KD, 2):
                    act.wait_ge(xs_ps, KD * l + k + 1)
                    a.activation(xs[:, k, 0:SLOTS], bank[k % 4][:, :], ACT.Copy, scale=gains[:, 1 + 2 * l, k:k + 1]).then_inc(xs_act, 1)

                def step(i, par4, lap, first, last):
                    cur, prev = par4 % 2, (par4 + 1) % 2
                    if not first:
                        act.wait_ge(t_ps, i + n0)
                        a.activation(act_gT[:, prev, :], bank[2][:, 0:P], ACT.Copy).then_inc(gt_ok, 1)
                    if not last:
                        act.wait_ge(h_ps, i + (n0 + 1))
                        if not (isinstance(i, int) and i < 2):
                            act.wait_ge(hg_ok, i + (n0 - 1))
                        a.activation(act_a[:, cur, :], bank[cur][:, 0:P], ACT.Silu).then_inc(ha_ok, 1)
                    if not first:
                        act.wait_ge(y_ps, i + n0)
                        stored(act, l, i, par4, lap, prev)
                        a.activation(yrow[:, prev, :], bank[3][:, :], ACT.Copy).then_inc(ya_ok, 1)

                pipeline(act, step)
                act.wait_ge(routed, l + 1)
                with act.If(act.value_load(most_i[0:1, 0:1], min_val=0, max_val=SLOTS) > CAP):
                    for j in range(2):
                        act.wait_ge(y_out[j], 16 * NEXP * (l + 1))
                    for r in range(PASSES - 1):
                        with act.Fori(0, NEXP) as e:
                            n = e + r * NEXP
                            act.wait_ge(more_step[l], n * STEPS + HID)
                            a.activation(act_a[:, 0, :], bank[0][:, 0:P], ACT.Silu).then_inc(more_step[l], 1)
                            act.wait_ge(more_step[l], n * STEPS + TURNED)
                            a.activation(act_gT[:, 0, :], bank[2][:, 0:P], ACT.Copy).then_inc(more_step[l], 1)
                            act.wait_ge(more_step[l], n * STEPS + PROD)
                            act.wait_ge(more_out[l], n * 32)
                            a.activation(yrow[:, 0, :], bank[3][:, :], ACT.Copy).then_inc(more_step[l], 1)

            def s5_output_weights():
                for m in range(2):
                    act.wait_ge(ct_ps, m + 1)
                    for h in range(2):
                        ps = bank[4 + 2 * m + h][:, :]
                        a.activation(cT[:, m, 4 * h:4 * h + 4, :].rearrange("p k q -> p (k q)"), ps, ACT.Copy,
                                     scale=(1.0, -1.0)[m]).then_inc(cT_ok, 1)
                        if m == 0:
                            a.activation(cTn[:, 4 * h:4 * h + 4, :].rearrange("p k q -> p (k q)"), ps, ACT.Copy, scale=-1.0).then_inc(cT_ok, 1)

            def s5_layer():
                act.wait_ge(c2_re, 1)
                for n, dst in enumerate((bT, bT2)):
                    for m in range(2):
                        act.wait_ge(bt_ps, 2 * n + m + 1)
                        if n:
                            act.wait_ge(b2_ok, 1)
                        for h in range(2):
                            a.activation(dst[:, m, 4 * h:4 * h + 4, :].rearrange("p k q -> p (k q)"), bank[2 * m + h][:, :], ACT.Copy).then_inc(bT_ok, 1)
                act.wait_ge(c2_ok, 1)
                a.activation(cTn2, cT2[:, 0, :, :], ACT.Copy, scale=-1.0).then_inc(cT_ok, 1)
                act.preload_act_table_set("gelu_apprx_tanh_and_others")
                with act.Fori(0, KD) as k:
                    act.wait_ge(yd5_ok, k + 1)
                    a.activation(yg5[:, bass.ds(k, 1), :], yg5[:, bass.ds(k, 1), :], ACT.Gelu_apprx_tanh).then_inc(gelu_ok, 1)
                act.preload_act_table_set("sigmoid_and_others")
                for i in range(4):
                    act.wait_ge(gz_ok, i + 1)
                    a.activation(m_in_f[:, i * 512:(i + 1) * 512], m_in_f[:, i * 512:(i + 1) * 512], ACT.Sigmoid).then_inc(gs_ok, 1)

            norm_a(1)
            norm_b(1)
            experts(0)
            norm_a(2)
            s5_output_weights()
            norm_b(2)
            s5_layer()
            act.preload_act_table_set(EXP_LN)
            norm_a(3)
            norm_b(3)
            experts(1)
            norm_a(4)

        @block.vector
        def _(dve):
            c = Chain(dve, dve_ch)
            v = nc.vector

            def norm_a(n):
                dve.wait_ge(ssq_ok, 2 * n + 2)
                v.tensor_scalar(msq[:, n, :], ssq[:, n, :], 1.0 / D, EPS, ALU.mult, ALU.add).then_inc(msq_ok, 1)
                dve.wait_ge(rstd_ok, n + 1)
                for t in range(NT):
                    v.tensor_scalar(xn[:, t, :], res[:, t, :], rstd[:, n, t:t + 1], None, ALU.mult).then_inc(xn_ok, 1)

            def norm_b(n):
                for b in range(2, 4):
                    dve.wait_ge(xT_ps, 4 * n + b + 1)
                    for k in (2 * b, 2 * b + 1):
                        v.tensor_scalar(xT[:, k, :], bank[b][:, (k % 2) * T:(k % 2) * T + T], gains[:, n, k:k + 1], None,
                                        ALU.mult).then_inc(xT_dve, 1)

            norm_a(0)
            dve.wait_ge(gain_in, 16)
            norm_b(0)
            dve.wait_ge(par_in, 16 * N_PAR)
            dve.wait_ge(cw_ps, 1)
            v.tensor_copy(convw[:, :], bank[7][:, 0:TAPS * 12]).then_inc(cw_ok, 1)
            dve.wait_ge(cw_ok, 1)
            for i in range(3):
                dve.wait_ge(proj_got, 2 * i + 2)
                for j in range(TAPS):
                    for ch in range(4 * i, 4 * i + 4):
                        w = convw[:, 12 * j + ch:12 * j + ch + 1]
                        if j == 0:
                            ins = v.tensor_scalar(qkvT[:, ch, :], raw[:, ch, 0:T], w, None, ALU.mult)
                        else:
                            ins = v.scalar_tensor_tensor(out=qkvT[:, ch, :], in0=raw[:, ch, j:j + T], scalar=w,
                                                         in1=qkvT[:, ch, :], op0=ALU.mult, op1=ALU.add)
                        if j < TAPS - 1:
                            c.mark(ins)
                    if j < TAPS - 1:
                        c.wait()
                ins.then_inc(conv_ok, 1)
            def s5_parameters():
                w = lambda n: s5w[:, n, :]
                tt, ts, stt = v.tensor_tensor, v.tensor_scalar, v.scalar_tensor_tensor
                dt = bc(s5dt, (NS5, 2, 64))
                two = lambda ap: ap.rearrange("j (h q) -> j h q", h=2)
                c.mark(ts(w(LRE), w(LRE), -1e-4, None, ALU.min))
                dve.wait_ge(s5_dt, 1)
                c.link(tt(two(w(THE)), two(w(LIM)), dt, ALU.mult))
                c.link(tt(two(w(MAG)), two(w(LRE)), dt, ALU.mult))
                c.link(ts(w(TK), w(THE), 1.0 / (TWO_PI[0] + TWO_PI[1] + TWO_PI[2]), ROUND, ALU.mult, ALU.add))
                c.link(ts(w(TK), w(TK), ROUND, None, ALU.subtract))
                c.link(stt(out=w(TR), in0=w(TK), scalar=-TWO_PI[0], in1=w(THE), op0=ALU.mult, op1=ALU.add))
                for part in TWO_PI[1:]:
                    c.link(stt(out=w(TR), in0=w(TK), scalar=-part, in1=w(TR), op0=ALU.mult, op1=ALU.add))
                ts(w(TR), w(TR), PI, -PI, ALU.min, ALU.max).then_inc(s5_arg, 1)
                c.mark(tt(w(DEN), w(LRE), w(LRE), ALU.mult))
                c.link(tt(w(TMP), w(LIM), w(LIM), ALU.mult))
                c.link(tt(w(DEN), w(DEN), w(TMP), ALU.add))
                c.link(v.reciprocal(w(DEN), w(DEN)))
                dve.wait_ge(s5_trig, 3)
                c.link(tt(w(COS), w(TH), w(TH), ALU.mult))
                c.link(ts(w(COS), w(COS), -2.0, 1.0, ALU.mult, ALU.add))
                c.mark(tt(w(NRE), w(MAG), w(COS), ALU.mult))
                c.link(tt(w(THE), w(MAG), w(SIN), ALU.mult))
                c.link(ts(w(NRE), w(NRE), -1.0, None, ALU.add))
                c.mark(tt(w(CRE), w(NRE), w(LRE), ALU.mult))
                c.mark(tt(w(TMP), w(THE), w(LIM), ALU.mult))
                c.mark(tt(w(CIM), w(THE), w(LRE), ALU.mult))
                c.link(tt(w(TK), w(NRE), w(LIM), ALU.mult))
                c.mark(tt(w(CRE), w(CRE), w(TMP), ALU.add))
                c.link(tt(w(CIM), w(CIM), w(TK), ALU.subtract))
                c.mark(tt(w(CRE), w(CRE), w(DEN), ALU.mult))
                tt(w(CIM), w(CIM), w(DEN), ALU.mult).then_inc(s5_par, 1)
                dve.wait_ge(consts, 3)
                c.link(v.tensor_reduce(cmask[:, 0:1], level[:, 4, :], AX.X, ALU.add))
                c.link(ts(cmask[:, 0:1], cmask[:, 0:1], 1.0 / 16, None, ALU.mult))
                c.mark(ts(cmask[:, 1:2], cmask[:, 0:1], -1.0, 1.0, ALU.mult, ALU.add))
                dve.wait_ge(s5_tps, 1)
                c.mark(v.tensor_copy(gains[:, 2, :], bank[7][:, 5 * NS5:5 * NS5 + KD]))
                c.link(v.tensor_copy(s5d[:, :], bank[7][:, 5 * NS5 + KD:5 * NS5 + 2 * KD]))
                v.tensor_copy(s5t[:, 0:5, :], bank[7][:, 0:5 * NS5].rearrange("p (n j) -> p n j", n=5)).then_inc(s5t_ok, 1)

            s5_parameters()
            for kind, n in plan:
                if kind == "beta":
                    y = sml[:, SP_, :].rearrange("p (h t) -> p t h", t=NT)
                    dve.wait_ge(ba_got, 1)
                    v.tensor_tensor(y, ba[:, :, 4:8], dn_par[:, 1:2, :].to_broadcast((P, NT, DNH)), ALU.add).then_inc(ab_ok, 1)
                    dve.wait_ge(be_ok, 1)
                    c.link(v.tensor_scalar(sml[:, E1, :], sml[:, E1, :], 1.0, None, ALU.add))
                    c.link(v.reciprocal(sml[:, BETA, :], sml[:, E1, :]))
                    dve.wait_ge(sp_ok, 1)
                    c.link(v.scalar_tensor_tensor(out=sml[:, SP_, :], in0=sml[:, SP_, :], scalar=0.0, in1=sml[:, T1, :],
                                                  op0=ALU.max, op1=ALU.add))
                    v.scalar_tensor_tensor(out=sml[:, G, :].rearrange("p (h t) -> p h t", t=NT),
                                           in0=sml[:, SP_, :].rearrange("p (h t) -> p h t", t=NT), scalar=-1.0,
                                           in1=bc(neg_a[:, :], (P, DNH, NT)), op0=ALU.mult, op1=ALU.mult).then_inc(g_ok, 1)
                if kind == "rows":
                    dve.wait_ge(rows_ps, 1)
                    v.tensor_copy(sml[:, DCOL:DCOL + 2, :], bank[4][:, 0:16].rearrange("p (a u) -> p a u", a=2)).then_inc(dcol_ok, 1)
                    dve.wait_ge(dcol_ok, 1)
                    dve.wait_ge(expd_ok, 2)
                    ps = halves(0)
                    for u in range(NU):
                        ins = v.scalar_tensor_tensor(out=dmT[:, u, :], in0=ps[u], scalar=sml[:, DCOL, u:u + 1],
                                                     in1=negchunk[:, :], op0=ALU.subtract, op1=ALU.add)
                        if u < NU - 1:
                            c.mark(ins)
                    ins.then_inc(diff_ok, 1)
                    c.mark(v.tensor_copy(sml[:, KF, :], sml[:, DCOL, :]))
                    v.tensor_tensor(sml[:, TF, :], sml[:, DTOT, :], sml[:, DCOL, :], ALU.subtract).then_inc(fac_ok, 1)
                if kind == "l2":
                    dve.wait_ge(rs_ok, 1)
                    c.link(v.scalar_tensor_tensor(out=qT, in0=qT, scalar=DND ** -0.5, in1=rs, op0=ALU.mult, op1=ALU.mult))
                    v.tensor_copy(sml[:, E1, :], sml[:, BETA, :]).then_inc(qn_ok, 1)
                    dve.wait_ge(rs_ok, 2)
                    v.tensor_tensor(kT, kT, rs, ALU.mult).then_inc(kn_ok, 1)
                    dve.wait_ge(kn_ok, 1)
                    for h in range(2):
                        v.tensor_tensor(kbT[:, 4 * h:4 * h + 4, :].rearrange("p u q -> p (u q)"),
                                        kT[:, 4 * h:4 * h + 4, :].rearrange("p u q -> p (u q)"), bank[2 + h][:, :],
                                        ALU.mult).then_inc(kb_ok, 1)
                if kind == "turn":
                    dve.wait_ge(vt_ps, 1)
                    for h in range(2):
                        s = slice(4 * h, 4 * h + 4)
                        v.tensor_tensor(vbeta[:, s, :], bank[h][:, :].rearrange("p (u q) -> p u q", q=P),
                                        bc(sml[:, BETA, s], (P, 4, P)), ALU.mult).then_inc(vt_ok, 1)
                    dve.wait_ge(fac_exp, 1)
                    c.link(v.tensor_tensor(sml[:, KF, :], sml[:, KF, :], sml[:, BETA, :], ALU.mult))
                    dve.wait_ge(kt_ps, 1)
                    for h in range(2):
                        s = slice(4 * h, 4 * h + 4)
                        ps = bank[2 + h][:, :].rearrange("p (u q) -> p u q", q=P)
                        c.mark(v.tensor_tensor(kbe[:, s, :], ps, bc(sml[:, KF, s], (P, 4, P)), ALU.mult))
                        v.tensor_tensor(ktail[:, s, :], ps, bc(sml[:, TF, s], (P, 4, P)), ALU.mult).then_inc(kt_ok, 1)
                if kind == "gram":
                    dve.wait_ge(dm_ok, 1)
                    for m, dst in enumerate((mT, attnT)):
                        dve.wait_ge(gram_ps, m + 1)
                        for h in range(2):
                            v.tensor_tensor(dst[:, 4 * h:4 * h + 4, :].rearrange("p u q -> p (u q)"), bank[4 + 2 * m + h][:, :],
                                            dmT[:, 4 * h:4 * h + 4, :].rearrange("p u q -> p (u q)"), ALU.mult).then_inc(gram_ok, 1)
                    dve.wait_ge(expd_ok, 2)
                    dve.wait_ge(gram_ps, 2)
                    c.link(v.tensor_tensor(qT, qT, expd, ALU.mult))
                if kind == "level":
                    if n == 0:
                        dve.wait_ge(p1_ps, 1)
                        for h in range(2):
                            ins = v.scalar_tensor_tensor(
                                out=X[:, 4 * h:4 * h + 4, :], in0=bank[h][:, :].rearrange("p (u q) -> p u q", q=P), scalar=-1.0,
                                in1=ident[:, :].unsqueeze(1).to_broadcast((P, 4, P)),
                                op0=ALU.mult, op1=ALU.add)
                            if h == 0:
                                c.mark(ins)
                        ins.then_inc(x_ok, 1)
                        dve.wait_ge(bt_ok, 1)
                        v.scalar_tensor_tensor(out=XT, in0=btl, scalar=-1.0,
                                               in1=ident[:, :].unsqueeze(1).to_broadcast((P, NU, P)),
                                               op0=ALU.mult, op1=ALU.add).then_inc(xt_ok, 1)
                if kind == "delta":
                    for m, dst in enumerate((X, XT)):
                        if m == 0 and n == 5:
                            continue
                        dve.wait_ge((delta_ps, deltaT_ps)[m], n)
                        dve.wait_ge((x_ok, xt_ok)[m], n)
                        for h in range(2):
                            d = dst[:, 4 * h:4 * h + 4, :].rearrange("p u q -> p (u q)")
                            ins = v.tensor_tensor(d, d, bank[2 - 2 * m + h][:, :], ALU.subtract)
                            if h == 0:
                                c.mark(ins)
                        ins.then_inc((x_ok, xt_ok)[m], 1)
                if kind == "wu":
                    dve.wait_ge(wu_ps, 2)
                    for h in range(2):
                        v.tensor_copy(uu[:, 4 * h:4 * h + 4, :].rearrange("p u q -> p (u q)"), bank[2 + h][:, :]).then_inc(u_ok, 1)
                    dve.wait_ge(u_ok, 2)
                if kind == "chunk":
                    t, lo = n // 2, CH * (n % 2)
                    uh = uu[lo:lo + CH, :, :].rearrange("p (h t) q -> p t h q", t=NT)[:, t, :, :]
                    dve.wait_ge(vs_ps, n + 1)
                    v.tensor_tensor(vnew[lo:lo + CH, 4 * t:4 * t + 4, :], uh,
                                    bank[0][lo:lo + CH, :].rearrange("p (h q) -> p h q", q=P), ALU.subtract).then_inc(vn_ok, 1)
                    dve.wait_ge(st_ps, n + 1)
                    for h in range(DNH):
                        u = 2 * h + t
                        ins = v.scalar_tensor_tensor(out=state[:, h, :], in0=state[:, h, :],
                                                     scalar=expd[:, u, lo + CH - 1:lo + CH], in1=bank[2][:, h * P:(h + 1) * P],
                                                     op0=ALU.mult, op1=ALU.add)
                        if h < DNH - 1:
                            c.mark(ins)
                    ins.then_inc(st_ok, 1)
                    dve.wait_ge(st_ok, n + 1)
                if kind == "dn_out":
                    dve.wait_ge(osq_ok, NU)
                    v.tensor_scalar(sml[:, SSO, :], sml[:, E1, :], 1.0 / DND, EPS, ALU.mult, ALU.add).then_inc(so_ok, 1)
                    dve.wait_ge(ro_ok, 1)
                    dve.wait_ge(proj_got, 8)
                    c.link(v.tensor_tensor(yg, oo, gate[:, :, :].rearrange("p t (h q) -> p (t h) q", q=P), ALU.mult))
                    v.tensor_tensor(yg, yg, bc(sml[:, RSO, :], (P, NU, P)), ALU.mult).then_inc(yg_ok, 1)
                if kind == "score":
                    dve.wait_ge(e_ok, n + 1)
                    if n >= 2:
                        dve.wait_ge(rc_ps, n - 1)
                    v.scalar_tensor_tensor(out=sb_sp[:, n % 2, :], in0=z3[n % 2][:, 0:3 * P], scalar=0.0, in1=sb_e[:, n % 2, :],
                                           op0=ALU.max, op1=ALU.add).then_inc(sp3_ok, 1)
                if kind == "suffix":
                    dve.wait_ge(rc_ps, n + 1)
                    if n >= 2:
                        dve.wait_ge(ys_ps, n - 1)
                    v.tensor_tensor(sb_w[:, n % 2, :], bank[6][:, 0:3 * P], negcausal3[:, :, :].rearrange("p a b -> p (a b)"),
                                    ALU.add).then_inc(lw_ok, 1)
            for i in range(4):
                h, t = i // 2, i % 2
                dve.wait_ge(mix_ps, i + 1)
                ins = v.tensor_tensor(res[:, t, h * 512:(h + 1) * 512], res[:, t, h * 512:(h + 1) * 512], bank[i][:, :], ALU.add)
                if i < 3:
                    c.mark(ins)
            ins.then_inc(res_ok, 1)

            def route(l):
                tt, ts, stt, red = v.tensor_tensor, v.tensor_scalar, v.scalar_tensor_tensor, v.tensor_reduce
                c.mark(v.memset(gpad[:, :, NGRP:], -BIG))
                c.mark(v.memset(base_i[:, :, :], 0))
                dve.wait_ge(log_ps, l + 1)
                logits = bank[4][:, 0:128].rearrange("p (t n) -> p t n", t=NT)
                c.mark(v.tensor_copy(gpad[:, :, 0:NGRP], logits[:, :, 0:NGRP]))
                c.link(v.tensor_copy(elog[:, :, :], logits[:, :, NGRP:NGRP + NEXP]))
                for t in range(NT):
                    c.mark(v.max(top8[:, t, 0, :], gpad[:, t, :]))
                c.wait()
                for t in range(NT):
                    c.mark(v.max_index(idx8[:, t, 0, :], top8[:, t, 0, :], gpad[:, t, :]))
                ts(rv[:, 0, :, 0], top8[:, :, 0, 0], -1.0, None, ALU.mult).then_inc(glog_ok, 1)
                c.wait()
                c.link(v.tensor_copy(idxf[:, :, 0, :], idx8[:, :, 0, :]))
                c.link(tt(goh[:, :, :], iota_e[:, 0:NGRP].unsqueeze(1).to_broadcast((P, NT, NGRP)),
                          idxf[:, :, 0, 0:1].to_broadcast((P, NT, NGRP)), ALU.is_equal))
                for t in range(NT):
                    c.mark(tt(prod[:, t, :].rearrange("p (g e) -> p g e", g=NGRP), elog[:, t, :].rearrange("p (g e) -> p g e", g=NGRP),
                              bc(goh[:, t, :], (P, NGRP, PERG)), ALU.mult))
                c.wait()
                for t in range(NT):
                    c.mark(red(ingrp[:, t, :], prod[:, t, :].rearrange("p (g e) -> p e g", g=NGRP), AX.X, ALU.add))
                c.wait()
                for t in range(NT):
                    c.mark(v.max(top8[:, t, 1, :], ingrp[:, t, :]))
                c.wait()
                for t in range(NT):
                    c.mark(v.max_index(idx8[:, t, 1, :], top8[:, t, 1, :], ingrp[:, t, :]))
                tt(rv[:, 2, :, 0], top8[:, :, 1, 1], top8[:, :, 1, 0], ALU.subtract).then_inc(dv_ok, 1)
                c.wait()
                c.link(v.tensor_copy(idxf[:, :, 1, :], idx8[:, :, 1, :]))
                c.link(stt(out=rv[:, 4, :, :], in0=idxf[:, :, 0, 0:1].to_broadcast((P, NT, 2)), scalar=float(PERG),
                           in1=idxf[:, :, 1, 0:2], op0=ALU.mult, op1=ALU.add))
                c.link(tt(onehot[:, :, :, :].rearrange("p t r e -> p (t r) e"), iota_e[:, :].unsqueeze(1).to_broadcast((P, 4, NEXP)),
                          bc(rv[:, 4, :, :].rearrange("p t r -> p (t r)"), (P, 4, NEXP)), ALU.is_equal))
                tt(sel[:, :, :], onehot[:, :, 0, :], onehot[:, :, 1, :], ALU.add).then_inc(sel_ok, 1)
                dve.wait_ge(gexp_ok, 2 * l + 2)
                dve.wait_ge(wexp_ok, l + 1)
                c.mark(v.reciprocal(rv[:, 5, :, 0], rv[:, 1, :, 0]))
                c.link(ts(rv[:, 6, :, 0], rv[:, 3, :, 0], 1.0, None, ALU.add))
                c.link(v.reciprocal(rv[:, 6, :, 0], rv[:, 6, :, 0]))
                c.link(tt(rv[:, 7, :, 0], rv[:, 5, :, 0], rv[:, 6, :, 0], ALU.mult))
                c.link(tt(rv[:, 7, :, 1], rv[:, 7, :, 0], rv[:, 3, :, 0], ALU.mult))
                dve.wait_ge(pos_ps, l + 1)
                c.mark(v.tensor_copy(pos[:, :, :], bank[5][:, 0:2 * NEXP].rearrange("p (t e) -> p t e", t=NT)))
                c.link(v.tensor_copy(cnt[:, :], bank[5][:, 2 * NEXP:3 * NEXP]))
                c.link(v.tensor_tensor_scan(cum[:, :], ones[:, 0:NEXP], cnt[:, :], 0.0, ALU.mult, ALU.add))
                c.link(tt(base[:, :], cum[:, :], cnt[:, :], ALU.subtract))
                c.mark(v.tensor_copy(base_i[0:1, 0, 0:NEXP], base[0:1, :]))
                for n in range(1, PASSES):
                    c.mark(ts(base_i[0:1, n, 0:NEXP], base[0:1, :], float(n * CAP), float(SLOTS), ALU.add, ALU.min))
                c.link(red(most[:, :], cnt[:, :], AX.X, ALU.max))
                c.mark(v.tensor_copy(most_i[:, :], most[0:1, :]))
                c.link(tt(slot_all[:, :, :], pos[:, :, :], base[:, :].unsqueeze(1).to_broadcast((P, NT, NEXP)), ALU.add))
                for src, row in ((slot_all, 8), (pos, 9)):
                    for t in range(NT):
                        c.mark(tt(prod2[:, t, :, :], onehot[:, t, :, :], src[:, t:t + 1, :].to_broadcast((P, 2, NEXP)), ALU.mult))
                    c.wait()
                    c.link(red(rv[:, row, :, :].rearrange("p t r -> p (t r)"), prod2[:, :, :, :].rearrange("p t r e -> p (t r) e"), AX.X, ALU.add))
                dve.wait_ge(consts, 5 + l)
                for t in range(NT):
                    c.mark(ts(perm[:, t, :], iota_slot[:, :], rv[:, 8, t, 0:1], None, ALU.is_equal))
                c.wait()
                for t in range(NT):
                    stt(out=perm[:, t, :], in0=iota_slot[:, :], scalar=rv[:, 8, t, 1:2], in1=perm[:, t, :],
                        op0=ALU.is_equal, op1=ALU.add).then_inc(perm_ok, 1)
                pas = rv[:, 10, :, :]
                c.link(ts(pas, rv[:, 9, :, :], float(CAP), None, ALU.is_ge))
                for n in range(2, T // CAP):
                    c.link(stt(out=pas, in0=rv[:, 9, :, :], scalar=float(n * CAP), in1=pas, op0=ALU.is_ge, op1=ALU.add))
                c.link(stt(out=pas, in0=pas, scalar=float((NEXP - 1) * CAP), in1=rv[:, 9, :, :], op0=ALU.mult, op1=ALU.add))
                c.link(stt(out=pas, in0=rv[:, 4, :, :], scalar=float(CAP), in1=pas, op0=ALU.mult, op1=ALU.add))
                v.tensor_copy(yidx[:, :, :], pas).then_inc(routed, 1)

            def input_factor(f0, done=None):
                for q, (m, f) in enumerate(((0, 0), (1, 1), (1, 0), (0, 1))):
                    ins = v.tensor_tensor(b_prod[:, q, :, :], s5b[:, m, :, :], bc(s5t[:, f0 + f, :], (P, NS5, 16)), ALU.mult)
                    if done is None or q < 3:
                        c.mark(ins)
                c.wait()
                if done is not None:
                    ins.then_inc(done, 1)
                    dve.wait_ge(done, 1)

            def s5_layer():
                tt, ts, stt = v.tensor_tensor, v.tensor_scalar, v.scalar_tensor_tensor
                def spread(w, n):
                    for g_ in range(2):
                        r = slice(64 * g_, 64 * g_ + 64)
                        dst = w[r, :, :, :].rearrange("p m k (j c) -> p m (k j) c", c=32)[:, :, :, 16 * g_:16 * g_ + 16]
                        tt(dst[:, 0], b_prod[r, 0], b_prod[r, 1], ALU.subtract).then_inc(wb_ok, 1)
                        tt(dst[:, 1], b_prod[r, 2], b_prod[r, 3], ALU.add).then_inc(wb_ok, 1)

                dve.wait_ge(cT_ok, 6)
                t128 = [bc(turn128[:, m, :], (P, NS5, 32)) for m in range(2)]
                flat_c = lambda ap: ap.rearrange("p k (j c) -> p (k j) c", c=32)
                c.mark(tt(c_tmp_v[0], flat_c(cT[:, 0, :, :]), t128[0], ALU.mult))
                c.link(tt(c_tmp_v[1], flat_c(cT[:, 1, :, :]), t128[1], ALU.mult))
                tt(flat_c(cT2[:, 0, :, :]), c_tmp_v[0], c_tmp_v[1], ALU.add).then_inc(c2_re, 1)
                dve.wait_ge(wz_ok, 1)
                spread(wide, 0)
                dve.wait_ge(wb_ok, 4)
                input_factor(5, b2_ok)
                dve.wait_ge(wz_ok, 2)
                spread(wide2, 1)
                dve.wait_ge(wb_ok, 8)
                dve.wait_ge(ct_ps, 2)
                dve.wait_ge(bt_ps, 2)

                def tile(j, jj):
                    b = jj % 2
                    ps = bank[jj][:, :].rearrange("p (a t) -> p a t", t=S5C)
                    cs = [rot[:, m, bass.ds(j, 1), :].to_broadcast((P, 4, S5C)) for m in range(2)]
                    dve.wait_ge(bu_ps, j + 1)
                    tt(m_in[:, b, 0, :].rearrange("p (a t) -> p a t", t=S5C), ps, cs[0], ALU.mult).then_inc(mc_ok, 1)
                    tt(m_in[:, b, 1, :].rearrange("p (a t) -> p a t", t=S5C), ps, cs[1], ALU.mult).then_inc(ms_ok, 1)

                def scans(j, jj, first):
                    b = jj % 2
                    if not first:
                        dve.wait_ge(c_used, j - 1)
                    mag = s5t[:, 0, bass.ds(j, 1)]
                    dve.wait_ge(gin_ok, j * 2 + 2)
                    for m in range(2):
                        v.tensor_tensor_scan(gst[:, b, m, :], mag.to_broadcast((P, T)), gin[:, b, m, :], 0.0,
                                             ALU.mult, ALU.add).then_inc(gst_ok, 1)
                    dve.wait_ge(gst_ok, j * 2 + 2)
                    tt(m_out[:, b, 0, :].rearrange("p (a t) -> p a t", t=S5C), gst[:, b, :, :].rearrange("p m (a t) -> p (m a) t", t=S5C),
                       rot[:, 0, bass.ds(j, 1), :].to_broadcast((P, 4, S5C)), ALU.mult).then_inc(oc_ok, 1)

                def skip(k, par):
                    dve.wait_ge(c_used, k * 4 + 4)
                    s_ = bass.ds(k, 1)
                    u_, o_ = xT[:, s_, :].rearrange("p k t -> p (k t)"), yg5[:, s_, :].rearrange("p k t -> p (k t)")
                    stt(out=o_, in0=u_, scalar=s5d[:, s_], in1=bank[4 + par][:, 0:T], op0=ALU.mult, op1=ALU.add).then_inc(yd5_ok, 1)

                def chunk(k, par):
                    for jj in range(4):
                        tile(k * 4 + jj, jj)
                        scans(k * 4 + (jj - 1), (jj - 1) % 4, False)
                        if jj == 2:
                            skip(k - 1, par)

                tile(0, 0)
                for jj in range(3):
                    tile(jj + 1, jj + 1)
                    scans(jj, jj, jj < 2)
                with dve.Fori(0, KD // 2 - 1) as turn:
                    chunk(turn * 2 + 1, 0)
                    chunk(turn * 2 + 2, 1)
                chunk(KD - 1, 0)
                scans(NS5 - 1, 3, False)
                skip(KD - 1, 1)

            def glu():
                tt = v.tensor_tensor
                dve.wait_ge(bias_in, 16)
                for i in range(4):
                    h, t = i // 2, i % 2
                    z = m_in_f[:, i * 512:(i + 1) * 512]
                    dve.wait_ge(glu_ps, 4 * h + 2 + t + 1)
                    tt(z, bank[4 * h + 2 + t][:, :], bias_glu[:, D + h * 512:D + (h + 1) * 512], ALU.add).then_inc(gz_ok, 1)
                    y = m_out_f[:, i * 512:(i + 1) * 512]
                    c.link(tt(y, bank[4 * h + t][:, :], bias_glu[:, h * 512:(h + 1) * 512], ALU.add))
                    dve.wait_ge(gs_ok, i + 1)
                    c.link(tt(y, y, z, ALU.mult))
                    r = res[:, t, h * 512:(h + 1) * 512]
                    ins = tt(r, r, y, ALU.add)
                    if i < 3:
                        c.mark(ins)
                ins.then_inc(res_ok, 1)

            def experts(l):
                n0, x0 = NEXP * l, (NEXP + 2) * l
                route(l)
                c.link(v.memset(xs[:, :, SLOTS:], 0.0))
                for k in range(1, KD, 2):
                    dve.wait_ge(xs_ps, KD * l + k + 1)
                    v.tensor_scalar(xs[:, k, 0:SLOTS], bank[k % 4][:, :], gains[:, 1 + 2 * l, k:k + 1], None, ALU.mult).then_inc(xs_dve, 1)
                dve.wait_ge(xs_act, 4 * (l + 1))
                dve.wait_ge(xs_dve, 4 * (l + 1))

                def take(i, par):
                    first = v.value_load(base_i[0:1, 0, bass.ds(i, 1)], min_val=0, max_val=SLOTS)
                    v.tensor_copy(xe[:, par, :, :], xs[:, :, bass.ds(first, CAP)]).then_inc(xe_ok, 1)

                take(0, 0)
                take(1, 1)
                if l == 0:
                    dve.wait_ge(coarse_ok, 1)

                def step(i, par4, lap, first, last):
                    cur, prev = par4 % 2, (par4 + 1) % 2
                    if not last:
                        dve.wait_ge(ha_ok, i + (n0 + 1))
                        if not (isinstance(i, int) and i < 2):
                            dve.wait_ge(t_ps, i + (n0 - 1))
                        v.tensor_tensor(act_g[:, cur, :], act_a[:, cur, :], bank[cur][:, P:2 * P], ALU.mult).then_inc(hg_ok, 1)
                        take(i + 2, cur)
                        if l == 0:
                            ri = bass.ds(i, 1)
                            one = lambda tab, m: tab[:, m:m + 1, ri, :].rearrange("p m j n -> p (m j) n")
                            coarse = rot_c[:, :, ri, :].rearrange("p m j n -> p (m j) n")
                            if not (isinstance(i, int) and i == 0):
                                dve.wait_ge(rot_ok, i * 2)
                            for m in range(2):
                                v.tensor_tensor(rtmp[:, m, :, :, :], bc(coarse, (P, 2, 16, 8)),
                                                one(rot_f, m).unsqueeze(1).to_broadcast((P, 2, 16, 8)), ALU.mult).then_inc(rot_m, 1)
                            dve.wait_ge(rot_m, i * 2 + 2)
                            out_ = [rot[:, m, ri, :].rearrange("p j (n f) -> p (j n) f", f=8) for m in range(2)]
                            v.tensor_tensor(out_[0], rtmp[:, 0, 0, :, :], rtmp[:, 1, 1, :, :], ALU.subtract).then_inc(rot_ok, 1)
                            v.tensor_tensor(out_[1], rtmp[:, 0, 1, :, :], rtmp[:, 1, 0, :, :], ALU.add).then_inc(rot_ok, 1)

                pipeline(dve, step)
                dve.wait_ge(routed, l + 1)
                with dve.If(dve.value_load(most_i[0:1, 0:1], min_val=0, max_val=SLOTS) > CAP):
                    dve.wait_ge(xe_ok, (NEXP + 2) * (l + 1))
                    for r in range(PASSES - 1):
                        with dve.Fori(0, NEXP) as e:
                            n = e + r * NEXP
                            dve.wait_ge(more_step[l], n * STEPS)
                            first_slot = v.value_load(base_i[0:1, r + 1, bass.ds(e, 1)], min_val=0, max_val=SLOTS)
                            v.tensor_copy(xe[:, 0, :, :], xs[:, :, bass.ds(first_slot, CAP)]).then_inc(more_step[l], 1)
                            dve.wait_ge(more_step[l], n * STEPS + SILU)
                            v.tensor_tensor(act_g[:, 0, :], act_a[:, 0, :], bank[0][:, P:2 * P], ALU.mult).then_inc(more_step[l], 1)
                for t in range(NT):
                    for r in range(2):
                        dve.wait_ge(y_in[2 * t + r], 16 * (l + 1))
                        ins = v.scalar_tensor_tensor(out=res[:, t, :], in0=ygath[:, t, r, :], scalar=rv[:, 7, t, r:r + 1], in1=res[:, t, :],
                                                     op0=ALU.mult, op1=ALU.add)
                        if (t, r) != (NT - 1, 1):
                            c.link(ins)
                ins.then_inc(res_ok, 1)

            norm_a(1)
            norm_b(1)
            experts(0)
            dve.wait_ge(c_in, 32)
            dve.wait_ge(res_ok, 2)
            for h in range(2):
                v.tensor_scalar(wide_c[:, :, :, h, :].rearrange("p m k q -> p (m k) q"), s5c.rearrange("p m k q -> p (m k) q"),
                                cmask[:, h:h + 1], None, ALU.mult).then_inc(wc_ok, 1)
            norm_a(2)
            dve.wait_ge(raw_in, 32)
            input_factor(3)
            norm_b(2)
            s5_layer()
            glu()
            norm_a(3)
            norm_b(3)
            experts(1)
            norm_a(4)
            dve.wait_ge(fg_in, 16)
            dve.wait_ge(xn_ok, 10)
            for t in range(NT):
                v.tensor_tensor(xn[:, t, :], xn[:, t, :], gain_fin, ALU.mult).then_inc(fin_ok, 1)

        @block.tensor
        def _(pe):
            mm = nc.tensor.matmul

            def norm(n, contiguous=False):
                pe.wait_ge(xn_ok, 2 * n + 2)
                for b in range(4):
                    for k in (2 * b, 2 * b + 1):
                        for t in range(NT):
                            src = xn[:, t, k * P:(k + 1) * P] if contiguous else xn[:, t, k:D:KD]
                            ins = nc.tensor.transpose(bank[b][:, (k % 2) * T + t * P:(k % 2) * T + (t + 1) * P], src, ident[:, :])
                    ins.then_inc(xT_ps, 1)

            def xT_here(n):
                pe.wait_ge(xT_act, 4 * (n + 1))
                pe.wait_ge(xT_dve, 4 * (n + 1))

            def w_here(i):
                pe.wait_ge(w_in[i % NW], 16 * (i // NW + 1))

            pe.wait_ge(consts, 1)
            norm(0)
            xT_here(0)
            for i, name in enumerate(PROJ_BLOCKS):
                w_here(i)
                if i == 1:
                    pe.wait_ge(consts, 4)
                    pe.wait_ge(par_in, 16 * N_PAR)
                    nc.tensor.transpose(bank[7][:, 0:TAPS * 12], convw_rows[:, :], ident[0:TAPS * 12, 0:TAPS * 12]).then_inc(cw_ps, 1)
                    pe.wait_ge(cw_ok, 1)
                if i >= 2:
                    pe.wait_ge(proj_got, 2 * (i - 1))
                w = ring_w[:, i % NW, :, :]
                for h in range(2):
                    ps = bank[4 + 2 * (i % 2) + h]
                    if name in ("gate", "sb_v"):
                        for k in range(KD):
                            ins = mm(ps[:, :], xT[:, k, h * P:(h + 1) * P], w[:, k, :], start=(k == 0), stop=(k == KD - 1))
                    else:
                        for cc in range(2):
                            col = (2 * h + cc) * P
                            for k in range(KD):
                                ins = mm(ps[:, cc * T:(cc + 1) * T], w[:, k, col:col + P], xT[:, k, :], start=(k == 0), stop=(k == KD - 1))
                    ins.then_inc(proj_ps, 1)
                if i == 3:
                    for t in range(NT):
                        for k in range(KD):
                            ins = mm(bank[0][:, 8 * t:8 * t + 8], xT[:, k, t * P:(t + 1) * P], wba[:, k, :], start=(k == 0), stop=(k == KD - 1))
                    ins.then_inc(ba_ps, 1)
            pe.wait_ge(s5_par, 1)
            pe.wait_ge(proj_got, 12)
            for n, row in enumerate((MAG, COS, SIN, CRE, CIM)):
                ins = nc.tensor.transpose(bank[7][:, n * NS5:(n + 1) * NS5], s5w[:, row, :], ident[0:NS5, 0:NS5])
            nc.tensor.transpose(bank[7][:, 5 * NS5:5 * NS5 + 2 * KD], s5w[0:2 * KD, VEC, :], ident[0:2 * KD, 0:2 * KD]).then_inc(s5_tps, 1)
            for kind, n in plan:
                if kind == "rows":
                    pe.wait_ge(g_ok, 1)
                    pe.wait_ge(proj_got, 14)
                    ps, ps2 = halves(0), halves(2)
                    for u in range(NU):
                        mm(ps[u], sml[:, G, u:u + 1].to_broadcast((P, P)), chunk_incl[:, :], start=True, stop=True)
                        mm(ps2[u], sml[:, BETA, u:u + 1].to_broadcast((P, P)), ident[:, :], start=True, stop=True)
                    mm(bank[4][:, 0:8], chunk_incl[:, :], sml[:, G, :], start=True, stop=True)
                    mm(bank[4][:, 8:16], chunk_ones[:, :], sml[:, G, :], start=True, stop=True).then_inc(rows_ps, 1)
                if kind == "l2":
                    for m, sq in enumerate((sq_q, sq_k)):
                        pe.wait_ge(sq_ok, m + 1)
                        pe.wait_ge(s5t_ok, 1)
                        if m:
                            pe.wait_ge(dcol_ok, 1)
                        for h in range(2):
                            ins = mm(bank[(6, 4)[m] + h][:, :], ones[:, :], sq[:, 4 * h:4 * h + 4, :].rearrange("p u q -> p (u q)"),
                                     start=True, stop=True)
                        ins.then_inc(ssum_ps, 1)
                if kind == "turn":
                    pe.wait_ge(silu_ok, 3)
                    pe.wait_ge(expd_ok, 2)
                    pe.wait_ge(diff_ok, 1)
                    for u, ps in enumerate(halves(0)):
                        ins = nc.tensor.transpose(ps, vT[:, u, :], ident[:, :])
                    ins.then_inc(vt_ps, 1)
                    pe.wait_ge(kn_ok, 1)
                    pe.wait_ge(kb_ok, 2)
                    for u, ps in enumerate(halves(2)):
                        ins = nc.tensor.transpose(ps, kT[:, u, :], ident[:, :])
                    ins.then_inc(kt_ps, 1)
                if kind == "gram":
                    pe.wait_ge(rs_ok, 2)
                    pe.wait_ge(qn_ok, 1)
                    for m, rhs in enumerate((kbT, qT)):
                        for u, ps in enumerate(halves(4 + 2 * m)):
                            ins = mm(ps, kT[:, u, :], rhs[:, u, :], start=True, stop=True)
                        ins.then_inc(gram_ps, 1)
                if kind == "level":
                    pe.wait_ge(bt_ok, n + 1)
                    if n == 0:
                        pe.wait_ge(vt_ok, 2)
                        for u, ps in enumerate(halves(0)):
                            ins = nc.tensor.transpose(ps, btl[:, u, :], ident[:, :])
                        ins.then_inc(p1_ps, 1)
                    else:
                        pe.wait_ge(x_ok, n)
                        pe.wait_ge(xt_ok, n)
                        for u, ps in enumerate(halves(0)):
                            ins = mm(ps, btl[:, u, :], X[:, u, :], start=True, stop=True)
                        ins.then_inc(p1_ps, 1)
                if kind == "delta":
                    pe.wait_ge(p1_ok, 2 * n)
                    pe.wait_ge(xt_ok, n)
                    if n == 1:
                        pe.wait_ge(kt_ok, 2)
                    if n < 5:
                        for u, ps in enumerate(halves(2)):
                            ins = mm(ps, XT[:, u, :], P1[:, u, :], start=True, stop=True)
                        ins.then_inc(delta_ps, 1)
                    for u, ps in enumerate(halves(0)):
                        ins = mm(ps, P1[:, u, :], XT[:, u, :], start=True, stop=True)
                    ins.then_inc(deltaT_ps, 1)
                if kind == "wu":
                    pe.wait_ge(xt_ok, 6)
                    for u, ps in enumerate(halves(0)):
                        ins = mm(ps, kbe[:, u, :], XT[:, u, :], start=True, stop=True)
                    ins.then_inc(wu_ps, 1)
                    for u, ps in enumerate(halves(2)):
                        ins = mm(ps, XT[:, u, :], vbeta[:, u, :], start=True, stop=True)
                    ins.then_inc(wu_ps, 1)
                if kind == "chunk":
                    t, lo = n // 2, CH * (n % 2)
                    part = slice(lo, lo + CH)
                    if n == 0:
                        pe.wait_ge(wT_ok, 2)
                        pe.wait_ge(u_ok, 2)
                        pe.wait_ge(consts, 4)
                    else:
                        pe.wait_ge(st_ok, n)
                        pe.wait_ge(o_ok, n)
                    for h in range(DNH):
                        ins = mm(bank[0][part, h * P:(h + 1) * P], wT[:, 2 * h + t, part], state[:, h, :], start=True, stop=True)
                    ins.then_inc(vs_ps, 1)
                    pe.wait_ge(vn_ok, n + 1)
                    for h in range(DNH):
                        u = 2 * h + t
                        mm(bank[1][part, h * P:(h + 1) * P], qT[:, u, part], state[:, h, :], start=True, stop=False)
                        ins = mm(bank[1][part, h * P:(h + 1) * P], attnT[part, u, part], vnew[part, 4 * t + h, :], start=False, stop=True)
                    ins.then_inc(o_ps, 1)
                    for h in range(DNH):
                        ins = mm(bank[2][:, h * P:(h + 1) * P], ktail[part, 2 * h + t, :], vnew[part, 4 * t + h, :], start=True, stop=True)
                    ins.then_inc(st_ps, 1)
                if kind == "dn_out":
                    pe.wait_ge(yg_ok, 1)
                    for t in range(NT):
                        for h in range(DNH):
                            ins = nc.tensor.transpose(bank[h // 2][:, (h % 2) * T + t * P:(h % 2) * T + (t + 1) * P],
                                                      yg[:, 4 * t + h, :], ident[:, :])
                    ins.then_inc(yd_ps, 1)
                hp, q2 = slice(64 * (n % 2), 64 * (n % 2) + 64), n // 2
                if kind == "score":
                    if n == 0:
                        pe.wait_ge(gram_ok, 4)
                    if n >= 2:
                        pe.wait_ge(sp3_ok, n - 1)
                    mm(z3[n % 2][:, 0:T], sbkT[hp, q2, 0:P], sbqT[hp, q2, :], start=True, stop=True)
                    mm(z3[n % 2][:, T:3 * P], sbkT[hp, q2, P:T], sbqT[hp, q2, P:T], start=True, stop=True).then_inc(z_ps, 1)
                if kind == "suffix":
                    pe.wait_ge(spm_ok, n + 1)
                    if n >= 1:
                        pe.wait_ge(lw_ok, n)
                    s = sb_sp[:, n % 2, :]
                    r = bank[6]
                    mm(r[:, 0:T], sbkT[hp, q2, 0:P], sbqT[hp, q2, :], start=True, stop=False)
                    mm(r[:, 0:T], neg_upto[:, :], s[:, 0:T], start=False, stop=False)
                    mm(r[:, P:T], neg_ones[:, :], s[:, T:3 * P], start=False, stop=True)
                    mm(r[:, T:3 * P], sbkT[hp, q2, P:T], sbqT[hp, q2, P:T], start=True, stop=False)
                    mm(r[:, T:3 * P], neg_upto[:, :], s[:, T:3 * P], start=False, stop=True).then_inc(rc_ps, 1)
                if kind == "mixv":
                    pe.wait_ge(w_ok, n + 1)
                    if n >= 2 and n % 2 == 0:
                        pe.wait_ge(ys_ok, n // 2)
                    o = bank[7][hp, 0:T]
                    w = sb_w[:, n % 2, :]
                    mm(o, sbv[:, 0, n * SBD:(n + 1) * SBD], w[:, 0:T], start=True, stop=False)
                    mm(o[:, P:T], sbv[:, 1, n * SBD:(n + 1) * SBD], w[:, T:3 * P], start=False, stop=True).then_inc(ys_ps, 1)
            pe.wait_ge(yd_ok, 2)
            pe.wait_ge(ys_ok, 4)
            for h in range(2):
                w_here(W_OUT0 + h)
                for t in range(NT):
                    for k in range(KD):
                        ins = mm(bank[2 * h + t][:, :], yT[:, k, t * P:(t + 1) * P], ring_w[:, (W_OUT0 + h) % NW, k, :],
                                 start=(k == 0), stop=(k == KD - 1))
                    ins.then_inc(mix_ps, 1)

            def experts(l):
                n0, x0, w0 = NEXP * l, (NEXP + 2) * l, W_EXP[l]
                for t in range(NT):
                    for k in range(KD):
                        ins = mm(bank[4][:, 64 * t:64 * t + NGRP + NEXP], xT[:, k, t * P:(t + 1) * P], wr[:, l, k, :],
                                 start=(k == 0), stop=(k == KD - 1))
                ins.then_inc(log_ps, 1)
                pe.wait_ge(sel_ok, l + 1)
                b5 = bank[5]
                mm(b5[:, 0:NEXP], before[:, :], sel[:, 0, :], start=True, stop=True)
                mm(b5[:, NEXP:2 * NEXP], before[:, :], sel[:, 1, :], start=True, stop=False)
                mm(b5[:, NEXP:2 * NEXP], ones[:, :], sel[:, 0, :], start=False, stop=True)
                mm(b5[:, 2 * NEXP:3 * NEXP], ones[:, :], sel[:, 0, :], start=True, stop=False)
                mm(b5[:, 2 * NEXP:3 * NEXP], ones[:, :], sel[:, 1, :], start=False, stop=True).then_inc(pos_ps, 1)
                pe.wait_ge(perm_ok, 2 * (l + 1))
                for k in range(KD):
                    if k >= 4:
                        pe.wait_ge((xs_act, xs_dve)[k % 2], 4 * l + (k - 4) // 2 + 1)
                    for t in range(NT):
                        ins = mm(bank[k % 4][:, :], xn[:, t, k:D:KD], perm[:, t, :], start=(t == 0), stop=(t == NT - 1))
                    ins.then_inc(xs_ps, 1)
                pe.wait_ge(xs_act, 4 * (l + 1))
                pe.wait_ge(xs_dve, 4 * (l + 1))

                def step(i, par4, lap, first, last):
                    cur, prev = par4 % 2, (par4 + 1) % 2
                    if not last:
                        pe.wait_ge(xe_ok, i + (x0 + 1))
                        slot, more = (w0 + par4) % NW, (w0 + par4) // NW
                        pe.wait_ge(w_in[slot], lap * 16 + 16 * (more + 1))
                        if not (isinstance(i, int) and i < 2):
                            pe.wait_ge(hg_ok, i + (n0 - 1))

                        def hidden(k):
                            for g in range(2):
                                w = ring_w[:, slot, k, :].rearrange("p (m g f) -> p g m f", m=2, g=2)[:, g, :, :]
                                ins = mm(bank[cur][g * CAP:(g + 1) * CAP, 0:2 * P], xe[:, cur, k, :], w,
                                         start=(k == 0), stop=(k == KD - 1))
                            return ins

                        for k in range(KD // 2):
                            if k == KD // 2 - 1 and not first:
                                pe.wait_ge(hg_ok, i + n0)
                            hidden(k)
                    if not first:
                        if last:
                            pe.wait_ge(hg_ok, i + n0)
                        nc.tensor.transpose(bank[2][:, 0:P], act_g[:, prev, :], ident[:, :]).then_inc(t_ps, 1)
                    if not last:
                        for k in range(KD // 2, KD):
                            ins = hidden(k)
                        ins.then_inc(h_ps, 1)
                    if not first:
                        pe.wait_ge(gt_ok, i + n0)
                        vs, vmore = (par4 - 1) % NV, (NEXP * l + par4 - 1) // NV
                        pe.wait_ge(v_in[vs], lap * 16 + 16 * (vmore + 1))
                        if not (isinstance(i, int) and i < 2):
                            pe.wait_ge(ya_ok, i + (n0 - 1))
                        for k in range(2):
                            for h2 in range(2):
                                ins = mm(bank[3][h2 * CAP:(h2 + 1) * CAP, :], act_gT[:, prev, k * CAP:(k + 1) * CAP],
                                         ring_v[:, vs, k, h2 * 512:(h2 + 1) * 512], start=(k == 0), stop=(k == 1))
                        ins.then_inc(y_ps, 1)

                pipeline(pe, step)
                pe.wait_ge(routed, l + 1)
                with pe.If(pe.value_load(most_i[0:1, 0:1], min_val=0, max_val=SLOTS) > CAP):
                    pe.wait_ge(ya_ok, NEXP * (l + 1))
                    for r in range(PASSES - 1):
                        with pe.Fori(0, NEXP) as e:
                            n = e + r * NEXP
                            pe.wait_ge(more_in[l], n * 32 + 32)
                            pe.wait_ge(more_step[l], n * STEPS + XE)
                            for k in range(KD):
                                for g in range(2):
                                    w = ring_w[:, 0, k, :].rearrange("p (m g f) -> p g m f", m=2, g=2)[:, g, :, :]
                                    ins = mm(bank[0][g * CAP:(g + 1) * CAP, 0:2 * P], xe[:, 0, k, :], w, start=(k == 0), stop=(k == KD - 1))
                            ins.then_inc(more_step[l], 1)
                            pe.wait_ge(more_step[l], n * STEPS + GATED)
                            mm(bank[2][0:1, P:P + 1], ones[:, 0:1], ones[:, 0:1], start=True, stop=True)
                            nc.tensor.transpose(bank[2][:, 0:P], act_g[:, 0, :], ident[:, :]).then_inc(more_step[l], 1)
                            pe.wait_ge(more_step[l], n * STEPS + GT)
                            for k in range(2):
                                for h2 in range(2):
                                    ins = mm(bank[3][h2 * CAP:(h2 + 1) * CAP, :], act_gT[:, 0, k * CAP:(k + 1) * CAP],
                                             ring_v[:, 0, k, h2 * 512:(h2 + 1) * 512], start=(k == 0), stop=(k == 1))
                            ins.then_inc(more_step[l], 1)

            def turn_weights(src, ps0, done):
                for m in range(2):
                    for k in range(KD):
                        ins = nc.tensor.transpose(bank[ps0 + 2 * m + k // 4][:, (k % 4) * P:(k % 4 + 1) * P], src(m, k), ident[:, :])
                    ins.then_inc(done, 1)

            def s5_layer():
                xT_here(2)
                pe.wait_ge(wb_ok, 4)
                turn_weights(lambda m, k: wide[:, m, k, :], 0, bt_ps)
                pe.wait_ge(wb_ok, 8)
                pe.wait_ge(bT_ok, 4)
                turn_weights(lambda m, k: wide2[:, m, k, :], 0, bt_ps)
                pe.wait_ge(bT_ok, 8)

                def drive(j):
                    k, r = j // 4, slice(32 * (j % 4), 32 * (j % 4) + 32)
                    if j >= 4:
                        pe.wait_ge(ms_ok, j - 3)
                    for m in range(2):
                        for n, w in enumerate((bT, bT2)):
                            ins = mm(bank[j % 4][:, m * T + n * P:m * T + (n + 1) * P], w[r, m, k, :], xT[r, k, n * P:(n + 1) * P],
                                     start=True, stop=True)
                    ins.then_inc(bu_ps, 1)

                def read(j):
                    k, r = j // 4, slice(32 * (j % 4), 32 * (j % 4) + 32)
                    pe.wait_ge(oc_ok, j + 1)
                    pe.wait_ge(os_ok, j + 1)
                    if j % 4 == 0 and k >= 2:
                        pe.wait_ge(yd5_ok, k - 1)
                    mo = m_out[:, j % 2, :, :]
                    for n, (w, wn) in enumerate(((cT, cTn), (cT2, cTn2))):
                        o = bank[4 + k % 2][r, n * P:(n + 1) * P]
                        re, im = slice(n * P, (n + 1) * P), slice(T + n * P, T + (n + 1) * P)
                        mm(o, w[:, 0, k, r], mo[:, 0, re], start=True, stop=False)
                        mm(o, w[:, 1, k, r], mo[:, 0, im], start=False, stop=False)
                        mm(o, wn[:, k, r], mo[:, 1, im], start=False, stop=False)
                        ins = mm(o, w[:, 1, k, r], mo[:, 1, re], start=False, stop=True)
                    ins.then_inc(c_used, 1)

                for j in range(3):
                    drive(j)
                pe.wait_ge(cT_ok, 7)
                pe.wait_ge(c2_ok, 1)
                for j in range(NS5):
                    if j + 3 < NS5:
                        drive(j + 3)
                    read(j)
                pe.wait_ge(gelu_ok, KD)
                for b in range(4):
                    w_here(W_GLU + b)
                    for t in range(NT):
                        for k in range(KD):
                            ins = mm(bank[2 * b + t][:, :], yg5[:, k, t * P:(t + 1) * P], ring_w[:, (W_GLU + b) % NW, k, :],
                                     start=(k == 0), stop=(k == KD - 1))
                        ins.then_inc(glu_ps, 1)

            norm(1)
            xT_here(1)
            experts(0)
            pe.wait_ge(wc_ok, 2)
            turn_weights(lambda m, k: wide_c[:, m, k, :, :].rearrange("p h q -> p (h q)"), 4, ct_ps)
            norm(2, contiguous=True)
            xT_here(2)
            s5_layer()
            norm(3)
            xT_here(3)
            experts(1)


_INS = ['x', 'mix_norm_even', 'w_in_even', 'dn_conv_w', 'dn_a_log', 'dn_dt_bias', 'dn_out_norm', 'w_out_even',
        'mix_norm_odd', 's5_lambda_re', 's5_lambda_im', 's5_log_step', 's5_b_re', 's5_b_im', 's5_c_re', 's5_c_im',
        's5_d', 'w_glu', 'b_glu', 'ffn_norm', 'w_router_group', 'w_router_expert', 'w_expert_in', 'w_expert_out',
        'final_norm']


def kernel(**inputs):
    import numpy as _np
    import concourse.bacc as _bacc
    from concourse import mybir as _mybir
    from concourse.bass_utils import run_bass_kernel_spmd as _run

    nc = _bacc.Bacc("TRN2", target_bir_lowering=False, num_devices=1)
    arrays, args = {}, []
    for name in _INS:
        a = _np.ascontiguousarray(inputs[name])
        arrays[f"in_{name}"] = a
        args.append(nc.dram_tensor(f"in_{name}", a.shape, _mybir.dt.from_np(a.dtype), kind="ExternalInput").ap())
    args.append(nc.dram_tensor("out", (1, T, D), F32, kind="ExternalOutput").ap())
    trunk(nc, *args)
    r = _run(nc, [arrays], core_ids=[0])
    return r.results[0]["out"]
```

```python
from contextlib import ExitStack

import concourse.bass as bass
from concourse import mybir

P = 128
T = 256
NT = T // P
D = 1024
KD = D // P
SBH, SBD = 8, 64
DNH, DND = 4, 128
TAPS = 4
CH = 64
NU = DNH * NT
NEXP, NGRP, PERG = 32, 4, 8
FF = 256
CAP = 64
PASSES = T // CAP
NP = NEXP // 2
SLOTS = 2 * T
NS5 = 32
S5C = 128
NW, NV = 4, 4
EPS = 1e-6
BIG = 1e30

F32 = mybir.dt.float32
I32 = mybir.dt.int32
U32 = mybir.dt.uint32
ALU = mybir.AluOpType
ACT = mybir.ActivationFunctionType
AX = mybir.AxisListType

PROJ_BLOCKS = ["dn_q", "dn_k", "dn_v", "sb_q", "sb_k", "sb_v", "gate"]
PROJ_COL = {"sb_q": 0, "sb_k": 512, "sb_v": 1024, "dn_q": 1536, "dn_k": 2048, "dn_v": 2560, "gate": 3080}
W_OUT0 = len(PROJ_BLOCKS)
W_GLU = W_OUT0 + NEXP
W_EXP = [W_OUT0, W_GLU + 2]

N_PAR = 16

TWO_PI = (6.28125, 0.0019350051879882812, 3.0199159795074593e-07)
ROUND = 1.5 * 2.0 ** 23
PI = 3.141592502593994
EXP_LN = "natural_log_exp_and_others"


class Chain:

    def __init__(self, eng, sem):
        self.eng, self.sem, self.n = eng, sem, 0

    def mark(self, ins):
        ins.then_inc(self.sem, 1)
        self.n += 1

    def wait(self):
        self.eng.wait_ge(self.sem, self.n)

    def link(self, ins):
        self.mark(ins)
        self.wait()


def bc(ap, shape):
    return ap.unsqueeze(len(ap.shape)).to_broadcast(shape)


def trunk(nc, x, mix_norm_even, w_in_even, dn_conv_w, dn_a_log, dn_dt_bias, dn_out_norm, w_out_even,
          mix_norm_odd, s5_lambda_re, s5_lambda_im, s5_log_step, s5_b_re, s5_b_im, s5_c_re, s5_c_im,
          s5_d, w_glu, b_glu, ffn_norm, w_router_group, w_router_expert, w_expert_in, w_expert_out,
          final_norm, out):
    ctx = ExitStack()
    with ctx:
        def sb(name, shape, dt=F32, stack=ctx):
            return stack.enter_context(nc.sbuf_tensor(name, shape, dt))

        def sem(name):
            return ctx.enter_context(nc.semaphore(name))

        bank = [ctx.enter_context(nc.psum_tensor(f"bank{i}", [P, 512], F32)) for i in range(8)]

        def halves(b0, n=P):
            return [bank[b0 + u // 4][:, (u % 4) * P:(u % 4) * P + n] for u in range(NU)]

        ring_w = sb("ring_w", [P, NW, KD, 512])
        ring_v = sb("ring_v", [P, NV, 2, D])
        res = sb("res", [P, NT, D])
        xn = sb("xn", [P, NT, D])
        xT = sb("xT", [P, KD, T])
        gains = sb("gains", [P, 4, KD])
        ssq = sb("ssq", [P, 5, NT])
        msq = sb("msq", [P, 5, NT])
        rstd = sb("rstd", [P, 5, NT])
        neghalf = sb("neghalf", [P, NU])
        one_col = sb("one_col", [P, 1])
        ident = sb("ident", [P, P])
        ones = sb("ones", [P, P])
        before = sb("before", [P, P])

        wr = sb("wr", [P, 2, KD, NGRP + NEXP])
        iota_e = sb("iota_e", [P, NEXP])
        row_no = sb("row_no", [P, PASSES * NP])

        s5t = sb("s5t", [P, 7, NS5])
        cmask = sb("cmask", [P, 2])
        s5d = sb("s5d", [P, KD])

        mixer = ExitStack()
        neg_upto = sb("neg_upto", [P, P], stack=mixer)
        neg_ones = sb("neg_ones", [P, P], stack=mixer)
        causal3 = sb("causal3", [P, 3, P], stack=mixer)
        negcausal3 = sb("negcausal3", [P, 3, P], stack=mixer)
        chunk_incl = sb("chunk_incl", [P, P], stack=mixer)
        negchunk = sb("negchunk", [P, P], stack=mixer)
        chunk_ones = sb("chunk_ones", [P, P], stack=mixer)
        level = sb("level", [P, 6, P], stack=mixer)
        wba = sb("wba", [P, KD, 8], stack=mixer)
        convw_rows = sb("convw_rows", [TAPS * 12, P], stack=mixer)
        convw = sb("convw", [P, TAPS * 12], stack=mixer)
        dn_par = sb("dn_par", [P, 2, DNH], stack=mixer)
        neg_a = sb("neg_a", [P, DNH], stack=mixer)
        out_gain = sb("out_gain", [P, 1], stack=mixer)
        eps_col = sb("eps_col", [P, 1], stack=mixer)
        raw = sb("raw", [P, 12, TAPS - 1 + T], stack=mixer)
        qkvT = sb("qkvT", [P, 12, T], stack=mixer)
        gate = sb("gate", [P, NT, 512], stack=mixer)
        sbqT = sb("sbqT", [P, 4, T], stack=mixer)
        sbkT = sb("sbkT", [P, 4, T], stack=mixer)
        sbv = sb("sbv", [P, NT, 512], stack=mixer)
        yT = sb("yT", [P, KD, T], stack=mixer)
        ba = sb("ba", [P, NT, 8], stack=mixer)
        sml = sb("sml", [P, 16, NU], stack=mixer)
        state = sb("state", [P, DNH, DND], stack=mixer)
        sb_e = sb("sb_e", [P, 2, 3 * P], stack=mixer)
        sb_sp = sb("sb_sp", [P, 2, 3 * P], stack=mixer)
        sb_w = sb("sb_w", [P, 2, 3 * P], stack=mixer)
        mixer.close()

        def mat(ap):
            return ap.rearrange("p (u q) -> p u q", q=P)

        dmT, expd, btl, X, XT, P1, kbe, ktail = [mat(ring_v[:, m // 2, m % 2, :]) for m in range(8)]
        raw_flat = raw[:, :, :].rearrange("p c t -> p (c t)")
        vbeta, wT, uu = [mat(raw_flat[:, m * D:(m + 1) * D]) for m in range(3)]
        mT, attnT = [mat(xn[:, m, :]) for m in range(2)]
        qT = mat(qkvT[:, 0:4, :].rearrange("p c t -> p (c t)"))
        kT = mat(qkvT[:, 4:8, :].rearrange("p c t -> p (c t)"))
        vT = mat(qkvT[:, 8:12, :].rearrange("p c t -> p (c t)"))
        sq_q, sq_k, kbT = btl, X, P1
        rs = [XT, dmT]
        vnew, oo, yg = X, P1, btl
        BETA, G, SP_, E1, T1, DCOL, DTOT, KF, TF, SSO, RSO = range(11)

        s5w = yT[0:NS5, :, :].rearrange("p k t -> p (k t)").rearrange("p (n s) -> p n s", s=P)
        LRE, LIM, THE, TK, TR, TH, MAG, COS, SIN, DEN, NRE, CRE, CIM, TMP, VEC = range(15)
        s5dt = yT[0:NS5, 7, 250:252]

        rot = sb("rot", [P, 2, NS5, S5C])
        rot_f = sb("rot_f", [P, 2, NS5, 8])
        rot_c = sb("rot_c", [P, 2, NS5, 16])
        turn128 = sb("turn128", [P, 2, NS5])

        moe = ExitStack()
        iota_slot = sb("iota_slot", [P, SLOTS], stack=moe)
        s5tmp = sb("s5tmp", [P, 4, NS5, 8], stack=moe)
        xs = sb("xs", [P, KD, SLOTS + CAP], stack=moe)
        perm = sb("perm", [P, NT, SLOTS], stack=moe)
        xe = sb("xe", [P, KD, 2 * CAP], stack=moe)
        act_a = sb("act_a", [P, FF], stack=moe)
        act_g = sb("act_g", [P, FF], stack=moe)
        act_gT = sb("act_gT", [P, 2, 2 * CAP], stack=moe)
        yrow = sb("yrow", [P, D], stack=moe)
        gpad = sb("gpad", [P, NT, 8], stack=moe)
        elog = sb("elog", [P, NT, NEXP], stack=moe)
        top8 = sb("top8", [P, NT, 2, 8], stack=moe)
        idx8 = sb("idx8", [P, NT, 2, 8], U32, stack=moe)
        idxf = sb("idxf", [P, NT, 2, 8], stack=moe)
        goh = sb("goh", [P, NT, NGRP], stack=moe)
        prod = sb("prod", [P, NT, NEXP], stack=moe)
        ingrp = sb("ingrp", [P, NT, 8], stack=moe)
        rv = sb("rv", [P, 12, NT, 2], stack=moe)
        gexp = sb("gexp", [P, NT, NGRP], stack=moe)
        onehot = sb("onehot", [P, NT, 2, NEXP], stack=moe)
        sel = sb("sel", [P, NT, NEXP], stack=moe)
        pos = sb("pos", [P, NT, NEXP], stack=moe)
        cnt = sb("cnt", [P, NEXP], stack=moe)
        base = sb("base", [P, NEXP], stack=moe)
        slot_all = sb("slot_all", [P, NT, NEXP], stack=moe)
        prod2 = sb("prod2", [P, NT, 2, NEXP], stack=moe)
        base_i = sb("base_i", [1, PASSES, NEXP + 2], I32, stack=moe)
        most = sb("most", [P, 1], stack=moe)
        most_i = sb("most_i", [1, 1], I32, stack=moe)
        pick_part = sb("pick_part", [P, T], stack=moe)
        moe.close()
        rtmp = s5tmp[:, 0:2, :, :].rearrange("p m (r n) f -> p m r n f", r=2)
        pick = iota_slot[:, :].rearrange("p (b c) -> p b c", b=2)
        cum = prod[:, 0, :]
        key_row, weight_row = [perm[:, m, :].rearrange("p (r c) -> p r c", r=2) for m in range(2)]

        s5 = ExitStack()
        bT = sb("bT", [P, 2, KD, P], stack=s5)
        cT = sb("cT", [P, 2, KD, P], stack=s5)
        wide = sb("wide", [P, 2, KD, P], stack=s5)
        m_in = sb("m_in", [P, 2, 2, 2 * T], stack=s5)
        m_out = sb("m_out", [P, 2, 2, 2 * T], stack=s5)
        s5.close()
        def in_ring(slot, half=None):
            ap = ring_v[:, slot, :, :] if half is None else ring_v[:, slot, half, :]
            return ap
        cT2 = in_ring(0).rearrange("p m (k q) -> p m k q", k=KD)
        cTn, cTn2 = [in_ring(1, h).rearrange("p (k q) -> p k q", k=KD) for h in range(2)]
        bT2 = in_ring(2).rearrange("p m (k q) -> p m k q", k=KD)
        wide2 = in_ring(3).rearrange("p m (k q) -> p m k q", k=KD)
        c_tmp_g = [in_ring(1, 1).rearrange("p (j c) -> p j c", c=32), in_ring(0, 1).rearrange("p (j c) -> p j c", c=32)]
        flat = lambda ap: ap.rearrange("p a k q -> p (a k q)")
        wide_f = flat(wide[:, :, :, :])
        gin = wide_f[:, 0:1024].rearrange("p (b m t) -> p b m t", b=2, m=2)
        gst = wide_f[:, 1024:2048].rearrange("p (b m t) -> p b m t", b=2, m=2)
        c_tmp_v = [m_in[:, :, :, :].rearrange("p a b c -> p (a b c)")[:, m * 1024:(m + 1) * 1024].rearrange("p (j c) -> p j c", c=32) for m in range(2)]
        m_out_f, m_in_f = [m[:, :, :, :].rearrange("p a b c -> p (a b c)") for m in (m_out, m_in)]
        b_prod = m_out_f.rearrange("p (n j c) -> p n j c", n=4, c=16)
        wide_c = m_in_f.rearrange("p (m k h q) -> p m k h q", m=2, k=KD, h=2)
        s5b = ring_v[:, 2, 1, :].rearrange("p (m j c) -> p m j c", m=2, c=16)
        s5c = ring_v[:, 2, 0, :].rearrange("p (m k q) -> p m k q", m=2, k=KD)
        first_w = [rot[:, q, :, :].rearrange("p j c -> p (j c)").rearrange("p (k n) -> p k n", k=KD) for q in range(2)]
        gain_fin = rot[:, 0, 0:KD, :].rearrange("p j q -> p (j q)")
        yg5 = xn[:, :, :].rearrange("p t (k q) -> p (t k) q", q=T)
        bias_glu = ring_v[:, 3, :, :].rearrange("p k n -> p (k n)")


        x_in, gain_in, par_in = sem("x_in"), sem("gain_in"), sem("par_in")
        w_in = [sem(f"w_in{i}") for i in range(NW)]
        first_in = sem("first_in")
        v_in = [sem(f"v_in{i}") for i in range(NV)]
        consts = sem("consts")
        pool_ch, dve_ch, act_ch = sem("pool_chain"), sem("dve_chain"), sem("act_chain")
        ssq_ok, msq_ok, rstd_ok, xn_ok = sem("ssq_ok"), sem("msq_ok"), sem("rstd_ok"), sem("xn_ok")
        xT_ps, xT_act, xT_dve = sem("xT_ps"), sem("xT_act"), sem("xT_dve")
        res_ok = sem("res_ok")
        cw_ps, cw_ok = sem("cw_ps"), sem("cw_ok")
        proj_ps, proj_got = sem("proj_ps"), sem("proj_got")
        conv_ok, silu_ok, sq_ok = sem("conv_ok"), sem("silu_ok"), sem("sq_ok")
        ba_ps, ba_got = sem("ba_ps"), sem("ba_got")
        be_ok, ab_ok, sp_ok, g_ok = sem("be_ok"), sem("ab_ok"), sem("sp_ok"), sem("g_ok")
        rows_ps, dcol_ok, expd_ok, diff_ok, dm_ok = [sem(n) for n in ("rows_ps", "dcol_ok", "expd_ok", "diff_ok", "dm_ok")]
        ssum_ps, rs_ok, qn_ok, kn_ok, fac_ok, fac_exp = [sem(n) for n in ("ssum_ps", "rs_ok", "qn_ok", "kn_ok", "fac_ok", "fac_exp")]
        vt_ps, kt_ps, vt_ok, kt_ok = [sem(n) for n in ("vt_ps", "kt_ps", "vt_ok", "kt_ok")]
        kb_ok, gram_ps, gram_ok, bt_ok = [sem(n) for n in ("kb_ok", "gram_ps", "gram_ok", "bt_ok")]
        p1_ps, p1_ok, delta_ps, deltaT_ps, x_ok, xt_ok = [sem(n) for n in ("p1_ps", "p1_ok", "delta_ps", "deltaT_ps", "x_ok", "xt_ok")]
        wu_ps, wT_ok, u_ok = [sem(n) for n in ("wu_ps", "wT_ok", "u_ok")]
        vs_ps, vn_ok, o_ps, st_ps, st_ok, o_ok = [sem(n) for n in ("vs_ps", "vn_ok", "o_ps", "st_ps", "st_ok", "o_ok")]
        so_ok, ro_ok, yg_ok, yd_ps, yd_ok = [sem(n) for n in ("so_ok", "ro_ok", "yg_ok", "yd_ps", "yd_ok")]
        z_ps, e_ok, sp3_ok, spm_ok, rc_ps, lw_ok, w_ok, ys_ps, ys_ok = [
            sem(n) for n in ("z_ps", "e_ok", "sp3_ok", "spm_ok", "rc_ps", "lw_ok", "w_ok", "ys_ps", "ys_ok")]
        mix_ps, zm_ok, gate_ok = sem("mix_ps"), sem("zm_ok"), sem("gate_ok")
        osq_ok = sem("osq_ok")
        log_ps, glog_ok, gexp_ok, dv_ok, wexp_ok = [sem(n) for n in ("log_ps", "glog_ok", "gexp_ok", "dv_ok", "wexp_ok")]
        sel_ok, pos_ps, routed, perm_ok = [sem(n) for n in ("sel_ok", "pos_ps", "routed", "perm_ok")]
        xs_ps, xs_act, xs_dve = [sem(n) for n in ("xs_ps", "xs_act", "xs_dve")]
        xe_ok, h_ps, ha_ok, hg_ok, t_ps, gt_ok, y_ps, ya_ok = [
            sem(n) for n in ("xe_ok", "h_ps", "ha_ok", "hg_ok", "t_ps", "gt_ok", "y_ps", "ya_ok")]
        more_in, more_step = [[sem(f"more_{n}{l}") for l in range(2)] for n in ("in", "step")]
        STEPS = 14
        XE0, XE1, HID, SILU, GATED, TURNED, GT, PROD, ROW0, ROW1, PART0, PART1, PICK, COMB = range(1, STEPS + 1)
        MORE = (PASSES - 1) * NP
        s5_dt, s5_arg, s5_trig, s5_par, s5_tps, s5t_ok = [sem(n) for n in ("s5_dt", "s5_arg", "s5_trig", "s5_par", "s5_tps", "s5t_ok")]
        c2_re, b2_ok = sem("c2_re"), sem("b2_ok")
        c_in, c_used = sem("c_in"), sem("c_used")
        coarse_ok, rot_m, rot_ok, raw_in, bias_in = [sem(n) for n in ("coarse_ok", "rot_m", "rot_ok", "raw_in", "bias_in")]
        wz_ok, wb_ok, wc_ok, bt_ps, ct_ps, bT_ok, cT_ok = [sem(n) for n in ("wz_ok", "wb_ok", "wc_ok", "bt_ps", "ct_ps", "bT_ok", "cT_ok")]
        bu_ps, mc_ok, ms_ok, gin_ok, c2_ok, gst_ok, oc_ok, os_ok, yd5_ok, gelu_ok = [sem(n) for n in (
            "bu_ps", "mc_ok", "ms_ok", "gin_ok", "c2_ok", "gst_ok", "oc_ok", "os_ok", "yd5_ok", "gelu_ok")]
        glu_ps, gz_ok, gs_ok, fin_ok, out_done, fg_in = [sem(n) for n in ("glu_ps", "gz_ok", "gs_ok", "fin_ok", "out_done", "fg_in")]
        key_ps, key_ok, part_ok, pick_ok, comb_ps = [sem(n) for n in ("key_ps", "key_ok", "part_ok", "pick_ok", "comb_ps")]

        early = [("beta", 0), ("l2", 0), ("rows", 0), ("kb", 0)]
        pair_a = lambda n: 2 * (n % 2)
        plan = [("turn", 0), ("gram", 0)]
        chain = [("level", n) for n in range(6)] + [("wu", 0)] + [("chunk", n) for n in range(4)] + [("dn_out", 0)]
        for s, item in enumerate(chain):
            plan.append(item)
            if 0 <= s - 2 < SBH:
                plan.append(("mixv", s - 2))
            if 0 <= s - 1 < SBH:
                plan.append(("suffix", s - 1))
            if item[0] == "level" and item[1]:
                plan.append(("delta", item[1]))
            if s < SBH:
                plan.append(("score", s))
            if item[0] == "chunk" and item[1] >= 2:
                plan.append(("gate", item[1] - 2))
        z3 = [bank[4], bank[5]]
        GATE_PARTS = [(1, 2), (2, 2), (2, 2), (2, 3)]
        gate_bank = [bank[3], bank[4]]
        mix_bank = [bank[b] for b in (3, 5, 6, 7)]
        MIX_BEFORE = 10

        block = ctx.enter_context(nc.Block())

        def pairs(eng, step):
            for i in range(2):
                step(i, i, 0)
            with eng.Fori(0, NP // 2 - 1) as turn:
                for j in range(2):
                    step(turn * 2 + (2 + j), j, turn + 1)

        @block.sync
        def _(sp):
            for t in range(NT):
                sp.dma_start(res[:, t, :], x[0, t * P:(t + 1) * P, :]).then_inc(x_in, 16)

            sp.dma_start(gains[:, 0, :], mix_norm_even[0].rearrange("(p k) -> p k", k=KD)).then_inc(gain_in, 16)

            def load_w(i, src):
                sp.dma_start(ring_w[:, i % NW, :, :], src).then_inc(w_in[i % NW], 16)

            def load_parameters():
                small_loads = [
                    (gains[:, 1, :], ffn_norm[0].rearrange("(p k) -> p k", k=KD)),
                    (gains[:, 3, :], ffn_norm[1].rearrange("(p k) -> p k", k=KD)),
                    (convw_rows[:, :], dn_conv_w[0].rearrange("j (c p) -> (j c) p", p=P)),
                    (wba[:, :, :], w_in_even[0].rearrange("(p k) n -> p k n", k=KD)[:, :, 3072:3080]),
                    (dn_par[:, 0, :], dn_a_log.partition_broadcast(P)[:, 0, :]),
                    (dn_par[:, 1, :], dn_dt_bias.partition_broadcast(P)[:, 0, :]),
                    (out_gain[:, :], dn_out_norm[0].rearrange("(p o) -> p o", o=1)),
                    (s5w[0:KD, VEC, :], mix_norm_odd[0].rearrange("(k p) -> k p", p=P)),
                    (s5w[KD:2 * KD, VEC, :], s5_d[0].rearrange("(k p) -> k p", p=P)),
                    (s5w[:, LRE, :], s5_lambda_re[0].rearrange("(j h) q -> j (h q)", h=2)),
                    (s5w[:, LIM, :], s5_lambda_im[0].rearrange("(j h) q -> j (h q)", h=2)),
                    (s5dt, s5_log_step[0].rearrange("(j h) -> j h", h=2)),
                ] + [(wr[:, l, :, 0:NGRP], w_router_group[l].rearrange("(p k) n -> p k n", k=KD)) for l in range(2)] + [
                    (wr[:, l, :, NGRP:], w_router_expert[l].rearrange("(p k) n -> p k n", k=KD)) for l in range(2)]
                for dst, src in small_loads:
                    sp.dma_start(dst, src).then_inc(par_in, 16)
                assert len(small_loads) == N_PAR

            win = w_in_even[0].rearrange("(p k) n -> p k n", k=KD)
            for i, name in enumerate(PROJ_BLOCKS):
                if i == 2:
                    load_parameters()
                if i >= NW:
                    sp.wait_ge(proj_ps, 2 * (i - NW + 1))
                load_w(i, win[:, :, PROJ_COL[name]:PROJ_COL[name] + 512])
            wo = w_out_even[0].rearrange("(k p) n -> p k n", p=P)
            for h in range(2):
                i = W_OUT0 + h
                sp.wait_ge(proj_ps, 2 * (i - NW + 1))
                load_w(i, wo[:, :, h * 512:(h + 1) * 512])

            def load_expert_w(l, e, n=None):
                dst, done = (first_w[e], first_in) if n is None else (ring_w[:, n % NW, :, :], w_in[n % NW])
                sp.dma_start(dst, w_expert_in[l][e].rearrange("(p k) n -> p k n", k=KD)).then_inc(done, 16)

            def load_expert_v(l, e, slot):
                sp.dma_start(ring_v[:, slot, :, :], w_expert_out[l][e].rearrange("(k p) n -> p k n", k=2)).then_inc(v_in[slot], 16)

            def experts(l):
                w0, n0 = W_EXP[l], NP * l
                if l == 0:
                    for e in range(2, 4):
                        sp.wait_ge(proj_ps, 2 * (w0 + e - NW + 1))
                        load_expert_w(l, e, w0 + e)
                    sp.wait_ge(yd_ps, 1)
                    for e in range(2):
                        load_expert_v(l, e, e)
                    for e in range(4, 6):
                        sp.wait_ge(mix_ps, 2 * (e - 3))
                        load_expert_w(l, e, w0 + e)
                    for e in range(2):
                        load_expert_w(l, e)
                    for e in range(2, 4):
                        load_expert_v(l, e, e)
                else:
                    sp.wait_ge(c_used, NS5)
                    for e in range(2):
                        load_expert_w(l, e)
                        load_expert_v(l, e, e)
                    load_expert_v(l, 2, 2)
                    for e in range(2, 6):
                        sp.wait_ge(glu_ps, 2 * (e - 1))
                        load_expert_w(l, e, w0 + e)
                    sp.wait_ge(res_ok, 3 * NT)
                    load_expert_v(l, 3, 3)

                def next_pair(p, par):
                    sp.wait_ge(y_ps, p + (n0 - 1))
                    for q in range(2):
                        load_expert_v(l, p * 2 + q, 2 * par + q)
                    if isinstance(p, int) and p == NP - 1:
                        return
                    sp.wait_ge(h_ps, p + n0)
                    for q in range(2):
                        load_expert_w(l, p * 2 + (2 + q), w0 + 2 * par + 2 + q)

                with sp.Fori(0, NP // 2 - 2) as turn:
                    for j in range(2):
                        next_pair(turn * 2 + (2 + j), j)
                for p in range(NP - 2, NP):
                    next_pair(p, p % 2)
                sp.wait_ge(routed, l + 1)
                with sp.If(sp.value_load(most_i[0:1, 0:1], min_val=0, max_val=SLOTS) > CAP):
                    sp.wait_ge(h_ps, NP * (l + 1))
                    sp.wait_ge(y_ps, NP * (l + 1))
                    for r in range(PASSES - 1):
                        with sp.Fori(0, NP) as i:
                            sp.wait_ge(more_step[l], (i + r * NP) * STEPS)
                            for q in range(2):
                                e = i * 2 + q
                                sp.dma_start(ring_w[:, q, :, :], w_expert_in[l][e].rearrange("(p k) n -> p k n", k=KD)).then_inc(more_in[l], 16)
                                sp.dma_start(ring_v[:, q, :, :], w_expert_out[l][e].rearrange("(k p) n -> p k n", k=2)).then_inc(more_in[l], 16)
                    sp.wait_ge(more_step[l], MORE * STEPS)

            experts(0)
            sp.wait_ge(y_ps, NP)
            for m, src in enumerate((s5_c_re, s5_c_im)):
                sp.dma_start(s5c[:, m, :, :], src[0].rearrange("(k g) c q -> (g c) k q", k=KD)).then_inc(c_in, 16)
            for m, src in enumerate((s5_b_re, s5_b_im)):
                sp.dma_start(s5b[:, m, :, :], src[0].rearrange("(j h) q c -> (h q) j c", h=2)).then_inc(raw_in, 16)
            wg = w_glu[0].rearrange("(k p) n -> p k n", p=P)
            for b in range(4):
                h, kind = b // 2, b % 2
                load_w(W_GLU + b, wg[:, :, kind * D + h * 512:kind * D + (h + 1) * 512])
            sp.wait_ge(bt_ps, 4)
            sp.dma_start(bias_glu, b_glu.partition_broadcast(P)[:, 0, :]).then_inc(bias_in, 16)
            experts(1)
            sp.dma_start(gain_fin, final_norm.partition_broadcast(P)).then_inc(fg_in, 16)
            for t in range(NT):
                sp.wait_ge(fin_ok, t + 1)
                sp.dma_start(out[0, t * P:(t + 1) * P, :], xn[:, t, :]).then_inc(out_done, 16)
            sp.wait_ge(out_done, 16 * NT)

        @block.gpsimd
        def _(pool):
            c = Chain(pool, pool_ch)
            g = nc.gpsimd

            def norm(n):
                pool.wait_ge(msq_ok, n + 1)
                g.tensor_tensor(rstd[:, n, :], msq[:, n, :], neghalf[:, 0:NT], ALU.pow).then_inc(rstd_ok, 1)

            c.mark(g.memset(neghalf[:, :], -0.5))
            c.link(g.memset(ones[:, :], 1.0))
            g.affine_select(out=ident[:, :], in_=ones[:, :], pattern=[[-1, P]], compare_op=ALU.is_equal, fill=0.0,
                            base=0, channel_multiplier=1).then_inc(consts, 1)
            norm(0)
            c.mark(g.memset(neg_ones[:, :], -1.0))
            c.mark(g.memset(level[:, :, :], 0.0))
            c.mark(g.memset(one_col[:, :], 1.0))
            c.mark(g.memset(eps_col[:, :], EPS))
            c.link(g.memset(causal3[:, 1, :], 1.0))

            def where(dst, src, pattern, base, cm, op=ALU.is_ge, fill=0.0):
                return g.affine_select(out=dst, in_=src, pattern=pattern, compare_op=op, fill=fill,
                                       base=base, channel_multiplier=cm)

            c.mark(where(before[:, :], ones[:, :], [[1, P]], 0, -1, ALU.is_gt))
            c.mark(where(causal3[:, 0, :], ones[:, :], [[1, P]], 0, -1, ALU.is_gt))
            c.mark(where(causal3[:, 2, :], ones[:, :], [[1, P]], 0, -1, ALU.is_gt))
            c.mark(where(neg_upto[:, :], neg_ones[:, :], [[-1, P]], 0, 1))
            two = lambda ap: ap.rearrange("p (c i) -> p c i", i=CH)
            c.link(where(two(chunk_ones[:, :]), two(ones[:, :]), [[-CH, 2], [0, CH]], 0, 1))
            c.link(where(two(chunk_ones[:, :]), two(chunk_ones[:, :]), [[CH, 2], [0, CH]], CH - 1, -1))
            c.link(where(chunk_incl[:, :], chunk_ones[:, :], [[1, P]], 0, -1))
            c.mark(g.tensor_scalar(negchunk[:, :], chunk_incl[:, :], 1.0, BIG, ALU.subtract, ALU.mult))
            c.mark(g.tensor_scalar(negcausal3[:, :, :], causal3[:, :, :], 1.0, BIG, ALU.subtract, ALU.mult))
            for l in range(6):
                s = 2 ** l
                half = level[:, l, :].rearrange("p (c h i) -> p c h i", h=2, i=s)[:, :, 1, :]
                c.link(g.memset(half, 1.0))
                c.link(where(half, half, [[-2 * s, P // (2 * s)], [0, s]], 0, 1))
                c.link(where(half, half, [[2 * s, P // (2 * s)], [0, s]], s - 1, -1))
            c.wait()
            g.memset(raw[:, :, 0:TAPS - 1], 0.0).then_inc(consts, 1)
            g.memset(state[:, :, :], 0.0).then_inc(consts, 1)
            c.mark(g.iota(row_no[:, :], [[2 * CAP, PASSES * NP]], base=0, channel_multiplier=1, allow_small_or_imprecise_dtypes=True))
            g.iota(iota_e[:, :], [[1, NEXP]], base=0, channel_multiplier=0, allow_small_or_imprecise_dtypes=True).then_inc(consts, 1)

            for c_ in range(2):
                pool.wait_ge(silu_ok, c_ + 1)
                v = (qT, kT)[c_]
                g.tensor_tensor((sq_q, sq_k)[c_], v, v, ALU.mult).then_inc(sq_ok, 1)
            for kind, n in plan:
                for m in [0, 1] if (kind, n) == ("level", 0) else [n + 1] if kind == "level" and n < 5 else []:
                    pool.wait_ge(gram_ok, 2)
                    if m:
                        pool.wait_ge(p1_ps, m)
                    if m == 1:
                        pool.wait_ge(xt_ok, 1)
                    g.tensor_tensor(btl, mT, level[:, m:m + 1, :].to_broadcast((P, NU, P)), ALU.mult).then_inc(bt_ok, 1)
                if kind == "score":
                    pool.wait_ge(sp3_ok, n + 1)
                    g.tensor_tensor(sb_sp[:, n % 2, :], sb_sp[:, n % 2, :], causal3[:, :, :].rearrange("p a b -> p (a b)"),
                                    ALU.mult).then_inc(spm_ok, 1)
                if kind == "dn_out":
                    pool.wait_ge(so_ok, 1)
                    g.tensor_tensor(sml[:, RSO, :], sml[:, SSO, :], neghalf[:, :], ALU.pow).then_inc(ro_ok, 1)

            def slot_numbers(l):
                pool.wait_ge(res_ok, NT * (1 + 2 * l))
                g.iota(iota_slot[:, :], [[1, SLOTS]], base=0, channel_multiplier=0, allow_small_or_imprecise_dtypes=True).then_inc(consts, 1)

            def coarse_turns():
                def cmul(dst, x_, y_, n):
                    xr, xi = x_[0], x_[1]
                    yr, yi = [z if n == 1 else z.to_broadcast((P, NS5, n)) for z in y_]
                    t = [s5tmp[:, q, :, 0:n] for q in range(4)]
                    for q, (a_, b_) in enumerate(((xr, yr), (xi, yi), (xr, yi), (xi, yr))):
                        c.mark(g.tensor_tensor(t[q], a_, b_, ALU.mult))
                    c.wait()
                    c.mark(g.tensor_tensor(dst[0], t[0], t[1], ALU.subtract))
                    c.link(g.tensor_tensor(dst[1], t[2], t[3], ALU.add))

                def at(tab, lo, hi=None):
                    return [tab[:, m, :, lo:(hi or lo + 1)] for m in range(2)]

                pool.wait_ge(s5t_ok, 1)
                for tab in (rot_f, rot_c):
                    c.mark(g.memset(tab[:, 0, :, 0:1], 1.0))
                    c.mark(g.memset(tab[:, 1, :, 0:1], 0.0))
                c.mark(g.tensor_copy(rot_f[:, 0, :, 1], s5t[:, 1, :]))
                c.link(g.tensor_copy(rot_f[:, 1, :, 1], s5t[:, 2, :]))
                cmul(at(rot_f, 2), at(rot_f, 1), at(rot_f, 1), 1)
                cmul(at(rot_f, 3), at(rot_f, 2), at(rot_f, 1), 1)
                cmul(at(rot_f, 4), at(rot_f, 2), at(rot_f, 2), 1)
                cmul(at(rot_f, 5, 8), at(rot_f, 1, 4), at(rot_f, 4), 3)
                cmul(at(rot_c, 1), at(rot_f, 4), at(rot_f, 4), 1)
                cmul(at(rot_c, 2), at(rot_c, 1), at(rot_c, 1), 1)
                cmul(at(rot_c, 3), at(rot_c, 2), at(rot_c, 1), 1)
                cmul(at(rot_c, 4), at(rot_c, 2), at(rot_c, 2), 1)
                cmul(at(rot_c, 5, 8), at(rot_c, 1, 4), at(rot_c, 4), 3)
                cmul(at(rot_c, 8), at(rot_c, 4), at(rot_c, 4), 1)
                cmul(at(rot_c, 9, 16), at(rot_c, 1, 8), at(rot_c, 8), 7)
                cmul([turn128[:, m, :].unsqueeze(2) for m in range(2)], at(rot_c, 8), at(rot_c, 8), 1)
                f, late = [s5t[:, 3 + m, :].unsqueeze(2) for m in range(2)], [s5t[:, 5 + m, :].unsqueeze(2) for m in range(2)]
                t = [s5tmp[:, q, :, 0:1] for q in range(4)]
                for q, (a_, b_) in enumerate(((0, 0), (1, 1), (1, 0), (0, 1))):
                    c.mark(g.tensor_tensor(t[q], f[a_], turn128[:, b_, :].unsqueeze(2), ALU.mult))
                c.wait()
                c.mark(g.tensor_tensor(late[0], t[0], t[1], ALU.add))
                c.link(g.tensor_tensor(late[1], t[2], t[3], ALU.subtract))
                g.memset(s5tmp[:, 0, 0, 0:1], 0.0).then_inc(coarse_ok, 1)

            def zeros(w):
                g.memset(w[:, :, :, :], 0.0).then_inc(wz_ok, 1)

            def late_output_weights():
                t128 = [bc(turn128[:, m, :], (P, NS5, 32)) for m in range(2)]
                flat_c = lambda ap: ap.rearrange("p k (j c) -> p (k j) c", c=32)
                pool.wait_ge(cT_ok, 6)
                c.mark(g.tensor_tensor(c_tmp_g[0], flat_c(cT[:, 1, :, :]), t128[0], ALU.mult))
                c.link(g.tensor_tensor(c_tmp_g[1], flat_c(cT[:, 0, :, :]), t128[1], ALU.mult))
                g.tensor_tensor(flat_c(cT2[:, 1, :, :]), c_tmp_g[0], c_tmp_g[1], ALU.subtract).then_inc(c2_ok, 1)
                pool.wait_ge(c2_ok, 1)

            def s5_layer():
                late_output_weights()

                def turn_back(j, b):
                    pool.wait_ge(mc_ok, j + 1)
                    pool.wait_ge(ms_ok, j + 1)
                    g.tensor_tensor(gin[:, b, 0, :], m_in[:, b, 0, 0:T], m_in[:, b, 1, T:], ALU.add).then_inc(gin_ok, 1)
                    g.tensor_tensor(gin[:, b, 1, :], m_in[:, b, 0, T:], m_in[:, b, 1, 0:T], ALU.subtract).then_inc(gin_ok, 1)

                def by_sine(j, b):
                    pool.wait_ge(gst_ok, j * 2 + 2)
                    g.tensor_tensor(m_out[:, b, 1, :].rearrange("p (a t) -> p a t", t=S5C), gst[:, b, :, :].rearrange("p m (a t) -> p (m a) t", t=S5C),
                                    rot[:, 1, bass.ds(j, 1), :].to_broadcast((P, 4, S5C)), ALU.mult).then_inc(os_ok, 1)

                turn_back(0, 0)
                turn_back(1, 1)
                with pool.Fori(0, NS5 // 2 - 1) as turn:
                    for b in range(2):
                        by_sine(turn * 2 + b, b)
                        turn_back(turn * 2 + (b + 2), b)
                for b in range(2):
                    by_sine(NS5 - 2 + b, b)

            norm(1)
            slot_numbers(0)
            coarse_turns()
            pool.wait_ge(res_ok, 2 * NT)
            zeros(wide)
            norm(2)
            zeros(wide2)
            s5_layer()
            norm(3)
            slot_numbers(1)
            norm(4)

        @block.scalar
        def _(act):
            c = Chain(act, act_ch)
            a = nc.scalar

            def norm_a(n):
                if n == 0:
                    act.wait_ge(x_in, 16 * NT)
                for t in range(NT):
                    if n:
                        act.wait_ge(res_ok, NT * (n - 1) + t + 1)
                    a.activation(xn[:, t, :], res[:, t, :], ACT.Square, accum_out=ssq[:, n, t:t + 1]).then_inc(ssq_ok, 1)

            def norm_b(n):
                for b in range(2):
                    act.wait_ge(xT_ps, 4 * n + b + 1)
                    for k in (2 * b, 2 * b + 1):
                        a.activation(xT[:, k, :], bank[b][:, (k % 2) * T:(k % 2) * T + T], ACT.Copy,
                                     scale=gains[:, n, k:k + 1]).then_inc(xT_act, 1)

            norm_a(0)
            act.wait_ge(gain_in, 16)
            norm_b(0)
            act.wait_ge(par_in, 16 * N_PAR)
            a.activation(s5dt, s5dt, ACT.Exp).then_inc(s5_dt, 1)
            act.preload_act_table_set("silu_and_others")

            def mixer_step(kind, n):
                if kind == "beta":
                    act.wait_ge(ba_ps, 1)
                    a.activation(ba[:, :, :], bank[0][:, 0:16].rearrange("p (t n) -> p t n", t=NT), ACT.Copy).then_inc(ba_got, 1)
                    act.wait_ge(ba_got, 1)
                    c.link(a.activation(sml[:, E1, :].rearrange("p (h t) -> p t h", t=NT), ba[:, :, 0:4], ACT.Exp, scale=-1.0))
                    a.activation(neg_a[:, :], dn_par[:, 0, :], ACT.Exp).then_inc(be_ok, 1)
                    act.wait_ge(ab_ok, 1)
                    c.link(a.activation(sml[:, T1, :], sml[:, SP_, :], ACT.Abs))
                    c.link(a.activation(sml[:, T1, :], sml[:, T1, :], ACT.Exp, scale=-1.0))
                    a.activation(sml[:, T1, :], sml[:, T1, :], ACT.Ln, bias=one_col[:, :]).then_inc(sp_ok, 1)
                if kind == "rows":
                    act.wait_ge(rows_ps, 1)
                    for h in range(2):
                        a.activation(expd[:, 4 * h:4 * h + 4, :].rearrange("p u q -> p (u q)"), bank[h][:, :], ACT.Exp).then_inc(expd_ok, 1)
                if kind == "decays":
                    act.wait_ge(diff_ok, 1)
                    a.activation(dmT, dmT, ACT.Exp).then_inc(dm_ok, 1)
                    act.wait_ge(fac_ok, 1)
                    a.activation(sml[:, KF:KF + 2, :], sml[:, KF:KF + 2, :], ACT.Exp).then_inc(fac_exp, 1)
                if kind == "l2":
                    for m in range(2):
                        act.wait_ge(ssum_ps, m + 1)
                        for h in range(2):
                            c.mark(a.activation(rs[m][:, 4 * h:4 * h + 4, :].rearrange("p u q -> p (u q)"),
                                                bank[2 * m + h][:, :], ACT.Ln, bias=eps_col[:, :]))
                        c.wait()
                        a.activation(rs[m], rs[m], ACT.Exp, scale=-0.5).then_inc(rs_ok, 1)
                if kind == "level":
                    act.wait_ge(p1_ps, n + 1)
                    if n:
                        for h in range(2):
                            a.activation(P1[:, 4 * h:4 * h + 4, :].rearrange("p u q -> p (u q)"), bank[pair_a(n) + h][:, :], ACT.Copy).then_inc(p1_ok, 1)
                if kind == "wu":
                    act.wait_ge(wu_ps, 1)
                    for h in range(2):
                        a.activation(wT[:, 4 * h:4 * h + 4, :].rearrange("p u q -> p (u q)"), bank[h][:, :], ACT.Copy).then_inc(wT_ok, 1)
                if kind == "chunk":
                    lo = CH * (n % 2)
                    act.wait_ge(o_ps, n + 1)
                    a.activation(oo[lo:lo + CH, 4 * (n // 2):4 * (n // 2) + 4, :].rearrange("p u q -> p (u q)"),
                                 bank[1][lo:lo + CH, :], ACT.Copy).then_inc(o_ok, 1)
                if kind == "gate":
                    if n == 0:
                        act.preload_act_table_set("silu_and_others")
                    act.wait_ge(proj_ps, 12 + n + 1)
                    a.activation(gate[:, n, :], gate_bank[n][:, :], ACT.Silu).then_inc(gate_ok, 1)
                if kind == "dn_out":
                    act.wait_ge(o_ok, 4)
                    for u in range(NU):
                        a.activation(yg[:, u, :], oo[:, u, :], ACT.Square, accum_out=sml[:, E1, u:u + 1]).then_inc(osq_ok, 1)
                    act.wait_ge(yd_ps, 1)
                    for h in range(2):
                        a.activation(yT[:, 4 + 2 * h:6 + 2 * h, :], bank[h][:, :].rearrange("p (c t) -> p c t", t=T), ACT.Copy,
                                     scale=out_gain[:, :]).then_inc(yd_ok, 1)
                if kind == "score":
                    act.wait_ge(z_ps, n + 1)
                    if n >= 2:
                        act.wait_ge(sp3_ok, n - 1)
                    c.link(a.activation(sb_e[:, n % 2, :], z3[n % 2][:, 0:3 * P], ACT.Abs))
                    c.link(a.activation(sb_e[:, n % 2, :], sb_e[:, n % 2, :], ACT.Exp, scale=-1.0))
                    a.activation(sb_e[:, n % 2, :], sb_e[:, n % 2, :], ACT.Ln, bias=one_col[:, :]).then_inc(e_ok, 1)
                if kind == "suffix":
                    act.wait_ge(lw_ok, n + 1)
                    a.activation(sb_w[:, n % 2, :], sb_w[:, n % 2, :], ACT.Exp).then_inc(w_ok, 1)
                if kind == "mixv" and n % 2:
                    act.wait_ge(ys_ps, n + 1)
                    a.activation(yT[:, n // 2, :], bank[7][:, 0:T], ACT.Copy).then_inc(ys_ok, 1)

            act.wait_ge(consts, 3)
            for i, name in enumerate(PROJ_BLOCKS[:-1]):
                for h in range(2):
                    act.wait_ge(proj_ps, 2 * i + h + 1)
                    src = bank[4 + 2 * (i % 2) + h]
                    two = src[:, :].rearrange("p (c t) -> p c t", t=T)
                    if name in ("dn_q", "dn_k", "dn_v"):
                        ins = a.activation(raw[:, 4 * i + 2 * h:4 * i + 2 * h + 2, TAPS - 1:], two, ACT.Copy)
                    elif name == "sb_q":
                        ins = a.activation(sbqT[:, 2 * h:2 * h + 2, :], two, ACT.Copy, scale=SBD ** -0.5)
                    elif name == "sb_k":
                        ins = a.activation(sbkT[:, 2 * h:2 * h + 2, :], two, ACT.Copy)
                    else:
                        ins = a.activation(sbv[:, h, :], src[:, :], ACT.Copy)
                    ins.then_inc(proj_got, 1)
                    if (name, h) == ("sb_v", 0):
                        mixer_step("rows", 0)
                if 1 <= i <= 3:
                    act.wait_ge(conv_ok, i)
                    a.activation(qkvT[:, 4 * i - 4:4 * i, :], qkvT[:, 4 * i - 4:4 * i, :], ACT.Silu).then_inc(silu_ok, 1)
                if i == 3:
                    act.wait_ge(s5_arg, 1)
                    a.activation(s5w[:, SIN, :], s5w[:, TR, :], ACT.Sin).then_inc(s5_trig, 1)
                    a.activation(s5w[:, TH, :], s5w[:, TR, :], ACT.Sin, scale=0.5).then_inc(s5_trig, 1)
                    act.preload_act_table_set(EXP_LN)
                    a.activation(s5w[:, MAG, :], s5w[:, MAG, :], ACT.Exp).then_inc(s5_trig, 1)
                    mixer_step("beta", 0)
                if i == 4:
                    mixer_step("l2", 0)
            mixer_step("decays", 0)
            for item in plan:
                mixer_step(*item)
            act.preload_act_table_set(EXP_LN)

            def experts(l):
                n0 = NP * l
                act.wait_ge(glog_ok, l + 1)
                for t in range(NT):
                    a.activation(gexp[:, t, :], gpad[:, t, 0:NGRP], ACT.Exp, bias=rv[:, 0, t, 0:1],
                                 accum_out=rv[:, 1, t, 0:1]).then_inc(gexp_ok, 1)
                act.wait_ge(dv_ok, l + 1)
                a.activation(rv[:, 3, :, 0], rv[:, 2, :, 0], ACT.Exp).then_inc(wexp_ok, 1)
                act.preload_act_table_set("silu_and_others")
                for k in range(0, KD, 2):
                    act.wait_ge(xs_ps, KD * l + k + 1)
                    a.activation(xs[:, k, 0:SLOTS], bank[k % 4][:, :], ACT.Copy, scale=gains[:, 1 + 2 * l, k:k + 1]).then_inc(xs_act, 1)

                def step(i, par, lap):
                    act.wait_ge(h_ps, i + (n0 + 1))
                    a.activation(act_a[:, :], bank[0][:, 0:FF], ACT.Silu).then_inc(ha_ok, 1)
                    act.wait_ge(t_ps, i + (n0 + 1))
                    a.activation(act_gT[:, :, :].rearrange("p k c -> p (k c)"), bank[1][:, 0:FF], ACT.Copy).then_inc(gt_ok, 1)
                    act.wait_ge(y_ps, i + (n0 + 1))
                    for h in range(2):
                        a.activation(yrow[:, h * 512:(h + 1) * 512], bank[2 + h][:, :], ACT.Copy).then_inc(ya_ok, 1)

                pairs(act, step)
                act.wait_ge(routed, l + 1)
                with act.If(act.value_load(most_i[0:1, 0:1], min_val=0, max_val=SLOTS) > CAP):
                    act.wait_ge(comb_ps, NT * NP * (l + 1))
                    for r in range(PASSES - 1):
                        with act.Fori(0, NP) as i:
                            n = i + r * NP
                            act.wait_ge(more_step[l], n * STEPS + HID)
                            a.activation(act_a[:, :], bank[0][:, 0:FF], ACT.Silu).then_inc(more_step[l], 1)
                            act.wait_ge(more_step[l], n * STEPS + TURNED)
                            a.activation(act_gT[:, :, :].rearrange("p k c -> p (k c)"), bank[1][:, 0:FF], ACT.Copy).then_inc(more_step[l], 1)
                            act.wait_ge(more_step[l], n * STEPS + PROD)
                            for h in range(2):
                                a.activation(yrow[:, h * 512:(h + 1) * 512], bank[2 + h][:, :], ACT.Copy).then_inc(more_step[l], 1)

            def s5_output_weights():
                for m in range(2):
                    act.wait_ge(ct_ps, m + 1)
                    for h in range(2):
                        ps = bank[4 + 2 * m + h][:, :]
                        a.activation(cT[:, m, 4 * h:4 * h + 4, :].rearrange("p k q -> p (k q)"), ps, ACT.Copy,
                                     scale=(1.0, -1.0)[m]).then_inc(cT_ok, 1)
                        if m == 0:
                            a.activation(cTn[:, 4 * h:4 * h + 4, :].rearrange("p k q -> p (k q)"), ps, ACT.Copy, scale=-1.0).then_inc(cT_ok, 1)

            def s5_layer():
                for n, dst in enumerate((bT, bT2)):
                    for m in range(2):
                        act.wait_ge(bt_ps, 2 * n + m + 1)
                        if n:
                            act.wait_ge(b2_ok, 1)
                        for h in range(2):
                            a.activation(dst[:, m, 4 * h:4 * h + 4, :].rearrange("p k q -> p (k q)"), bank[2 * m + h][:, :], ACT.Copy).then_inc(bT_ok, 1)
                act.wait_ge(c2_re, 1)
                act.wait_ge(c2_ok, 1)
                a.activation(cTn2, cT2[:, 0, :, :], ACT.Copy, scale=-1.0).then_inc(cT_ok, 1)
                act.preload_act_table_set("gelu_apprx_tanh_and_others")
                with act.Fori(0, KD) as k:
                    act.wait_ge(yd5_ok, k + 1)
                    a.activation(yg5[:, bass.ds(k, 1), :], yg5[:, bass.ds(k, 1), :], ACT.Gelu_apprx_tanh).then_inc(gelu_ok, 1)
                act.preload_act_table_set("sigmoid_and_others")
                for i in range(4):
                    act.wait_ge(gz_ok, i + 1)
                    a.activation(m_in_f[:, i * 512:(i + 1) * 512], m_in_f[:, i * 512:(i + 1) * 512], ACT.Sigmoid).then_inc(gs_ok, 1)

            norm_a(1)
            norm_b(1)
            experts(0)
            norm_a(2)
            s5_output_weights()
            norm_b(2)
            s5_layer()
            act.preload_act_table_set(EXP_LN)
            norm_a(3)
            norm_b(3)
            experts(1)
            norm_a(4)

        @block.vector
        def _(dve):
            c = Chain(dve, dve_ch)
            v = nc.vector

            def mean_square(n):
                dve.wait_ge(ssq_ok, 2 * n + 2)
                v.tensor_scalar(msq[:, n, :], ssq[:, n, :], 1.0 / D, EPS, ALU.mult, ALU.add).then_inc(msq_ok, 1)

            def norm_a(n):
                mean_square(n)
                dve.wait_ge(rstd_ok, n + 1)
                for t in range(NT):
                    v.tensor_scalar(xn[:, t, :], res[:, t, :], rstd[:, n, t:t + 1], None, ALU.mult).then_inc(xn_ok, 1)

            def norm_b(n):
                for b in range(2, 4):
                    dve.wait_ge(xT_ps, 4 * n + b + 1)
                    for k in (2 * b, 2 * b + 1):
                        v.tensor_scalar(xT[:, k, :], bank[b][:, (k % 2) * T:(k % 2) * T + T], gains[:, n, k:k + 1], None,
                                        ALU.mult).then_inc(xT_dve, 1)

            norm_a(0)
            dve.wait_ge(gain_in, 16)
            norm_b(0)
            dve.wait_ge(par_in, 16 * N_PAR)
            dve.wait_ge(cw_ps, 1)
            v.tensor_copy(convw[:, :], bank[7][:, 0:TAPS * 12]).then_inc(cw_ok, 1)
            dve.wait_ge(cw_ok, 1)
            for i in range(3):
                dve.wait_ge(proj_got, 2 * i + 2)
                for j in range(TAPS):
                    for ch in range(4 * i, 4 * i + 4):
                        w = convw[:, 12 * j + ch:12 * j + ch + 1]
                        if j == 0:
                            ins = v.tensor_scalar(qkvT[:, ch, :], raw[:, ch, 0:T], w, None, ALU.mult)
                        else:
                            ins = v.scalar_tensor_tensor(out=qkvT[:, ch, :], in0=raw[:, ch, j:j + T], scalar=w,
                                                         in1=qkvT[:, ch, :], op0=ALU.mult, op1=ALU.add)
                        if j < TAPS - 1:
                            c.mark(ins)
                    if j < TAPS - 1:
                        c.wait()
                ins.then_inc(conv_ok, 1)
            def s5_parameters():
                w = lambda n: s5w[:, n, :]
                tt, ts, stt = v.tensor_tensor, v.tensor_scalar, v.scalar_tensor_tensor
                dt = bc(s5dt, (NS5, 2, 64))
                two = lambda ap: ap.rearrange("j (h q) -> j h q", h=2)
                c.mark(ts(w(LRE), w(LRE), -1e-4, None, ALU.min))
                dve.wait_ge(s5_dt, 1)
                c.link(tt(two(w(THE)), two(w(LIM)), dt, ALU.mult))
                c.link(tt(two(w(MAG)), two(w(LRE)), dt, ALU.mult))
                c.link(ts(w(TK), w(THE), 1.0 / (TWO_PI[0] + TWO_PI[1] + TWO_PI[2]), ROUND, ALU.mult, ALU.add))
                c.link(ts(w(TK), w(TK), ROUND, None, ALU.subtract))
                c.link(stt(out=w(TR), in0=w(TK), scalar=-TWO_PI[0], in1=w(THE), op0=ALU.mult, op1=ALU.add))
                for part in TWO_PI[1:]:
                    c.link(stt(out=w(TR), in0=w(TK), scalar=-part, in1=w(TR), op0=ALU.mult, op1=ALU.add))
                ts(w(TR), w(TR), PI, -PI, ALU.min, ALU.max).then_inc(s5_arg, 1)
                c.mark(tt(w(DEN), w(LRE), w(LRE), ALU.mult))
                c.link(tt(w(TMP), w(LIM), w(LIM), ALU.mult))
                c.link(tt(w(DEN), w(DEN), w(TMP), ALU.add))
                c.link(v.reciprocal(w(DEN), w(DEN)))
                dve.wait_ge(s5_trig, 3)
                c.link(tt(w(COS), w(TH), w(TH), ALU.mult))
                c.link(ts(w(COS), w(COS), -2.0, 1.0, ALU.mult, ALU.add))
                c.mark(tt(w(NRE), w(MAG), w(COS), ALU.mult))
                c.link(tt(w(THE), w(MAG), w(SIN), ALU.mult))
                c.link(ts(w(NRE), w(NRE), -1.0, None, ALU.add))
                c.mark(tt(w(CRE), w(NRE), w(LRE), ALU.mult))
                c.mark(tt(w(TMP), w(THE), w(LIM), ALU.mult))
                c.mark(tt(w(CIM), w(THE), w(LRE), ALU.mult))
                c.link(tt(w(TK), w(NRE), w(LIM), ALU.mult))
                c.mark(tt(w(CRE), w(CRE), w(TMP), ALU.add))
                c.link(tt(w(CIM), w(CIM), w(TK), ALU.subtract))
                c.mark(tt(w(CRE), w(CRE), w(DEN), ALU.mult))
                tt(w(CIM), w(CIM), w(DEN), ALU.mult).then_inc(s5_par, 1)
                dve.wait_ge(consts, 3)
                c.link(v.tensor_reduce(cmask[:, 0:1], level[:, 4, :], AX.X, ALU.add))
                c.link(ts(cmask[:, 0:1], cmask[:, 0:1], 1.0 / 16, None, ALU.mult))
                c.mark(ts(cmask[:, 1:2], cmask[:, 0:1], -1.0, 1.0, ALU.mult, ALU.add))

            def s5_take():
                dve.wait_ge(s5_tps, 1)
                c.mark(v.tensor_copy(gains[:, 2, :], bank[7][:, 5 * NS5:5 * NS5 + KD]))
                c.link(v.tensor_copy(s5d[:, :], bank[7][:, 5 * NS5 + KD:5 * NS5 + 2 * KD]))
                v.tensor_copy(s5t[:, 0:5, :], bank[7][:, 0:5 * NS5].rearrange("p (n j) -> p n j", n=5)).then_inc(s5t_ok, 1)

            s5_parameters()
            for kind, n in early + plan:
                if kind == "beta":
                    y = sml[:, SP_, :].rearrange("p (h t) -> p t h", t=NT)
                    dve.wait_ge(ba_got, 1)
                    v.tensor_tensor(y, ba[:, :, 4:8], dn_par[:, 1:2, :].to_broadcast((P, NT, DNH)), ALU.add).then_inc(ab_ok, 1)
                    dve.wait_ge(be_ok, 1)
                    c.link(v.tensor_scalar(sml[:, E1, :], sml[:, E1, :], 1.0, None, ALU.add))
                    c.link(v.reciprocal(sml[:, BETA, :], sml[:, E1, :]))
                    dve.wait_ge(sp_ok, 1)
                    c.link(v.scalar_tensor_tensor(out=sml[:, SP_, :], in0=sml[:, SP_, :], scalar=0.0, in1=sml[:, T1, :],
                                                  op0=ALU.max, op1=ALU.add))
                    v.scalar_tensor_tensor(out=sml[:, G, :].rearrange("p (h t) -> p h t", t=NT),
                                           in0=sml[:, SP_, :].rearrange("p (h t) -> p h t", t=NT), scalar=-1.0,
                                           in1=bc(neg_a[:, :], (P, DNH, NT)), op0=ALU.mult, op1=ALU.mult).then_inc(g_ok, 1)
                if kind == "rows":
                    dve.wait_ge(rows_ps, 1)
                    v.tensor_copy(sml[:, DCOL:DCOL + 2, :], bank[4][:, 0:16].rearrange("p (a u) -> p a u", a=2)).then_inc(dcol_ok, 1)
                    dve.wait_ge(dcol_ok, 1)
                    dve.wait_ge(expd_ok, 2)
                    ps = halves(0)
                    for u in range(NU):
                        ins = v.scalar_tensor_tensor(out=dmT[:, u, :], in0=ps[u], scalar=sml[:, DCOL, u:u + 1],
                                                     in1=negchunk[:, :], op0=ALU.subtract, op1=ALU.add)
                        if u < NU - 1:
                            c.mark(ins)
                    ins.then_inc(diff_ok, 1)
                    c.mark(v.tensor_copy(sml[:, KF, :], sml[:, DCOL, :]))
                    v.tensor_tensor(sml[:, TF, :], sml[:, DTOT, :], sml[:, DCOL, :], ALU.subtract).then_inc(fac_ok, 1)
                if kind == "l2":
                    dve.wait_ge(rs_ok, 1)
                    v.scalar_tensor_tensor(out=qT, in0=qT, scalar=DND ** -0.5, in1=rs[0], op0=ALU.mult, op1=ALU.mult).then_inc(qn_ok, 1)
                    dve.wait_ge(rs_ok, 2)
                    v.tensor_tensor(kT, kT, rs[1], ALU.mult).then_inc(kn_ok, 1)
                    dve.wait_ge(kn_ok, 1)
                if kind == "kb":
                    for h in range(2):
                        v.tensor_tensor(kbT[:, 4 * h:4 * h + 4, :].rearrange("p u q -> p (u q)"),
                                        kT[:, 4 * h:4 * h + 4, :].rearrange("p u q -> p (u q)"), bank[2 + h][:, :],
                                        ALU.mult).then_inc(kb_ok, 1)
                    s5_take()
                if kind == "turn":
                    dve.wait_ge(vt_ps, 1)
                    for h in range(2):
                        s = slice(4 * h, 4 * h + 4)
                        v.tensor_tensor(vbeta[:, s, :], bank[h][:, :].rearrange("p (u q) -> p u q", q=P),
                                        bc(sml[:, BETA, s], (P, 4, P)), ALU.mult).then_inc(vt_ok, 1)
                    dve.wait_ge(fac_exp, 1)
                    c.link(v.tensor_tensor(sml[:, KF, :], sml[:, KF, :], sml[:, BETA, :], ALU.mult))
                    dve.wait_ge(kt_ps, 1)
                    for h in range(2):
                        s = slice(4 * h, 4 * h + 4)
                        ps = bank[2 + h][:, :].rearrange("p (u q) -> p u q", q=P)
                        c.mark(v.tensor_tensor(kbe[:, s, :], ps, bc(sml[:, KF, s], (P, 4, P)), ALU.mult))
                        v.tensor_tensor(ktail[:, s, :], ps, bc(sml[:, TF, s], (P, 4, P)), ALU.mult).then_inc(kt_ok, 1)
                if kind == "gram":
                    dve.wait_ge(dm_ok, 1)
                    for m, dst in enumerate((mT, attnT)):
                        dve.wait_ge(gram_ps, m + 1)
                        for h in range(2):
                            v.tensor_tensor(dst[:, 4 * h:4 * h + 4, :].rearrange("p u q -> p (u q)"), bank[4 + 2 * m + h][:, :],
                                            dmT[:, 4 * h:4 * h + 4, :].rearrange("p u q -> p (u q)"), ALU.mult).then_inc(gram_ok, 1)
                    dve.wait_ge(expd_ok, 2)
                    dve.wait_ge(gram_ps, 2)
                    c.link(v.tensor_tensor(qT, qT, expd, ALU.mult))
                if kind == "level":
                    if n == 0:
                        dve.wait_ge(bt_ok, 1)
                        v.scalar_tensor_tensor(out=XT, in0=btl, scalar=-1.0,
                                               in1=ident[:, :].unsqueeze(1).to_broadcast((P, NU, P)),
                                               op0=ALU.mult, op1=ALU.add).then_inc(xt_ok, 1)
                        dve.wait_ge(p1_ps, 1)
                        for h in range(2):
                            ins = v.scalar_tensor_tensor(
                                out=X[:, 4 * h:4 * h + 4, :], in0=bank[h][:, :].rearrange("p (u q) -> p u q", q=P), scalar=-1.0,
                                in1=ident[:, :].unsqueeze(1).to_broadcast((P, 4, P)),
                                op0=ALU.mult, op1=ALU.add)
                            if h == 0:
                                c.mark(ins)
                        ins.then_inc(x_ok, 1)
                if kind == "delta":
                    for m, dst in enumerate((X, XT)):
                        if m == 0 and n == 5:
                            continue
                        dve.wait_ge((delta_ps, deltaT_ps)[m], n)
                        dve.wait_ge((x_ok, xt_ok)[m], n)
                        for h in range(2):
                            d = dst[:, 4 * h:4 * h + 4, :].rearrange("p u q -> p (u q)")
                            ins = v.tensor_tensor(d, d, bank[(2 - pair_a(n), pair_a(n))[m] + h][:, :], ALU.subtract)
                            if h == 0:
                                c.mark(ins)
                        ins.then_inc((x_ok, xt_ok)[m], 1)
                if kind == "wu":
                    dve.wait_ge(wu_ps, 2)
                    for h in range(2):
                        v.tensor_copy(uu[:, 4 * h:4 * h + 4, :].rearrange("p u q -> p (u q)"), bank[2 + h][:, :]).then_inc(u_ok, 1)
                    dve.wait_ge(u_ok, 2)
                if kind == "chunk":
                    t, lo = n // 2, CH * (n % 2)
                    uh = uu[lo:lo + CH, :, :].rearrange("p (h t) q -> p t h q", t=NT)[:, t, :, :]
                    dve.wait_ge(vs_ps, n + 1)
                    v.tensor_tensor(vnew[lo:lo + CH, 4 * t:4 * t + 4, :], uh,
                                    bank[0][lo:lo + CH, :].rearrange("p (h q) -> p h q", q=P), ALU.subtract).then_inc(vn_ok, 1)
                    dve.wait_ge(st_ps, n + 1)
                    for h in range(DNH):
                        u = 2 * h + t
                        ins = v.scalar_tensor_tensor(out=state[:, h, :], in0=state[:, h, :],
                                                     scalar=expd[:, u, lo + CH - 1:lo + CH], in1=bank[2][:, h * P:(h + 1) * P],
                                                     op0=ALU.mult, op1=ALU.add)
                        if h < DNH - 1:
                            c.mark(ins)
                    ins.then_inc(st_ok, 1)
                    dve.wait_ge(st_ok, n + 1)
                if kind == "dn_out":
                    dve.wait_ge(osq_ok, NU)
                    v.tensor_scalar(sml[:, SSO, :], sml[:, E1, :], 1.0 / DND, EPS, ALU.mult, ALU.add).then_inc(so_ok, 1)
                    dve.wait_ge(ro_ok, 1)
                    dve.wait_ge(gate_ok, 2)
                    c.link(v.tensor_tensor(yg, oo, gate[:, :, :].rearrange("p t (h q) -> p (t h) q", q=P), ALU.mult))
                    v.tensor_tensor(yg, yg, bc(sml[:, RSO, :], (P, NU, P)), ALU.mult).then_inc(yg_ok, 1)
                if kind == "score":
                    dve.wait_ge(e_ok, n + 1)
                    if n >= 2:
                        dve.wait_ge(rc_ps, n - 1)
                    v.scalar_tensor_tensor(out=sb_sp[:, n % 2, :], in0=z3[n % 2][:, 0:3 * P], scalar=0.0, in1=sb_e[:, n % 2, :],
                                           op0=ALU.max, op1=ALU.add).then_inc(sp3_ok, 1)
                    if n >= 2:
                        dve.wait_ge(ys_ps, n - 1)
                    v.tensor_tensor(sb_w[:, n % 2, :], z3[n % 2][:, 0:3 * P], negcausal3[:, :, :].rearrange("p a b -> p (a b)"),
                                    ALU.add).then_inc(zm_ok, 1)
                if kind == "suffix":
                    dve.wait_ge(rc_ps, n + 1)
                    dve.wait_ge(zm_ok, n + 1)
                    v.tensor_tensor(sb_w[:, n % 2, :], sb_w[:, n % 2, :], bank[6][:, 0:3 * P], ALU.add).then_inc(lw_ok, 1)
            for i in range(4):
                h, t = i // 2, i % 2
                dve.wait_ge(mix_ps, i + 1)
                ins = v.tensor_tensor(res[:, t, h * 512:(h + 1) * 512], res[:, t, h * 512:(h + 1) * 512], mix_bank[i][:, :], ALU.add)
                if h == 0:
                    c.mark(ins)
                else:
                    ins.then_inc(res_ok, 1)

            def route(l):
                tt, ts, stt, red = v.tensor_tensor, v.tensor_scalar, v.scalar_tensor_tensor, v.tensor_reduce
                c.mark(v.memset(gpad[:, :, NGRP:], -BIG))
                c.mark(v.memset(base_i[:, :, :], 0))
                dve.wait_ge(log_ps, l + 1)
                logits = bank[4][:, 0:128].rearrange("p (t n) -> p t n", t=NT)
                c.mark(v.tensor_copy(gpad[:, :, 0:NGRP], logits[:, :, 0:NGRP]))
                c.link(v.tensor_copy(elog[:, :, :], logits[:, :, NGRP:NGRP + NEXP]))
                for t in range(NT):
                    c.mark(v.max(top8[:, t, 0, :], gpad[:, t, :]))
                c.wait()
                for t in range(NT):
                    c.mark(v.max_index(idx8[:, t, 0, :], top8[:, t, 0, :], gpad[:, t, :]))
                ts(rv[:, 0, :, 0], top8[:, :, 0, 0], -1.0, None, ALU.mult).then_inc(glog_ok, 1)
                c.wait()
                c.link(v.tensor_copy(idxf[:, :, 0, :], idx8[:, :, 0, :]))
                c.link(tt(goh[:, :, :], iota_e[:, 0:NGRP].unsqueeze(1).to_broadcast((P, NT, NGRP)),
                          idxf[:, :, 0, 0:1].to_broadcast((P, NT, NGRP)), ALU.is_equal))
                for t in range(NT):
                    c.mark(tt(prod[:, t, :].rearrange("p (g e) -> p g e", g=NGRP), elog[:, t, :].rearrange("p (g e) -> p g e", g=NGRP),
                              bc(goh[:, t, :], (P, NGRP, PERG)), ALU.mult))
                c.wait()
                for t in range(NT):
                    c.mark(red(ingrp[:, t, :], prod[:, t, :].rearrange("p (g e) -> p e g", g=NGRP), AX.X, ALU.add))
                c.wait()
                for t in range(NT):
                    c.mark(v.max(top8[:, t, 1, :], ingrp[:, t, :]))
                c.wait()
                for t in range(NT):
                    c.mark(v.max_index(idx8[:, t, 1, :], top8[:, t, 1, :], ingrp[:, t, :]))
                tt(rv[:, 2, :, 0], top8[:, :, 1, 1], top8[:, :, 1, 0], ALU.subtract).then_inc(dv_ok, 1)
                c.wait()
                c.link(v.tensor_copy(idxf[:, :, 1, :], idx8[:, :, 1, :]))
                c.link(stt(out=rv[:, 4, :, :], in0=idxf[:, :, 0, 0:1].to_broadcast((P, NT, 2)), scalar=float(PERG),
                           in1=idxf[:, :, 1, 0:2], op0=ALU.mult, op1=ALU.add))
                c.link(tt(onehot[:, :, :, :].rearrange("p t r e -> p (t r) e"), iota_e[:, :].unsqueeze(1).to_broadcast((P, 4, NEXP)),
                          bc(rv[:, 4, :, :].rearrange("p t r -> p (t r)"), (P, 4, NEXP)), ALU.is_equal))
                tt(sel[:, :, :], onehot[:, :, 0, :], onehot[:, :, 1, :], ALU.add).then_inc(sel_ok, 1)
                dve.wait_ge(gexp_ok, 2 * l + 2)
                dve.wait_ge(wexp_ok, l + 1)
                c.mark(v.reciprocal(rv[:, 5, :, 0], rv[:, 1, :, 0]))
                c.link(ts(rv[:, 6, :, 0], rv[:, 3, :, 0], 1.0, None, ALU.add))
                c.link(v.reciprocal(rv[:, 6, :, 0], rv[:, 6, :, 0]))
                c.link(tt(rv[:, 7, :, 0], rv[:, 5, :, 0], rv[:, 6, :, 0], ALU.mult))
                c.link(tt(rv[:, 7, :, 1], rv[:, 7, :, 0], rv[:, 3, :, 0], ALU.mult))
                dve.wait_ge(pos_ps, l + 1)
                c.mark(v.tensor_copy(pos[:, :, :], bank[5][:, 0:2 * NEXP].rearrange("p (t e) -> p t e", t=NT)))
                c.link(v.tensor_copy(cnt[:, :], bank[5][:, 2 * NEXP:3 * NEXP]))
                c.link(v.tensor_tensor_scan(cum, ones[:, 0:NEXP], cnt[:, :], 0.0, ALU.mult, ALU.add))
                c.link(tt(base[:, :], cum, cnt[:, :], ALU.subtract))
                c.link(tt(slot_all[:, :, :], pos[:, :, :], base[:, :].unsqueeze(1).to_broadcast((P, NT, NEXP)), ALU.add))
                def chosen(src, row):
                    for t in range(NT):
                        c.mark(tt(prod2[:, t, :, :], onehot[:, t, :, :], src[:, t:t + 1, :].to_broadcast((P, 2, NEXP)), ALU.mult))
                    c.wait()
                    c.link(red(rv[:, row, :, :].rearrange("p t r -> p (t r)"), prod2[:, :, :, :].rearrange("p t r e -> p (t r) e"), AX.X, ALU.add))

                chosen(slot_all, 8)
                dve.wait_ge(consts, 5 + l)
                for t in range(NT):
                    c.mark(ts(perm[:, t, :], iota_slot[:, :], rv[:, 8, t, 0:1], None, ALU.is_equal))
                c.wait()
                for t in range(NT):
                    stt(out=perm[:, t, :], in0=iota_slot[:, :], scalar=rv[:, 8, t, 1:2], in1=perm[:, t, :],
                        op0=ALU.is_equal, op1=ALU.add).then_inc(perm_ok, 1)
                c.mark(v.tensor_copy(base_i[0:1, 0, 0:NEXP], base[0:1, :]))
                for n in range(1, PASSES):
                    c.mark(ts(base_i[0:1, n, 0:NEXP], base[0:1, :], float(n * CAP), float(SLOTS), ALU.add, ALU.min))
                c.link(red(most[:, :], cnt[:, :], AX.X, ALU.max))
                c.mark(v.tensor_copy(most_i[:, :], most[0:1, :]))
                chosen(pos, 9)
                pas = rv[:, 10, :, :]
                c.link(ts(pas, rv[:, 9, :, :], float(CAP), None, ALU.is_ge))
                for n in range(2, T // CAP):
                    c.link(stt(out=pas, in0=rv[:, 9, :, :], scalar=float(n * CAP), in1=pas, op0=ALU.is_ge, op1=ALU.add))
                c.link(stt(out=pas, in0=pas, scalar=float((NEXP - 1) * CAP), in1=rv[:, 9, :, :], op0=ALU.mult, op1=ALU.add))
                ins = stt(out=pas, in0=rv[:, 4, :, :], scalar=float(CAP), in1=pas, op0=ALU.mult, op1=ALU.add)
                ins.then_inc(routed, 1)

            def input_factor(f0, done=None):
                for q, (m, f) in enumerate(((0, 0), (1, 1), (1, 0), (0, 1))):
                    ins = v.tensor_tensor(b_prod[:, q, :, :], s5b[:, m, :, :], bc(s5t[:, f0 + f, :], (P, NS5, 16)), ALU.mult)
                    if done is None or q < 3:
                        c.mark(ins)
                c.wait()
                if done is not None:
                    ins.then_inc(done, 1)
                    dve.wait_ge(done, 1)

            def s5_layer():
                tt, ts, stt = v.tensor_tensor, v.tensor_scalar, v.scalar_tensor_tensor
                def spread(w, n):
                    for g_ in range(2):
                        r = slice(64 * g_, 64 * g_ + 64)
                        dst = w[r, :, :, :].rearrange("p m k (j c) -> p m (k j) c", c=32)[:, :, :, 16 * g_:16 * g_ + 16]
                        tt(dst[:, 0], b_prod[r, 0], b_prod[r, 1], ALU.subtract).then_inc(wb_ok, 1)
                        tt(dst[:, 1], b_prod[r, 2], b_prod[r, 3], ALU.add).then_inc(wb_ok, 1)

                dve.wait_ge(wz_ok, 1)
                spread(wide, 0)
                dve.wait_ge(wb_ok, 4)
                input_factor(5, b2_ok)
                dve.wait_ge(wz_ok, 2)
                spread(wide2, 1)
                dve.wait_ge(wb_ok, 8)
                dve.wait_ge(ct_ps, 2)
                dve.wait_ge(cT_ok, 6)
                t128 = [bc(turn128[:, m, :], (P, NS5, 32)) for m in range(2)]
                flat_c = lambda ap: ap.rearrange("p k (j c) -> p (k j) c", c=32)
                c.mark(tt(c_tmp_v[0], flat_c(cT[:, 0, :, :]), t128[0], ALU.mult))
                c.link(tt(c_tmp_v[1], flat_c(cT[:, 1, :, :]), t128[1], ALU.mult))
                tt(flat_c(cT2[:, 0, :, :]), c_tmp_v[0], c_tmp_v[1], ALU.add).then_inc(c2_re, 1)
                dve.wait_ge(c2_re, 1)
                dve.wait_ge(bt_ps, 2)

                def tile(j, jj):
                    b = jj % 2
                    ps = bank[jj][:, :].rearrange("p (a t) -> p a t", t=S5C)
                    cs = [rot[:, m, bass.ds(j, 1), :].to_broadcast((P, 4, S5C)) for m in range(2)]
                    dve.wait_ge(bu_ps, j + 1)
                    tt(m_in[:, b, 0, :].rearrange("p (a t) -> p a t", t=S5C), ps, cs[0], ALU.mult).then_inc(mc_ok, 1)
                    tt(m_in[:, b, 1, :].rearrange("p (a t) -> p a t", t=S5C), ps, cs[1], ALU.mult).then_inc(ms_ok, 1)

                def scans(j, jj, first):
                    b = jj % 2
                    if not first:
                        dve.wait_ge(c_used, j - 1)
                    mag = s5t[:, 0, bass.ds(j, 1)]
                    dve.wait_ge(gin_ok, j * 2 + 2)
                    for m in range(2):
                        v.tensor_tensor_scan(gst[:, b, m, :], mag.to_broadcast((P, T)), gin[:, b, m, :], 0.0,
                                             ALU.mult, ALU.add).then_inc(gst_ok, 1)
                    dve.wait_ge(gst_ok, j * 2 + 2)
                    tt(m_out[:, b, 0, :].rearrange("p (a t) -> p a t", t=S5C), gst[:, b, :, :].rearrange("p m (a t) -> p (m a) t", t=S5C),
                       rot[:, 0, bass.ds(j, 1), :].to_broadcast((P, 4, S5C)), ALU.mult).then_inc(oc_ok, 1)

                def skip(k, par):
                    dve.wait_ge(c_used, k * 4 + 4)
                    s_ = bass.ds(k, 1)
                    u_, o_ = xT[:, s_, :].rearrange("p k t -> p (k t)"), yg5[:, s_, :].rearrange("p k t -> p (k t)")
                    stt(out=o_, in0=u_, scalar=s5d[:, s_], in1=bank[4 + par][:, 0:T], op0=ALU.mult, op1=ALU.add).then_inc(yd5_ok, 1)

                def chunk(k, par):
                    for jj in range(4):
                        tile(k * 4 + jj, jj)
                        scans(k * 4 + (jj - 1), (jj - 1) % 4, False)
                        if jj == 2:
                            skip(k - 1, par)

                tile(0, 0)
                for jj in range(3):
                    tile(jj + 1, jj + 1)
                    scans(jj, jj, jj < 2)
                with dve.Fori(0, KD // 2 - 1) as turn:
                    chunk(turn * 2 + 1, 0)
                    chunk(turn * 2 + 2, 1)
                chunk(KD - 1, 0)
                scans(NS5 - 1, 3, False)
                skip(KD - 1, 1)

            def glu():
                tt = v.tensor_tensor
                dve.wait_ge(bias_in, 16)
                for i in range(4):
                    h, t = i // 2, i % 2
                    z = m_in_f[:, i * 512:(i + 1) * 512]
                    dve.wait_ge(glu_ps, 4 * h + 2 + t + 1)
                    tt(z, bank[4 * h + 2 + t][:, :], bias_glu[:, D + h * 512:D + (h + 1) * 512], ALU.add).then_inc(gz_ok, 1)
                    y = m_out_f[:, i * 512:(i + 1) * 512]
                    c.link(tt(y, bank[4 * h + t][:, :], bias_glu[:, h * 512:(h + 1) * 512], ALU.add))
                    dve.wait_ge(gs_ok, i + 1)
                    c.link(tt(y, y, z, ALU.mult))
                    r = res[:, t, h * 512:(h + 1) * 512]
                    ins = tt(r, r, y, ALU.add)
                    if h == 0:
                        c.mark(ins)
                    else:
                        ins.then_inc(res_ok, 1)

            def experts(l):
                n0 = NP * l
                route(l)
                c.link(v.memset(xs[:, :, SLOTS:], 0.0))
                for k in range(1, KD, 2):
                    dve.wait_ge(xs_ps, KD * l + k + 1)
                    v.tensor_scalar(xs[:, k, 0:SLOTS], bank[k % 4][:, :], gains[:, 1 + 2 * l, k:k + 1], None, ALU.mult).then_inc(xs_dve, 1)
                dve.wait_ge(xs_act, 4 * (l + 1))
                dve.wait_ge(xs_dve, 4 * (l + 1))

                def take(i, r, done):
                    for q in range(2):
                        first = v.value_load(base_i[0:1, r, bass.ds(i * 2 + q, 1)], min_val=0, max_val=SLOTS)
                        v.tensor_copy(xe[:, :, q * CAP:(q + 1) * CAP], xs[:, :, bass.ds(first, CAP)]).then_inc(done, 1)

                def match(n, par, done):
                    for r, dst in enumerate((pick[:, par, :], pick_part[:, :])):
                        v.scalar_tensor_tensor(out=dst, in0=key_row[:, r, :], scalar=row_no[:, bass.ds(n, 1)], in1=weight_row[:, r, :],
                                               op0=ALU.is_equal, op1=ALU.mult).then_inc(done, 1)

                take(0, 0, xe_ok)
                dve.wait_ge(key_ps, l + 1)
                c.link(v.tensor_copy(perm[:, 0, :], bank[4][:, :]))
                v.tensor_copy(perm[:, 1, :], bank[5][:, :]).then_inc(key_ok, 1)
                dve.wait_ge(key_ok, l + 1)
                if l == 0:
                    dve.wait_ge(coarse_ok, 1)

                def turns(j, first):
                    rj = bass.ds(j, 1)
                    one = lambda tab, m: tab[:, m:m + 1, rj, :].rearrange("p m j n -> p (m j) n")
                    coarse = rot_c[:, :, rj, :].rearrange("p m j n -> p (m j) n")
                    if not first:
                        dve.wait_ge(rot_ok, j * 2)
                    for m in range(2):
                        v.tensor_tensor(rtmp[:, m, :, :, :], bc(coarse, (P, 2, 16, 8)),
                                        one(rot_f, m).unsqueeze(1).to_broadcast((P, 2, 16, 8)), ALU.mult).then_inc(rot_m, 1)
                    dve.wait_ge(rot_m, j * 2 + 2)
                    out_ = [rot[:, m, rj, :].rearrange("p j (n f) -> p (j n) f", f=8) for m in range(2)]
                    v.tensor_tensor(out_[0], rtmp[:, 0, 0, :, :], rtmp[:, 1, 1, :, :], ALU.subtract).then_inc(rot_ok, 1)
                    v.tensor_tensor(out_[1], rtmp[:, 0, 1, :, :], rtmp[:, 1, 0, :, :], ALU.add).then_inc(rot_ok, 1)

                def step(i, par, lap):
                    dve.wait_ge(ha_ok, i + (n0 + 1))
                    v.tensor_tensor(act_g[:, :], act_a[:, :], bank[0][:, FF:2 * FF], ALU.mult).then_inc(hg_ok, 1)
                    take(i + 1, 0, xe_ok)
                    if not (isinstance(i, int) and i == 0):
                        dve.wait_ge(pick_ok, i + n0)
                    match(i, par, part_ok)
                    dve.wait_ge(part_ok, i * 2 + (2 * n0 + 2))
                    v.tensor_tensor(pick[:, par, :], pick[:, par, :], pick_part[:, :], ALU.add).then_inc(pick_ok, 1)
                    if l == 0:
                        for q in range(2):
                            turns(i * 2 + q, isinstance(i, int) and i == q == 0)

                pairs(dve, step)
                dve.wait_ge(routed, l + 1)
                with dve.If(dve.value_load(most_i[0:1, 0:1], min_val=0, max_val=SLOTS) > CAP):
                    dve.wait_ge(xe_ok, 2 * (NP + 1) * (l + 1))
                    dve.wait_ge(pick_ok, NP * (l + 1))
                    for r in range(PASSES - 1):
                        with dve.Fori(0, NP) as i:
                            n = i + r * NP
                            dve.wait_ge(more_step[l], n * STEPS)
                            take(i, r + 1, more_step[l])
                            dve.wait_ge(more_step[l], n * STEPS + SILU)
                            v.tensor_tensor(act_g[:, :], act_a[:, :], bank[0][:, FF:2 * FF], ALU.mult).then_inc(more_step[l], 1)
                            dve.wait_ge(more_step[l], n * STEPS + ROW1)
                            match(i + (r + 1) * NP, 0, more_step[l])
                            dve.wait_ge(more_step[l], n * STEPS + PART1)
                            v.tensor_tensor(pick[:, 0, :], pick[:, 0, :], pick_part[:, :], ALU.add).then_inc(more_step[l], 1)
                    dve.wait_ge(more_step[l], MORE * STEPS)
                for t in range(NT):
                    dve.wait_ge(comb_ps, NT * NP * (l + 1) - (NT - 1 - t))
                    for h in range(2):
                        r_ = res[:, t, h * 512:(h + 1) * 512]
                        ins = v.tensor_tensor(r_, r_, bank[4 + 2 * t + h][:, :], ALU.add)
                        if h == 0:
                            c.mark(ins)
                    ins.then_inc(res_ok, 1)

            norm_a(1)
            norm_b(1)
            experts(0)
            dve.wait_ge(c_in, 32)
            dve.wait_ge(res_ok, 2 * NT)
            for h in range(2):
                v.tensor_scalar(wide_c[:, :, :, h, :].rearrange("p m k q -> p (m k) q"), s5c.rearrange("p m k q -> p (m k) q"),
                                cmask[:, h:h + 1], None, ALU.mult).then_inc(wc_ok, 1)
            norm_a(2)
            dve.wait_ge(raw_in, 32)
            input_factor(3)
            norm_b(2)
            s5_layer()
            glu()
            norm_a(3)
            norm_b(3)
            experts(1)
            mean_square(4)
            dve.wait_ge(fg_in, 16)
            dve.wait_ge(rstd_ok, 5)
            for t in range(NT):
                v.scalar_tensor_tensor(out=xn[:, t, :], in0=res[:, t, :], scalar=rstd[:, 4, t:t + 1], in1=gain_fin,
                                       op0=ALU.mult, op1=ALU.mult).then_inc(fin_ok, 1)

        @block.tensor
        def _(pe):
            mm = nc.tensor.matmul

            def norm(n, contiguous=False):
                pe.wait_ge(xn_ok, 2 * n + 2)
                for b in range(4):
                    for k in (2 * b, 2 * b + 1):
                        for t in range(NT):
                            src = xn[:, t, k * P:(k + 1) * P] if contiguous else xn[:, t, k:D:KD]
                            ins = nc.tensor.transpose(bank[b][:, (k % 2) * T + t * P:(k % 2) * T + (t + 1) * P], src, ident[:, :])
                    ins.then_inc(xT_ps, 1)

            def xT_here(n):
                pe.wait_ge(xT_act, 4 * (n + 1))
                pe.wait_ge(xT_dve, 4 * (n + 1))

            def w_here(i):
                pe.wait_ge(w_in[i % NW], 16 * (i // NW + 1))

            pe.wait_ge(consts, 1)
            norm(0)
            xT_here(0)
            def mix_product(b, k):
                h, t = b // 2, b % 2
                return mm(mix_bank[b][:, :], yT[:, k, t * P:(t + 1) * P], ring_w[:, (W_OUT0 + h) % NW, k, :],
                          start=(k == 0), stop=(k == KD - 1))

            def heads_part(nums):
                for m in nums:
                    if m % KD == 0:
                        w_here(W_OUT0 + m // KD)
                    mix_product(m // (KD // 2), m % (KD // 2))

            def gate_part(chunk, half):
                before = sum(sum(p_) for p_ in GATE_PARTS[:chunk]) + sum(GATE_PARTS[chunk][:half])
                for m in range(before, before + GATE_PARTS[chunk][half]):
                    t, k, num = m // KD, m % KD, PROJ_BLOCKS.index("gate")
                    if m == 0:
                        w_here(num)
                    if m == KD:
                        pe.wait_ge(zm_ok, 7)
                    ins = mm(gate_bank[t][:, :], xT[:, k, t * P:(t + 1) * P], ring_w[:, num % NW, k, :], start=(k == 0), stop=(k == KD - 1))
                    if k == KD - 1:
                        ins.then_inc(proj_ps, 1)

            def mixer_step(kind, n):
                if kind == "rows":
                    pe.wait_ge(g_ok, 1)
                    pe.wait_ge(rs_ok, 2)
                    pe.wait_ge(proj_got, 10)
                    ps, ps2 = halves(0), halves(2)
                    for u in range(NU):
                        mm(ps[u], sml[:, G, u:u + 1].to_broadcast((P, P)), chunk_incl[:, :], start=True, stop=True)
                        mm(ps2[u], sml[:, BETA, u:u + 1].to_broadcast((P, P)), ident[:, :], start=True, stop=True)
                    mm(bank[4][:, 0:8], chunk_incl[:, :], sml[:, G, :], start=True, stop=True)
                    mm(bank[4][:, 8:16], chunk_ones[:, :], sml[:, G, :], start=True, stop=True).then_inc(rows_ps, 1)
                if kind == "l2":
                    for m, sq in enumerate((sq_q, sq_k)):
                        pe.wait_ge(sq_ok, m + 1)
                        pe.wait_ge(ba_got, 1)
                        for h in range(2):
                            ins = mm(bank[2 * m + h][:, :], ones[:, :], sq[:, 4 * h:4 * h + 4, :].rearrange("p u q -> p (u q)"),
                                     start=True, stop=True)
                        ins.then_inc(ssum_ps, 1)
                if kind == "turn":
                    pe.wait_ge(silu_ok, 3)
                    pe.wait_ge(expd_ok, 2)
                    pe.wait_ge(diff_ok, 1)
                    for u, ps in enumerate(halves(0)):
                        ins = nc.tensor.transpose(ps, vT[:, u, :], ident[:, :])
                    ins.then_inc(vt_ps, 1)
                    pe.wait_ge(kn_ok, 1)
                    pe.wait_ge(kb_ok, 2)
                    for u, ps in enumerate(halves(2)):
                        ins = nc.tensor.transpose(ps, kT[:, u, :], ident[:, :])
                    ins.then_inc(kt_ps, 1)
                if kind == "gram":
                    pe.wait_ge(proj_got, 12)
                    pe.wait_ge(s5t_ok, 1)
                    pe.wait_ge(qn_ok, 1)
                    for m, rhs in enumerate((kbT, qT)):
                        for u, ps in enumerate(halves(4 + 2 * m)):
                            ins = mm(ps, kT[:, u, :], rhs[:, u, :], start=True, stop=True)
                        ins.then_inc(gram_ps, 1)
                if kind == "level":
                    pe.wait_ge(bt_ok, n + 1)
                    if n == 0:
                        pe.wait_ge(vt_ok, 2)
                        for u, ps in enumerate(halves(0)):
                            ins = nc.tensor.transpose(ps, btl[:, u, :], ident[:, :])
                        ins.then_inc(p1_ps, 1)
                    else:
                        pe.wait_ge(x_ok, n)
                        if n == 1:
                            pe.wait_ge(kt_ok, 2)
                        for u, ps in enumerate(halves(pair_a(n))):
                            ins = mm(ps, btl[:, u, :], X[:, u, :], start=True, stop=True)
                        ins.then_inc(p1_ps, 1)
                if kind == "delta":
                    pe.wait_ge(p1_ok, 2 * n)
                    pe.wait_ge(xt_ok, n)
                    if n < 5:
                        for u, ps in enumerate(halves(2 - pair_a(n))):
                            ins = mm(ps, XT[:, u, :], P1[:, u, :], start=True, stop=True)
                        ins.then_inc(delta_ps, 1)
                    for u, ps in enumerate(halves(pair_a(n))):
                        ins = mm(ps, P1[:, u, :], XT[:, u, :], start=True, stop=True)
                    ins.then_inc(deltaT_ps, 1)
                if kind == "wu":
                    pe.wait_ge(xt_ok, 6)
                    for u, ps in enumerate(halves(0)):
                        ins = mm(ps, kbe[:, u, :], XT[:, u, :], start=True, stop=True)
                    ins.then_inc(wu_ps, 1)
                    for u, ps in enumerate(halves(2)):
                        ins = mm(ps, XT[:, u, :], vbeta[:, u, :], start=True, stop=True)
                    ins.then_inc(wu_ps, 1)
                if kind == "chunk":
                    t, lo = n // 2, CH * (n % 2)
                    part = slice(lo, lo + CH)
                    if n == 0:
                        pe.wait_ge(wT_ok, 2)
                        pe.wait_ge(u_ok, 2)
                        pe.wait_ge(consts, 4)
                    else:
                        pe.wait_ge(st_ok, n)
                        pe.wait_ge(o_ok, n)
                    for h in range(DNH):
                        ins = mm(bank[0][part, h * P:(h + 1) * P], wT[:, 2 * h + t, part], state[:, h, :], start=True, stop=True)
                    ins.then_inc(vs_ps, 1)
                    gate_part(n, 0)
                    pe.wait_ge(vn_ok, n + 1)
                    for h in range(DNH):
                        u = 2 * h + t
                        mm(bank[1][part, h * P:(h + 1) * P], qT[:, u, part], state[:, h, :], start=True, stop=False)
                        ins = mm(bank[1][part, h * P:(h + 1) * P], attnT[part, u, part], vnew[part, 4 * t + h, :], start=False, stop=True)
                    ins.then_inc(o_ps, 1)
                    for h in range(DNH):
                        ins = mm(bank[2][:, h * P:(h + 1) * P], ktail[part, 2 * h + t, :], vnew[part, 4 * t + h, :], start=True, stop=True)
                    ins.then_inc(st_ps, 1)
                    gate_part(n, 1)
                if kind == "dn_out":
                    pe.wait_ge(ys_ok, 4)
                    pe.wait_ge(gate_ok, 1)
                    heads_part(range(MIX_BEFORE))
                    pe.wait_ge(yg_ok, 1)
                    for t in range(NT):
                        for h in range(DNH):
                            ins = nc.tensor.transpose(bank[h // 2][:, (h % 2) * T + t * P:(h % 2) * T + (t + 1) * P],
                                                      yg[:, 4 * t + h, :], ident[:, :])
                    ins.then_inc(yd_ps, 1)
                hp, q2 = slice(64 * (n % 2), 64 * (n % 2) + 64), n // 2
                if kind == "score":
                    if n == 0:
                        pe.wait_ge(gram_ok, 4)
                    if n >= 2:
                        pe.wait_ge(zm_ok, n - 1)
                    mm(z3[n % 2][:, 0:T], sbkT[hp, q2, 0:P], sbqT[hp, q2, :], start=True, stop=True)
                    mm(z3[n % 2][:, T:3 * P], sbkT[hp, q2, P:T], sbqT[hp, q2, P:T], start=True, stop=True).then_inc(z_ps, 1)
                if kind == "suffix":
                    pe.wait_ge(spm_ok, n + 1)
                    if n >= 1:
                        pe.wait_ge(lw_ok, n)
                    s = sb_sp[:, n % 2, :]
                    r = bank[6]
                    mm(r[:, 0:T], neg_upto[:, :], s[:, 0:T], start=True, stop=False)
                    mm(r[:, P:T], neg_ones[:, :], s[:, T:3 * P], start=False, stop=True)
                    mm(r[:, T:3 * P], neg_upto[:, :], s[:, T:3 * P], start=True, stop=True).then_inc(rc_ps, 1)
                if kind == "mixv":
                    pe.wait_ge(w_ok, n + 1)
                    if n >= 2 and n % 2 == 0:
                        pe.wait_ge(ys_ok, n // 2)
                    o = bank[7][hp, 0:T]
                    w = sb_w[:, n % 2, :]
                    mm(o, sbv[:, 0, n * SBD:(n + 1) * SBD], w[:, 0:T], start=True, stop=False)
                    mm(o[:, P:T], sbv[:, 1, n * SBD:(n + 1) * SBD], w[:, T:3 * P], start=False, stop=True).then_inc(ys_ps, 1)

            for i, name in enumerate(PROJ_BLOCKS[:-1]):
                w_here(i)
                if i == 1:
                    pe.wait_ge(consts, 4)
                    pe.wait_ge(par_in, 16 * N_PAR)
                    nc.tensor.transpose(bank[7][:, 0:TAPS * 12], convw_rows[:, :], ident[0:TAPS * 12, 0:TAPS * 12]).then_inc(cw_ps, 1)
                    pe.wait_ge(cw_ok, 1)
                if i >= 2:
                    pe.wait_ge(proj_got, 2 * (i - 1))
                w = ring_w[:, i % NW, :, :]
                for h in range(2):
                    ps = bank[4 + 2 * (i % 2) + h]
                    if name == "sb_v":
                        for k in range(KD):
                            ins = mm(ps[:, :], xT[:, k, h * P:(h + 1) * P], w[:, k, :], start=(k == 0), stop=(k == KD - 1))
                    else:
                        for cc in range(2):
                            col = (2 * h + cc) * P
                            for k in range(KD):
                                ins = mm(ps[:, cc * T:(cc + 1) * T], w[:, k, col:col + P], xT[:, k, :], start=(k == 0), stop=(k == KD - 1))
                    ins.then_inc(proj_ps, 1)
                    if (name, h) == ("sb_v", 0):
                        mixer_step("rows", 0)
                if i == 3:
                    for t in range(NT):
                        for k in range(KD):
                            ins = mm(bank[0][:, 8 * t:8 * t + 8], xT[:, k, t * P:(t + 1) * P], wba[:, k, :], start=(k == 0), stop=(k == KD - 1))
                    ins.then_inc(ba_ps, 1)
                if i == 4:
                    mixer_step("l2", 0)
            pe.wait_ge(s5_par, 1)
            pe.wait_ge(proj_got, 12)
            for n, row in enumerate((MAG, COS, SIN, CRE, CIM)):
                ins = nc.tensor.transpose(bank[7][:, n * NS5:(n + 1) * NS5], s5w[:, row, :], ident[0:NS5, 0:NS5])
            nc.tensor.transpose(bank[7][:, 5 * NS5:5 * NS5 + 2 * KD], s5w[0:2 * KD, VEC, :], ident[0:2 * KD, 0:2 * KD]).then_inc(s5_tps, 1)
            for item in plan:
                mixer_step(*item)
            heads_part(range(MIX_BEFORE, 2 * KD))
            pe.wait_ge(yd_ok, 2)
            for b in range(4):
                for k in range(KD // 2, KD):
                    ins = mix_product(b, k)
                ins.then_inc(mix_ps, 1)

            def experts(l):
                n0, x0, w0 = NP * l, 2 * (NP + 1) * l, W_EXP[l]
                for t in range(NT):
                    for k in range(KD):
                        ins = mm(bank[4][:, 64 * t:64 * t + NGRP + NEXP], xT[:, k, t * P:(t + 1) * P], wr[:, l, k, :],
                                 start=(k == 0), stop=(k == KD - 1))
                ins.then_inc(log_ps, 1)
                pe.wait_ge(sel_ok, l + 1)
                b5 = bank[5]
                mm(b5[:, 0:NEXP], before[:, :], sel[:, 0, :], start=True, stop=True)
                mm(b5[:, NEXP:2 * NEXP], before[:, :], sel[:, 1, :], start=True, stop=False)
                mm(b5[:, NEXP:2 * NEXP], ones[:, :], sel[:, 0, :], start=False, stop=True)
                mm(b5[:, 2 * NEXP:3 * NEXP], ones[:, :], sel[:, 0, :], start=True, stop=False)
                mm(b5[:, 2 * NEXP:3 * NEXP], ones[:, :], sel[:, 1, :], start=False, stop=True).then_inc(pos_ps, 1)
                pe.wait_ge(perm_ok, 2 * (l + 1))
                for k in range(KD):
                    if k >= 4:
                        pe.wait_ge((xs_act, xs_dve)[k % 2], 4 * l + (k - 4) // 2 + 1)
                    for t in range(NT):
                        ins = mm(bank[k % 4][:, :], xn[:, t, k:D:KD], perm[:, t, :], start=(t == 0), stop=(t == NT - 1))
                    ins.then_inc(xs_ps, 1)
                pe.wait_ge(xs_act, 4 * (l + 1))
                pe.wait_ge(xs_dve, 4 * (l + 1))

                pe.wait_ge(routed, l + 1)
                for m, row in enumerate((10, 7)):
                    for r in range(2):
                        for t in range(NT):
                            ins = mm(bank[4 + m][:, (2 * r + t) * P:(2 * r + t + 1) * P], rv[:, row, t, r:r + 1].to_broadcast((P, P)),
                                     ident[:, :], start=True, stop=True)
                ins.then_inc(key_ps, 1)

                def hidden(weights):
                    for k in range(KD):
                        for q in range(2):
                            ins = mm(bank[0][q * CAP:(q + 1) * CAP, :], xe[:, k, q * CAP:(q + 1) * CAP], weights[q][:, k, :],
                                     start=(k == 0), stop=(k == KD - 1))
                    return ins

                def turn_hidden():
                    for k in range(2):
                        ins = nc.tensor.transpose(bank[1][:, k * P:(k + 1) * P], act_g[:, k * P:(k + 1) * P], ident[:, :])
                    return ins

                def product(slots):
                    for k in range(2):
                        for h in range(2):
                            for q in range(2):
                                ins = mm(bank[2 + h][q * CAP:(q + 1) * CAP, :], act_gT[:, k, q * CAP:(q + 1) * CAP],
                                         ring_v[:, slots[q], k, h * 512:(h + 1) * 512], start=(k == 0), stop=(k == 1))
                    return ins

                def combine(par, start, stop, tiles=range(NT)):
                    for t in tiles:
                        for h in range(2):
                            ins = mm(bank[4 + 2 * t + h][:, :], pick[:, par, t * P:(t + 1) * P], yrow[:, h * 512:(h + 1) * 512],
                                     start=start, stop=stop)
                    return ins

                def step(i, par, lap):
                    pe.wait_ge(xe_ok, i * 2 + (x0 + 2))
                    if isinstance(i, int) and i == 0:
                        pe.wait_ge(first_in, 32 * (l + 1))
                        hidden(first_w).then_inc(h_ps, 1)
                    else:
                        nums = [w0 + 2 * par + q for q in range(2)]
                        for m in nums:
                            pe.wait_ge(w_in[m % NW], lap * 16 + 16 * (m // NW + 1))
                        hidden([ring_w[:, m % NW, :, :] for m in nums]).then_inc(h_ps, 1)
                    before = not (isinstance(i, int) and i == 0)
                    if before:
                        pe.wait_ge(ya_ok, i * 2 + 2 * n0)
                        pe.wait_ge(pick_ok, i + n0)
                        if isinstance(i, int):
                            pe.wait_ge(key_ok, l + 1)
                        combine(1 - par, isinstance(i, int), False, [0]).then_inc(comb_ps, 1)
                    pe.wait_ge(hg_ok, i + (n0 + 1))
                    turn_hidden().then_inc(t_ps, 1)
                    if before:
                        combine(1 - par, isinstance(i, int), False, [1]).then_inc(comb_ps, 1)
                    pe.wait_ge(gt_ok, i + (n0 + 1))
                    for q in range(2):
                        pe.wait_ge(v_in[2 * par + q], lap * 16 + 16 * (NEXP * l // NV + 1))
                    product([2 * par + q for q in range(2)]).then_inc(y_ps, 1)

                fullest = pe.value_load(most_i[0:1, 0:1], min_val=0, max_val=SLOTS)
                pairs(pe, step)
                with pe.If(fullest > CAP):
                    pe.wait_ge(ya_ok, 2 * NP * (l + 1))
                    pe.wait_ge(pick_ok, NP * (l + 1))
                    for t in range(NT):
                        combine(1, False, False, [t]).then_inc(comb_ps, 1)

                    def more_pass(n, stop):
                        pe.wait_ge(more_in[l], n * 64 + 64)
                        pe.wait_ge(more_step[l], n * STEPS + XE1)
                        hidden([ring_w[:, q, :, :] for q in range(2)]).then_inc(more_step[l], 1)
                        pe.wait_ge(more_step[l], n * STEPS + GATED)
                        mm(bank[1][0:1, FF:FF + 1], ones[:, 0:1], ones[:, 0:1], start=True, stop=True)
                        turn_hidden().then_inc(more_step[l], 1)
                        pe.wait_ge(more_step[l], n * STEPS + GT)
                        product([0, 1]).then_inc(more_step[l], 1)
                        pe.wait_ge(more_step[l], n * STEPS + PICK)
                        combine(0, False, stop).then_inc(more_step[l], 1)

                    with pe.Fori(0, MORE - 1) as n:
                        more_pass(n, False)
                    more_pass(MORE - 1, True)
                with pe.Else():
                    pe.wait_ge(ya_ok, 2 * NP * (l + 1))
                    pe.wait_ge(pick_ok, NP * (l + 1))
                    for t in range(NT):
                        combine(1, False, True, [t]).then_inc(comb_ps, 1)

            def turn_weights(src, ps0, done):
                for m in range(2):
                    for k in range(KD):
                        ins = nc.tensor.transpose(bank[ps0 + 2 * m + k // 4][:, (k % 4) * P:(k % 4 + 1) * P], src(m, k), ident[:, :])
                    ins.then_inc(done, 1)

            def s5_layer():
                xT_here(2)
                pe.wait_ge(wb_ok, 4)
                turn_weights(lambda m, k: wide[:, m, k, :], 0, bt_ps)
                pe.wait_ge(wb_ok, 8)
                pe.wait_ge(bT_ok, 4)
                turn_weights(lambda m, k: wide2[:, m, k, :], 0, bt_ps)
                pe.wait_ge(bT_ok, 8)

                def drive(j):
                    k, r = j // 4, slice(32 * (j % 4), 32 * (j % 4) + 32)
                    if j >= 4:
                        pe.wait_ge(ms_ok, j - 3)
                    for m in range(2):
                        for n, w in enumerate((bT, bT2)):
                            ins = mm(bank[j % 4][:, m * T + n * P:m * T + (n + 1) * P], w[r, m, k, :], xT[r, k, n * P:(n + 1) * P],
                                     start=True, stop=True)
                    ins.then_inc(bu_ps, 1)

                def read(j):
                    k, r = j // 4, slice(32 * (j % 4), 32 * (j % 4) + 32)
                    pe.wait_ge(oc_ok, j + 1)
                    pe.wait_ge(os_ok, j + 1)
                    if j % 4 == 0 and k >= 2:
                        pe.wait_ge(yd5_ok, k - 1)
                    mo = m_out[:, j % 2, :, :]
                    for n, (w, wn) in enumerate(((cT, cTn), (cT2, cTn2))):
                        o = bank[4 + k % 2][r, n * P:(n + 1) * P]
                        re, im = slice(n * P, (n + 1) * P), slice(T + n * P, T + (n + 1) * P)
                        mm(o, w[:, 0, k, r], mo[:, 0, re], start=True, stop=False)
                        mm(o, w[:, 1, k, r], mo[:, 0, im], start=False, stop=False)
                        mm(o, wn[:, k, r], mo[:, 1, im], start=False, stop=False)
                        ins = mm(o, w[:, 1, k, r], mo[:, 1, re], start=False, stop=True)
                    ins.then_inc(c_used, 1)

                for j in range(3):
                    drive(j)
                pe.wait_ge(cT_ok, 7)
                pe.wait_ge(c2_ok, 1)
                for j in range(NS5):
                    if j + 3 < NS5:
                        drive(j + 3)
                    read(j)
                pe.wait_ge(gelu_ok, KD)
                for b in range(4):
                    w_here(W_GLU + b)
                    for t in range(NT):
                        for k in range(KD):
                            ins = mm(bank[2 * b + t][:, :], yg5[:, k, t * P:(t + 1) * P], ring_w[:, (W_GLU + b) % NW, k, :],
                                     start=(k == 0), stop=(k == KD - 1))
                        ins.then_inc(glu_ps, 1)

            norm(1)
            xT_here(1)
            experts(0)
            pe.wait_ge(wc_ok, 2)
            turn_weights(lambda m, k: wide_c[:, m, k, :, :].rearrange("p h q -> p (h q)"), 4, ct_ps)
            norm(2, contiguous=True)
            xT_here(2)
            s5_layer()
            norm(3)
            xT_here(3)
            experts(1)


_INS = ['x', 'mix_norm_even', 'w_in_even', 'dn_conv_w', 'dn_a_log', 'dn_dt_bias', 'dn_out_norm', 'w_out_even',
        'mix_norm_odd', 's5_lambda_re', 's5_lambda_im', 's5_log_step', 's5_b_re', 's5_b_im', 's5_c_re', 's5_c_im',
        's5_d', 'w_glu', 'b_glu', 'ffn_norm', 'w_router_group', 'w_router_expert', 'w_expert_in', 'w_expert_out',
        'final_norm']


def kernel(**inputs):
    import numpy as _np
    import concourse.bacc as _bacc
    from concourse import mybir as _mybir
    from concourse.bass_utils import run_bass_kernel_spmd as _run

    nc = _bacc.Bacc("TRN2", target_bir_lowering=False, num_devices=1)
    arrays, args = {}, []
    for name in _INS:
        a = _np.ascontiguousarray(inputs[name])
        arrays[f"in_{name}"] = a
        args.append(nc.dram_tensor(f"in_{name}", a.shape, _mybir.dt.from_np(a.dtype), kind="ExternalInput").ap())
    args.append(nc.dram_tensor("out", (1, T, D), F32, kind="ExternalOutput").ap())
    trunk(nc, *args)
    r = _run(nc, [arrays], core_ids=[0])
    return r.results[0]["out"]
```
